# Optimizing a Trainium2 kernel written in Bass

```python
import jax, jax.numpy as jnp
from jax import lax
import numpy as np
import jax
import jax.numpy as jnp

D_MODEL = 1024
BATCH = 1
SEQ = 512
DEPTH = 1

CHUNK = 64
D_MIX = D_MODEL
HEAD_DIM = 64
ATT_WIDTH = 3 * D_MIX // 8
ATT_HEADS = ATT_WIDTH // HEAD_DIM
ATT_PAST_CHUNKS = 8
ATT_BAND = (ATT_PAST_CHUNKS + 1) * CHUNK
REL_CLIP = 128
ML_WIDTH = 3 * D_MIX // 8
ML_HEADS = ML_WIDTH // HEAD_DIM
CONV_WIDTH = 4
GLA_WIDTH = D_MIX - ATT_WIDTH - ML_WIDTH
GLA_HEADS = 4
GLA_DV = GLA_WIDTH // GLA_HEADS
GLA_DK = GLA_DV // 2
GLA_KW = GLA_HEADS * GLA_DK
GLA_RANK = 16
GLA_TAU = 16.0
IN_SPLITS = (ATT_WIDTH, ATT_WIDTH, ATT_WIDTH, ATT_WIDTH,
             ML_WIDTH, ML_WIDTH, ML_WIDTH, ML_WIDTH, ML_HEADS, ML_HEADS, ML_WIDTH,
             GLA_KW, GLA_KW, GLA_WIDTH, GLA_RANK, GLA_WIDTH)
D_IN = sum(IN_SPLITS)
EPS = 1e-6
NEG = -1e30


def rmsnorm(x, g):
    xf = x.astype(jnp.float32)
    y = xf * lax.rsqrt(jnp.mean(xf * xf, axis=-1, keepdims=True) + EPS)
    return (y * g.astype(jnp.float32)).astype(x.dtype)

def head_rmsnorm(x, g, n_heads):
    b, s, w = x.shape
    y = rmsnorm(x.reshape(b, s, n_heads, w // n_heads), g.reshape(n_heads, w // n_heads))
    return y.reshape(b, s, w)

def causal_conv(x, w):
    k_w = w.shape[0]
    s = x.shape[1]
    xp = jnp.pad(x, ((0, 0), (k_w - 1, 0), (0, 0)))
    return sum(xp[:, j:j + s] * w[j] for j in range(k_w))

def band_chunk_attention(q, k, v, rel_bias):
    bsz, s, h, d = q.shape
    nc = s // CHUNK
    pad = ATT_PAST_CHUNKS * CHUNK
    qc = q.reshape(bsz, nc, CHUNK, h, d)
    kp = jnp.pad(k, ((0, 0), (pad, 0), (0, 0), (0, 0))).reshape(bsz, nc + ATT_PAST_CHUNKS, CHUNK, h, d)
    vp = jnp.pad(v, ((0, 0), (pad, 0), (0, 0), (0, 0))).reshape(bsz, nc + ATT_PAST_CHUNKS, CHUNK, h, d)
    kb = jnp.concatenate([kp[:, m:m + nc] for m in range(ATT_PAST_CHUNKS + 1)], axis=2)
    vb = jnp.concatenate([vp[:, m:m + nc] for m in range(ATT_PAST_CHUNKS + 1)], axis=2)
    scores = jnp.einsum('bnqhd,bnkhd->bnhqk', qc, kb).astype(jnp.float32) * (d ** -0.5)
    rel = jnp.arange(CHUNK)[:, None] + pad - jnp.arange(ATT_BAND)[None, :]
    bias = rel_bias[:, jnp.clip(rel, -REL_CLIP, REL_CLIP) + REL_CLIP].astype(jnp.float32)
    kpos = (jnp.arange(nc)[:, None] - ATT_PAST_CHUNKS) * CHUNK + jnp.arange(ATT_BAND)[None, :]
    valid = kpos >= 0
    scores = jnp.where(valid[None, :, None, None, :], scores + bias[None, None], NEG)
    p = jax.nn.softmax(scores, axis=-1).astype(v.dtype)
    o = jnp.einsum('bnhqk,bnkhd->bnqhd', p, vb)
    return o.reshape(bsz, s, h * d)

def mlstm_chunkwise(q, k, v, i_pre, f_pre):
    bsz, s, h, d = q.shape
    nc = s // CHUNK
    L = CHUNK
    dt = q.dtype
    qc = q.astype(jnp.float32).reshape(bsz, nc, L, h, d)
    kc = (k.astype(jnp.float32) * (d ** -0.5)).reshape(bsz, nc, L, h, d)
    vc = v.astype(jnp.float32).reshape(bsz, nc, L, h, d)
    ig = i_pre.astype(jnp.float32).reshape(bsz, nc, L, h).transpose(0, 1, 3, 2)
    lf = jax.nn.log_sigmoid(f_pre.astype(jnp.float32)).reshape(bsz, nc, L, h).transpose(0, 1, 3, 2)
    bcum = jnp.cumsum(lf, axis=-1)
    g = bcum[..., -1]
    a = g[..., None] - bcum + ig
    m_loc = jnp.max(a, axis=-1)
    w = jnp.exp(a - m_loc[..., None])
    c_loc = jnp.einsum('bnhj,bnjhv,bnjhk->bnhvk', w, vc, kc)
    n_loc = jnp.einsum('bnhj,bnjhk->bnhk', w, kc)

    def step(carry, xs):
        c_st, n_st, m_st = carry
        g_c, m_l, c_l, n_l = xs
        m_new = jnp.maximum(g_c + m_st, m_l)
        s_old = jnp.exp(g_c + m_st - m_new)
        s_new = jnp.exp(m_l - m_new)
        c_new = s_old[..., None, None] * c_st + s_new[..., None, None] * c_l
        n_new = s_old[..., None] * n_st + s_new[..., None] * n_l
        return (c_new, n_new, m_new), (c_st, n_st, m_st)

    init = (jnp.zeros((bsz, h, d, d), jnp.float32), jnp.zeros((bsz, h, d), jnp.float32),
            jnp.zeros((bsz, h), jnp.float32))
    xs = (jnp.moveaxis(g, 1, 0), jnp.moveaxis(m_loc, 1, 0), jnp.moveaxis(c_loc, 1, 0), jnp.moveaxis(n_loc, 1, 0))
    _, (c_prev, n_prev, m_prev) = lax.scan(step, init, xs)
    c_prev = jnp.moveaxis(c_prev, 0, 1)
    n_prev = jnp.moveaxis(n_prev, 0, 1)
    m_prev = jnp.moveaxis(m_prev, 0, 1)

    causal = jnp.tril(jnp.ones((L, L), dtype=bool))
    log_d = jnp.where(causal, bcum[..., :, None] - bcum[..., None, :] + ig[..., None, :], NEG)
    inter_log = bcum + m_prev[..., None]
    m_row = jnp.maximum(inter_log, jnp.max(log_d, axis=-1))
    d_mat = jnp.exp(log_d - m_row[..., None])
    inter_w = jnp.exp(inter_log - m_row)
    sc = jnp.einsum('bnthd,bnjhd->bnhtj', qc, kc) * d_mat
    num = jnp.einsum('bnhtj,bnjhv->bnthv', sc, vc) + \
        inter_w.transpose(0, 1, 3, 2)[..., None] * jnp.einsum('bnhvk,bnthk->bnthv', c_prev, qc)
    den = jnp.sum(sc, axis=-1) + inter_w * jnp.einsum('bnhk,bnthk->bnht', n_prev, qc)
    den = jnp.maximum(jnp.abs(den), jnp.exp(-m_row))
    out = num / den.transpose(0, 1, 3, 2)[..., None]
    return out.reshape(bsz, s, h * d).astype(dt)

def gla_chunkwise(q, k, v, log_alpha):
    bsz, s, h, dk = q.shape
    dv = v.shape[-1]
    nc = s // CHUNK
    L = CHUNK
    dt = q.dtype

    def to_chunks(t):
        return jnp.moveaxis(t.astype(jnp.float32).reshape(bsz, nc, L, h, t.shape[-1]), 1, 0)

    xs = (to_chunks(q * (dk ** -0.5)), to_chunks(k), to_chunks(v), to_chunks(log_alpha))
    causal = jnp.tril(jnp.ones((L, L), dtype=bool))

    def step(state, chunk):
        qx, kx, vx, la = chunk
        bcum = jnp.cumsum(la, axis=1)
        diff = bcum[:, :, None] - bcum[:, None, :]
        decay = jnp.where(causal[None, :, :, None, None], jnp.exp(jnp.minimum(diff, 0.0)), 0.0)
        att = jnp.einsum('bthd,bjhd,btjhd->bhtj', qx, kx, decay)
        o_intra = jnp.einsum('bhtj,bjhv->bthv', att, vx)
        o_inter = jnp.einsum('bthd,bhdv->bthv', qx * jnp.exp(bcum), state)
        btot = bcum[:, -1]
        k_dec = kx * jnp.exp(btot[:, None] - bcum)
        state_new = jnp.exp(btot)[..., None] * state + jnp.einsum('bjhd,bjhv->bhdv', k_dec, vx)
        return state_new, o_intra + o_inter

    _, o = lax.scan(step, jnp.zeros((bsz, h, dk, dv), jnp.float32), xs)
    return jnp.moveaxis(o, 0, 1).reshape(bsz, s, h * dv).astype(dt)

def hybrid_layer(x, norm_g, w_in, b_gates, conv_w, w_alpha, b_alpha, rel_bias, ml_norm_g, gla_norm_g, w_out):
    bsz, s, _ = x.shape
    hn = rmsnorm(x, norm_g)
    z = jnp.einsum('bsd,de->bse', hn, w_in)
    split_idx = [int(i) for i in np.cumsum(IN_SPLITS)[:-1]]
    (aq, ak, av, ag, mq, mk, mv, mo, mi, mf, mg, gq, gk, gv, ga, gg) = jnp.split(z, split_idx, axis=-1)

    att = band_chunk_attention(aq.reshape(bsz, s, ATT_HEADS, HEAD_DIM), ak.reshape(bsz, s, ATT_HEADS, HEAD_DIM),
                               av.reshape(bsz, s, ATT_HEADS, HEAD_DIM), rel_bias)
    y_a = att * jax.nn.silu(ag)

    qk = jax.nn.silu(causal_conv(jnp.concatenate([mq, mk], axis=-1), conv_w))
    mq_c, mk_c = qk[..., :ML_WIDTH], qk[..., ML_WIDTH:]
    h_ml = mlstm_chunkwise(mq_c.reshape(bsz, s, ML_HEADS, HEAD_DIM), mk_c.reshape(bsz, s, ML_HEADS, HEAD_DIM),
                           mv.reshape(bsz, s, ML_HEADS, HEAD_DIM),
                           mi + b_gates[:ML_HEADS], mf + b_gates[ML_HEADS:])
    y_b = jax.nn.sigmoid(mo) * head_rmsnorm(h_ml, ml_norm_g, ML_HEADS) * jax.nn.silu(mg)

    log_alpha = jax.nn.log_sigmoid((jnp.einsum('bsr,rk->bsk', ga, w_alpha) + b_alpha).astype(jnp.float32)) / GLA_TAU
    h_gla = gla_chunkwise(gq.reshape(bsz, s, GLA_HEADS, GLA_DK), gk.reshape(bsz, s, GLA_HEADS, GLA_DK),
                          gv.reshape(bsz, s, GLA_HEADS, GLA_DV), log_alpha.reshape(bsz, s, GLA_HEADS, GLA_DK))
    y_c = head_rmsnorm(h_gla, gla_norm_g, GLA_HEADS) * jax.nn.silu(gg)

    y = jnp.concatenate([y_a, y_b, y_c], axis=-1)
    return x + jnp.einsum('bse,ed->bsd', y, w_out)

def first_inputs(seed: int = 0) -> dict:
    key = jax.random.key(seed)
    ks = jax.random.split(key, 12)
    f32 = jnp.float32
    x = jax.random.normal(ks[0], (BATCH, SEQ, D_MODEL), f32)
    norm_g = 1.0 + 0.1 * jax.random.normal(ks[1], (DEPTH, D_MODEL), f32)
    w_in = jax.random.normal(ks[2], (DEPTH, D_MODEL, D_IN), f32) * D_MODEL ** -0.5
    f_bias = jnp.broadcast_to(jnp.linspace(3.0, 6.0, ML_HEADS, dtype=f32), (DEPTH, ML_HEADS))
    i_bias = 0.1 * jax.random.normal(ks[3], (DEPTH, ML_HEADS), f32)
    b_gates = jnp.concatenate([i_bias, f_bias + 0.1 * jax.random.normal(ks[4], (DEPTH, ML_HEADS), f32)], axis=-1)
    conv_w = jax.random.normal(ks[5], (DEPTH, CONV_WIDTH, 2 * ML_WIDTH), f32) * CONV_WIDTH ** -0.5
    w_alpha = jax.random.normal(ks[6], (DEPTH, GLA_RANK, GLA_KW), f32) * GLA_RANK ** -0.5
    b_alpha = 0.1 * jax.random.normal(ks[7], (DEPTH, GLA_KW), f32)
    rel_bias = 0.1 * jax.random.normal(ks[8], (DEPTH, ATT_HEADS, 2 * REL_CLIP + 1), f32)
    ml_norm_g = 1.0 + 0.1 * jax.random.normal(ks[9], (DEPTH, ML_WIDTH), f32)
    gla_norm_g = 1.0 + 0.1 * jax.random.normal(ks[10], (DEPTH, GLA_WIDTH), f32)
    k_out, k_fin = jax.random.split(ks[11])
    w_out = jax.random.normal(k_out, (DEPTH, D_MIX, D_MODEL), f32) * D_MIX ** -0.5
    final_g = 1.0 + 0.1 * jax.random.normal(k_fin, (D_MODEL,), f32)
    return {"x": x, "norm_g": norm_g, "w_in": w_in, "b_gates": b_gates, "conv_w": conv_w,
            "w_alpha": w_alpha, "b_alpha": b_alpha, "rel_bias": rel_bias, "ml_norm_g": ml_norm_g,
            "gla_norm_g": gla_norm_g, "w_out": w_out, "final_g": final_g}

def first_block(x, norm_g, w_in, b_gates, conv_w, w_alpha, b_alpha, rel_bias, ml_norm_g, gla_norm_g, w_out, final_g):
    for l in range(DEPTH):
        x = hybrid_layer(x, norm_g[l], w_in[l], b_gates[l], conv_w[l], w_alpha[l], b_alpha[l], rel_bias[l],
                         ml_norm_g[l], gla_norm_g[l], w_out[l])
    return rmsnorm(x, final_g)


DEPTH_2 = 2

MEM_LEN = 256
N_MIXERS = 3
N_MIX_HEADS = 12
MIX_WIDTH = N_MIX_HEADS * HEAD_DIM
N_MEM_HEADS = 4
MEM_WIDTH = N_MEM_HEADS * HEAD_DIM
OUT_WIDTH = MIX_WIDTH + MEM_WIDTH
Q_BLOCK = 128
MLA_Q_RANK = 256
MLA_KV_RANK = 128
MLA_NOPE_DIM = 64
MLA_ROPE_DIM = 32
MLA_QK_DIM = MLA_NOPE_DIM + MLA_ROPE_DIM
MLA_V_DIM = 64
ROPE_THETA = 10000.0
MOBA_BLOCK = 256
MOBA_TOPK = 3
D_FF = 2816
CONV_WIDTH_2 = 3
POS_OFFSET_MAX = 1024

FOX_IN = 3 * MIX_WIDTH + N_MIX_HEADS + MEM_WIDTH
MLA_IN = MLA_Q_RANK + MLA_KV_RANK + MLA_ROPE_DIM + MEM_WIDTH
MOBA_IN = 3 * MIX_WIDTH + MEM_WIDTH


def rmsnorm_2(x, g):
    xf = x.astype(jnp.float32)
    y = xf * lax.rsqrt(jnp.mean(xf * xf, axis=-1, keepdims=True) + EPS)
    return (y * g.astype(jnp.float32)).astype(x.dtype)

def alibi_slopes(n_heads):
    return 2.0 ** (-8.0 * jnp.arange(1, n_heads + 1, dtype=jnp.float32) / n_heads)

def rope(x, cos, sin):
    half = x.shape[-1] // 2
    x1, x2 = x[..., :half], x[..., half:]
    return jnp.concatenate([x1 * cos - x2 * sin, x1 * sin + x2 * cos], axis=-1)

def to_heads(t, n_heads):
    b, s, _ = t.shape
    return t.reshape(b, s, n_heads, -1).transpose(0, 2, 1, 3)

def from_heads(t):
    b, h, s, d = t.shape
    return t.transpose(0, 2, 1, 3).reshape(b, s, h * d)

def causal_block_attention(q, k, v, log_decay=None):
    b, h, s, dk = q.shape
    nq = s // Q_BLOCK
    q_chunks = q.reshape(b, h, nq, Q_BLOCK, dk).transpose(2, 0, 1, 3, 4)
    key_idx = jnp.arange(s)
    xs = [q_chunks, jnp.arange(nq)]
    if log_decay is not None:
        xs.append(log_decay.reshape(b, h, nq, Q_BLOCK).transpose(2, 0, 1, 3))

    def step(args):
        qc, i = args[0], args[1]
        logits = jnp.einsum('bhqd,bhkd->bhqk', qc, k).astype(jnp.float32)
        if log_decay is not None:
            logits = logits + args[2][..., None] - log_decay[:, :, None, :]
        q_idx = i * Q_BLOCK + jnp.arange(Q_BLOCK)
        logits = jnp.where(key_idx[None, :] <= q_idx[:, None], logits, -jnp.inf)
        p = jax.nn.softmax(logits, axis=-1).astype(v.dtype)
        return jnp.einsum('bhqk,bhkd->bhqd', p, v)

    out = lax.map(step, tuple(xs))
    return out.transpose(1, 2, 0, 3, 4).reshape(b, h, s, v.shape[-1])

def fox_mixer(p, b_f, q_gain, k_gain):
    q, k, v, f = jnp.split(p, [MIX_WIDTH, 2 * MIX_WIDTH, 3 * MIX_WIDTH], axis=-1)
    q = rmsnorm_2(to_heads(q, N_MIX_HEADS), q_gain) * HEAD_DIM ** -0.5
    k = rmsnorm_2(to_heads(k, N_MIX_HEADS), k_gain)
    log_f = jax.nn.log_sigmoid(f.astype(jnp.float32) + b_f.astype(jnp.float32))
    cum = lax.cumsum(log_f, axis=1).transpose(0, 2, 1)
    return from_heads(causal_block_attention(q, k, to_heads(v, N_MIX_HEADS), cum))

def mla_mixer(p, cos, sin, qa_norm, kva_norm, w_q_up, w_kv_up, q_gain, k_gain):
    b, s, _ = p.shape
    q_lat, kv_lat, k_r = jnp.split(p, [MLA_Q_RANK, MLA_Q_RANK + MLA_KV_RANK], axis=-1)
    q = (rmsnorm_2(q_lat, qa_norm) @ w_q_up).reshape(b, s, N_MIX_HEADS, MLA_QK_DIM)
    kv = (rmsnorm_2(kv_lat, kva_norm) @ w_kv_up).reshape(b, s, N_MIX_HEADS, MLA_NOPE_DIM + MLA_V_DIM)
    q = jnp.concatenate([q[..., :MLA_NOPE_DIM], rope(q[..., MLA_NOPE_DIM:], cos, sin)], axis=-1)
    k_rope = jnp.broadcast_to(rope(k_r[:, :, None, :], cos, sin), (b, s, N_MIX_HEADS, MLA_ROPE_DIM))
    k = jnp.concatenate([kv[..., :MLA_NOPE_DIM], k_rope], axis=-1)
    v = kv[..., MLA_NOPE_DIM:]
    q = rmsnorm_2(q, q_gain).transpose(0, 2, 1, 3) * MLA_QK_DIM ** -0.5
    k = rmsnorm_2(k, k_gain).transpose(0, 2, 1, 3)
    return from_heads(causal_block_attention(q, k, v.transpose(0, 2, 1, 3)))

def moba_attention(q, k, v, positions, slopes):
    b, h, s, d = q.shape
    nb = -(-s // MOBA_BLOCK)
    pad = nb * MOBA_BLOCK - s
    kb = jnp.pad(k, ((0, 0), (0, 0), (0, pad), (0, 0))).reshape(b, h, nb, MOBA_BLOCK, d)
    vb = jnp.pad(v, ((0, 0), (0, 0), (0, pad), (0, 0))).reshape(b, h, nb, MOBA_BLOCK, d)
    posb = jnp.pad(positions, ((0, 0), (0, pad))).reshape(b, nb, MOBA_BLOCK)
    n_sel = min(MOBA_TOPK, nb - 1)
    nq = s // Q_BLOCK

    def chunks(t):
        tail = t.shape[3:]
        t = t.reshape((b, h, nq, Q_BLOCK) + tail)
        perm = (0, 2, 1, 3) + tuple(range(4, t.ndim))
        return t.transpose(perm).reshape((b * nq, h, Q_BLOCK) + tail)

    xs = [chunks(q), positions.reshape(b * nq, Q_BLOCK),
          jnp.repeat(jnp.arange(b), nq), jnp.tile(jnp.arange(nq), b)]
    if n_sel > 0:
        k_mean = kb.mean(axis=3)
        gate = jnp.einsum('bhsd,bhnd->bhsn', q, k_mean).astype(jnp.float32)
        q_blk = jnp.arange(s) // MOBA_BLOCK
        gate = jnp.where(jnp.arange(nb)[None, :] < q_blk[:, None], gate, -jnp.inf)
        g_val, g_idx = lax.top_k(gate, n_sel)
        xs += [chunks(g_idx), chunks(jnp.isfinite(g_val))]

    def step(args):
        qc, pq, bi, ci = args[0], args[1], args[2], args[3]
        t_idx = ci * Q_BLOCK + jnp.arange(Q_BLOCK)
        own = (ci * Q_BLOCK) // MOBA_BLOCK
        kb_b, vb_b, posb_b = kb[bi], vb[bi], posb[bi]
        k_own = lax.dynamic_index_in_dim(kb_b, own, axis=1, keepdims=False)
        v_own = lax.dynamic_index_in_dim(vb_b, own, axis=1, keepdims=False)
        pos_own = lax.dynamic_index_in_dim(posb_b, own, axis=0, keepdims=False)
        dist_own = (pq[:, None] - pos_own[None, :]).astype(jnp.float32)
        s_own = (jnp.einsum('hqd,hjd->hqj', qc, k_own).astype(jnp.float32)
                 - slopes[:, None, None] * dist_own[None])
        own_idx = own * MOBA_BLOCK + jnp.arange(MOBA_BLOCK)
        s_own = jnp.where(own_idx[None, None, :] <= t_idx[None, :, None], s_own, -jnp.inf)
        if n_sel == 0:
            p_own = jax.nn.softmax(s_own, axis=-1).astype(v.dtype)
            return jnp.einsum('hqj,hjd->hqd', p_own, v_own)
        idx, ok = args[4], args[5]
        k_sel = jax.vmap(lambda blocks, i: blocks[i])(kb_b, idx)
        v_sel = jax.vmap(lambda blocks, i: blocks[i])(vb_b, idx)
        dist_sel = (pq[None, :, None, None] - posb_b[idx]).astype(jnp.float32)
        s_sel = (jnp.einsum('hqd,hqkjd->hqkj', qc, k_sel).astype(jnp.float32)
                 - slopes[:, None, None, None] * dist_sel)
        s_sel = jnp.where(ok[..., None], s_sel, -jnp.inf).reshape(h, Q_BLOCK, n_sel * MOBA_BLOCK)
        p = jax.nn.softmax(jnp.concatenate([s_sel, s_own], axis=-1), axis=-1).astype(v.dtype)
        p_sel = p[..., :n_sel * MOBA_BLOCK].reshape(h, Q_BLOCK, n_sel, MOBA_BLOCK)
        p_own = p[..., n_sel * MOBA_BLOCK:]
        return (jnp.einsum('hqkj,hqkjd->hqd', p_sel, v_sel)
                + jnp.einsum('hqj,hjd->hqd', p_own, v_own))

    out = lax.map(step, tuple(xs))
    return out.reshape(b, nq, h, Q_BLOCK, d).transpose(0, 2, 1, 3, 4).reshape(b, h, s, d)

def moba_mixer(p, positions, q_gain, k_gain):
    q, k, v = jnp.split(p, [MIX_WIDTH, 2 * MIX_WIDTH], axis=-1)
    q = rmsnorm_2(to_heads(q, N_MIX_HEADS), q_gain) * HEAD_DIM ** -0.5
    k = rmsnorm_2(to_heads(k, N_MIX_HEADS), k_gain)
    out = moba_attention(q, k, to_heads(v, N_MIX_HEADS), positions, alibi_slopes(N_MIX_HEADS))
    return from_heads(out)

def memory_cross(qm, k_mem, v_mem, q_gain, k_gain):
    b, s, _ = qm.shape
    q = rmsnorm_2(qm.reshape(b, s, N_MEM_HEADS, HEAD_DIM), q_gain) * HEAD_DIM ** -0.5
    k = rmsnorm_2(k_mem, k_gain)
    logits = jnp.einsum('bshd,bmhd->bhsm', q, k).astype(jnp.float32)
    p = jax.nn.softmax(logits, axis=-1).astype(v_mem.dtype)
    return jnp.einsum('bhsm,bmhd->bshd', p, v_mem).reshape(b, s, MEM_WIDTH)

def conv_ffn(h, w_up, conv_w, conv_b, w_down):
    u = h @ w_up
    c = u.shape[-1]
    u = lax.conv_general_dilated(u, conv_w[:, None, :].astype(u.dtype), window_strides=(1,),
                                 padding=[(CONV_WIDTH_2 - 1, 0)],
                                 dimension_numbers=('NWC', 'WIO', 'NWC'),
                                 feature_group_count=c) + conv_b
    gate, val = jnp.split(u, 2, axis=-1)
    return (jax.nn.silu(gate) * val) @ w_down

def second_inputs(seed: int = 0) -> dict:
    key = jax.random.key(seed)
    ks = iter(jax.random.split(key, 32))
    f32 = jnp.float32

    def dense(shape):
        return jax.random.normal(next(ks), shape, f32) * shape[-2] ** -0.5

    def gain(shape):
        return 1.0 + 0.05 * jax.random.normal(next(ks), shape, f32)

    n_fox = len(range(0, DEPTH_2, N_MIXERS))
    n_mla = len(range(1, DEPTH_2, N_MIXERS))
    n_moba = len(range(2, DEPTH_2, N_MIXERS))
    x = jax.random.normal(next(ks), (BATCH, SEQ, D_MODEL), f32)
    mem = jax.random.normal(next(ks), (BATCH, MEM_LEN, D_MODEL), f32)
    positions = (jnp.arange(SEQ, dtype=jnp.int32)[None, :]
                 + jax.random.randint(next(ks), (BATCH, 1), 0, POS_OFFSET_MAX, dtype=jnp.int32))
    return {
        'x': x,
        'mem': mem,
        'positions': positions,
        'norm_mix': gain((DEPTH_2, D_MODEL)),
        'norm_ffn': gain((DEPTH_2, D_MODEL)),
        'w_out': dense((DEPTH_2, OUT_WIDTH, D_MODEL)),
        'mem_norm': gain((D_MODEL,)),
        'w_mem_kv': dense((D_MODEL, 2 * MEM_WIDTH)),
        'mem_q_gain': gain((DEPTH_2, HEAD_DIM)),
        'mem_k_gain': gain((DEPTH_2, HEAD_DIM)),
        'fox_w_in': dense((n_fox, D_MODEL, FOX_IN)),
        'fox_b_f': jax.random.uniform(next(ks), (n_fox, N_MIX_HEADS), f32, 1.0, 5.0),
        'fox_q_gain': gain((n_fox, HEAD_DIM)),
        'fox_k_gain': gain((n_fox, HEAD_DIM)),
        'mla_w_in': dense((n_mla, D_MODEL, MLA_IN)),
        'mla_qa_norm': gain((n_mla, MLA_Q_RANK)),
        'mla_kva_norm': gain((n_mla, MLA_KV_RANK)),
        'mla_w_q_up': dense((n_mla, MLA_Q_RANK, N_MIX_HEADS * MLA_QK_DIM)),
        'mla_w_kv_up': dense((n_mla, MLA_KV_RANK, N_MIX_HEADS * (MLA_NOPE_DIM + MLA_V_DIM))),
        'mla_q_gain': gain((n_mla, MLA_QK_DIM)),
        'mla_k_gain': gain((n_mla, MLA_QK_DIM)),
        'moba_w_in': dense((n_moba, D_MODEL, MOBA_IN)),
        'moba_q_gain': gain((n_moba, HEAD_DIM)),
        'moba_k_gain': gain((n_moba, HEAD_DIM)),
        'ffn_w_up': dense((DEPTH_2, D_MODEL, 2 * D_FF)),
        'ffn_conv_w': dense((DEPTH_2, CONV_WIDTH_2, 2 * D_FF)),
        'ffn_conv_b': 0.01 * jax.random.normal(next(ks), (DEPTH_2, 2 * D_FF), f32),
        'ffn_w_down': dense((DEPTH_2, D_FF, D_MODEL)),
    }

def second_block(x, mem, positions, norm_mix, norm_ffn, w_out, mem_norm, w_mem_kv, mem_q_gain,
              mem_k_gain, fox_w_in, fox_b_f, fox_q_gain, fox_k_gain, mla_w_in, mla_qa_norm,
              mla_kva_norm, mla_w_q_up, mla_w_kv_up, mla_q_gain, mla_k_gain, moba_w_in,
              moba_q_gain, moba_k_gain, ffn_w_up, ffn_conv_w, ffn_conv_b, ffn_w_down):
    b, m = mem.shape[0], mem.shape[1]
    mem_kv = rmsnorm_2(mem, mem_norm) @ w_mem_kv
    k_mem = mem_kv[..., :MEM_WIDTH].reshape(b, m, N_MEM_HEADS, HEAD_DIM)
    v_mem = mem_kv[..., MEM_WIDTH:].reshape(b, m, N_MEM_HEADS, HEAD_DIM)
    inv_freq = ROPE_THETA ** (-jnp.arange(0, MLA_ROPE_DIM, 2, dtype=jnp.float32) / MLA_ROPE_DIM)
    ang = positions.astype(jnp.float32)[..., None] * inv_freq
    cos = jnp.cos(ang)[:, :, None, :].astype(x.dtype)
    sin = jnp.sin(ang)[:, :, None, :].astype(x.dtype)

    for i in range(DEPTH_2):
        kind, j = i % N_MIXERS, i // N_MIXERS
        h = rmsnorm_2(x, norm_mix[i])
        if kind == 0:
            p = h @ fox_w_in[j]
            o_mix = fox_mixer(p[..., :-MEM_WIDTH], fox_b_f[j], fox_q_gain[j], fox_k_gain[j])
        elif kind == 1:
            p = h @ mla_w_in[j]
            o_mix = mla_mixer(p[..., :-MEM_WIDTH], cos, sin, mla_qa_norm[j], mla_kva_norm[j],
                              mla_w_q_up[j], mla_w_kv_up[j], mla_q_gain[j], mla_k_gain[j])
        else:
            p = h @ moba_w_in[j]
            o_mix = moba_mixer(p[..., :-MEM_WIDTH], positions, moba_q_gain[j], moba_k_gain[j])
        o_mem = memory_cross(p[..., -MEM_WIDTH:], k_mem, v_mem, mem_q_gain[i], mem_k_gain[i])
        x = x + jnp.concatenate([o_mix, o_mem], axis=-1) @ w_out[i]
        x = x + conv_ffn(rmsnorm_2(x, norm_ffn[i]), ffn_w_up[i], ffn_conv_w[i], ffn_conv_b[i],
                         ffn_w_down[i])
    return x


def setup_inputs(seed=0):
    out = dict(first_inputs(seed))
    for name, value in second_inputs(seed + 1).items():
        if name != "x":
            out[name + "_2"] = value
    return out


def reference(
    x, norm_g, w_in, b_gates, conv_w, w_alpha, b_alpha, rel_bias, ml_norm_g, gla_norm_g, w_out,
    final_g, mem_2, positions_2, norm_mix_2, norm_ffn_2, w_out_2, mem_norm_2, w_mem_kv_2,
    mem_q_gain_2, mem_k_gain_2, fox_w_in_2, fox_b_f_2, fox_q_gain_2, fox_k_gain_2, mla_w_in_2,
    mla_qa_norm_2, mla_kva_norm_2, mla_w_q_up_2, mla_w_kv_up_2, mla_q_gain_2, mla_k_gain_2,
    moba_w_in_2, moba_q_gain_2, moba_k_gain_2, ffn_w_up_2, ffn_conv_w_2, ffn_conv_b_2,
    ffn_w_down_2,
):
    x = first_block(
        x, norm_g, w_in, b_gates, conv_w, w_alpha, b_alpha, rel_bias, ml_norm_g, gla_norm_g,
        w_out, final_g,
    )
    return second_block(
        x, mem_2, positions_2, norm_mix_2, norm_ffn_2, w_out_2, mem_norm_2, w_mem_kv_2,
        mem_q_gain_2, mem_k_gain_2, fox_w_in_2, fox_b_f_2, fox_q_gain_2, fox_k_gain_2,
        mla_w_in_2, mla_qa_norm_2, mla_kva_norm_2, mla_w_q_up_2, mla_w_kv_up_2, mla_q_gain_2,
        mla_k_gain_2, moba_w_in_2, moba_q_gain_2, moba_k_gain_2, ffn_w_up_2, ffn_conv_w_2,
        ffn_conv_b_2, ffn_w_down_2,
    )


_drawn_inputs = setup_inputs


def setup_inputs(seed=0):
    import zlib

    import numpy as np

    out = dict(_drawn_inputs(seed))
    spreads = {}
    factors = {'b_alpha': 3.353,
     'rel_bias': 8.0,
     'mem_norm_2': 8.0,
     'mem_q_gain_2': 8.0,
     'mem_k_gain_2': 8.0,
     'fox_q_gain_2': 3.997,
     'fox_k_gain_2': 4.813,
     'mla_qa_norm_2': 8.0,
     'mla_kva_norm_2': 5.508,
     'mla_q_gain_2': 8.0,
     'mla_k_gain_2': 8.0,
     'ffn_conv_b_2': 5.606}
    for name, (base, spread) in spreads.items():
        noise = np.random.default_rng([zlib.crc32(name.encode()), seed]).standard_normal(out[name].shape)
        drawn = base * np.exp(spread * noise) if base else spread * noise
        out[name] = jnp.asarray(drawn.astype(out[name].dtype))
    for name, factor in factors.items():
        out[name] = (out[name] * factor).astype(out[name].dtype)
    return out
```

```python
from contextlib import ExitStack

import numpy as np
import concourse.bass as bass
from concourse import mybir

F32 = mybir.dt.float32
F32R = mybir.dt.float32r
BF16 = mybir.dt.bfloat16
I32 = mybir.dt.int32
ALU = mybir.AluOpType
ACT = mybir.ActivationFunctionType
AX = mybir.AxisListType.X
P = 128
T = 512
D = 1024
EPS = 1e-6
NEG = -1e30
FF = 2816
CAP = 1536


def plan_chunks():
    out = []

    def fm(key, name, l, kt, c0, cols):
        for c in range(c0, c0 + cols, P):
            out.append((key, name, l, 0, kt, c, P))

    def tm(key, name, l, c0, cols, step=384):
        for c in range(c0, c0 + cols, step):
            n = min(step, c0 + cols - c)
            for half in range(2):
                out.append((key, name, l, half * 512, 4, c, n))

    fm("memk", "w_mem_kv_2", None, 8, 0, 256)
    tm("memv", "w_mem_kv_2", None, 256, 256)
    fm("aq", "w_in", 0, 8, 0, 384)
    fm("ak", "w_in", 0, 8, 384, 384)
    tm("av", "w_in", 0, 768, 384)
    tm("ag", "w_in", 0, 1152, 384)
    fm("mqk", "w_in", 0, 8, 1536, 768)
    tm("mv", "w_in", 0, 2304, 384)
    tm("mo", "w_in", 0, 2688, 384)
    fm("gate", "w_in", 0, 8, 3072, 128)
    tm("mg", "w_in", 0, 3084, 384)
    fm("gqk", "w_in", 0, 8, 3468, 256)
    tm("gv", "w_in", 0, 3724, 256)
    fm("ga", "w_in", 0, 8, 3980, 128)
    tm("gg", "w_in", 0, 3996, 256)
    tm("wo1", "w_out", 0, 0, 1024)

    def tail(l):
        fm("wo", "w_out_2", l, 8, 0, 1024)
        for half in range(2):
            for ct in range(11):
                c = (11 * half + ct) * P
                fm("up", "ffn_w_up_2", l, 8, c, P)
                fm("up", "ffn_w_up_2", l, 8, FF + c, P)
            for m in range(8):
                out.append(("down", "ffn_w_down_2", l, half * 1408, 11, m * P, P))

    fm("fqk", "fox_w_in_2", 0, 8, 0, 1536)
    tm("fv", "fox_w_in_2", 0, 1536, 768)
    fm("ff", "fox_w_in_2", 0, 8, 2304, 128)
    fm("fm", "fox_w_in_2", 0, 8, 2316, 256)
    tail(0)
    fm("ql", "mla_w_in_2", 0, 8, 0, 256)
    fm("kvl", "mla_w_in_2", 0, 8, 256, 128)
    out.append(("kr", "mla_w_in_2", 0, 0, 8, 384, 32))
    fm("mm", "mla_w_in_2", 0, 8, 416, 256)
    for c in range(0, 1152, 384):
        out.append(("qup", "mla_w_q_up_2", 0, 0, 2, c, 384))
    for c in range(0, 1536, 512):
        out.append(("kvup", "mla_w_kv_up_2", 0, 0, 1, c, 512))
    tail(1)
    return out


VECS = {}


def _vecs():
    at = 0
    for name, n in (("norm_g", 8), ("conv_w", 24), ("norm_mix", 16), ("norm_ffn", 16), ("mem_norm", 8),
                    ("qa", 2), ("kva", 1), ("b_alpha", 1), ("fq", 1), ("fk", 1), ("mq", 2), ("mk", 2),
                    ("cw0", 132), ("cb0", 44), ("cw1", 132), ("cb1", 44)):
        VECS[name] = (at, n)
        at += n
    return at


NVEC = _vecs()


class Handle:
    __slots__ = ("eng", "used", "val")

    def __init__(self, eng):
        self.eng, self.used, self.val = eng, False, 0


class Queues:

    ENG = ("pe", "act", "dve", "pool", "sp")

    def __init__(self):
        self.q = {e: [] for e in self.ENG}
        self.held = {e: [] for e in self.ENG}
        self.end = {}

    def op(self, eng, fn, deps):
        h = Handle(eng)
        flat = list(self.held[eng])
        self.held[eng] = []
        stack = list(deps)
        while stack:
            d = stack.pop()
            if d is None:
                continue
            if isinstance(d, (list, tuple)) and not (len(d) == 3 and d[0] == "dma"):
                stack.extend(d)
                continue
            if isinstance(d, Handle):
                d.used = True
            flat.append(d)
        if eng == "pool" and self.q[eng]:
            self.q[eng][-1][2].used = True
            flat.append(self.q[eng][-1][2])
        self.q[eng].append((fn, flat, h))
        self.end[eng] = h
        return h

    def last(self):
        return [self.end[e] for e in ("pe", "act", "dve", "pool") if e in self.end]

    def barrier(self):
        now = self.last()
        for h in now:
            h.used = True
        for e in ("pe", "act", "dve", "pool"):
            self.held[e] = self.held[e] + now
        return now

    def number(self):
        for e in self.ENG:
            n = 0
            for _, _, h in self.q[e]:
                if h.used:
                    n += 1
                    h.val = n

    def emit(self, eng, e, sems):
        seen = {}
        for fn, deps, h in self.q[eng]:
            need = {}
            for d in deps:
                s, v = (sems[d.eng], d.val) if isinstance(d, Handle) else (d[1], d[2])
                k = id(s)
                if v > seen.get(k, 0) and v > need.get(k, (None, 0))[1]:
                    need[k] = (s, v)
            for k, (s, v) in need.items():
                e.wait_ge(s, v)
                seen[k] = v
            ins = fn(e)
            if h.used:
                ins.then_inc(sems[eng], 1)


class Slot:

    def __init__(self, t):
        self.t, self.free = t, []

    def take(self):
        f, self.free = self.free, None
        assert f is not None, "slot in use"
        return f

    def done(self, *hs):
        self.free = list(hs)


class Ring:
    def __init__(self, slots):
        self.s, self.i = slots, 0

    def take(self):
        s = self.s[self.i % len(self.s)]
        self.i += 1
        return s, s.take()


def build(nc, d, out):
    q = Queues()
    ctx = ExitStack()
    chunks = plan_chunks()

    def sem(n):
        return ctx.enter_context(nc.semaphore(n))

    def sbuf(name, shape, dt=F32, scope=None):
        return (scope or ctx).enter_context(nc.sbuf_tensor(name, shape, dt))

    sems = {e: sem("s_" + e) for e in Queues.ENG}

    def mm(o, lhsT, rhs, start, stop, *deps):
        return q.op("pe", lambda e: e.matmul(o, lhsT, rhs, start=start, stop=stop), deps)

    def mmx(o, lhsT, rhs, start, stop, *deps):
        return q.op("pe", lambda e: e.matmul(o, lhsT, rhs, start=start, stop=stop, skip_group_check=True), deps)

    def tr(o, i, ident, *deps):
        return q.op("pe", lambda e: e.transpose(o, i, ident), deps)

    def act(o, i, f, *deps, bias=0.0, scale=1.0, acc=None):
        if acc is None:
            return q.op("act", lambda e: e.activation(o, i, f, bias=bias, scale=scale), deps)
        return q.op("act", lambda e: e.activation(o, i, f, bias=bias, scale=scale, accum_out=acc), deps)

    def acopy(o, i, *deps):
        return q.op("act", lambda e: e.copy(o, i), deps)

    def tt(o, a, b, op, *deps, eng="dve"):
        return q.op(eng, lambda e: e.tensor_tensor(o, a, b, op), deps)

    def ts(o, a, s1, s2, op0, op1, *deps, eng="dve"):
        if op1 is None:
            return q.op(eng, lambda e: e.tensor_scalar(o, a, s1, None, op0), deps)
        return q.op(eng, lambda e: e.tensor_scalar(o, a, s1, s2, op0, op1), deps)

    def stt(o, a, s, b, op0, op1, *deps, eng="dve"):
        return q.op(eng, lambda e: e.scalar_tensor_tensor(out=o, in0=a, scalar=s, in1=b, op0=op0, op1=op1), deps)

    def cp(o, i, *deps, eng="dve"):
        return q.op(eng, lambda e: e.tensor_copy(o, i), deps)

    def recip(o, i, *deps):
        return q.op("dve", lambda e: e.reciprocal(o, i), deps)

    def red(o, i, op, *deps, negate=None):
        return q.op("dve", lambda e: e.tensor_reduce(o, i, AX, op, negate=negate), deps)

    def mset(ap, v, *deps, eng="pool"):
        return q.op(eng, lambda e: e.memset(ap, v), deps)

    def sel(ap, pattern, cmp, fill, base, cm, *deps):
        return q.op("pool", lambda e: e.affine_select(out=ap, in_=ap, pattern=pattern, compare_op=cmp, fill=fill,
                                                       base=base, channel_multiplier=cm), deps)

    dcount = {}

    def dma(o, i, s, *deps):
        n = dcount[id(s)] = dcount.get(id(s), 0) + 16
        q.op("sp", lambda e: e.dma_start(o, i).then_inc(s, 16), deps)
        return ("dma", s, n)

    def table(name):
        end = q.end.get("act")
        q.op("act", lambda e: e.preload_act_table_set(name), ())
        if end is not None:
            q.end["act"] = end

    MUL, ADD, SUB, MAX, MIN = ALU.mult, ALU.add, ALU.subtract, ALU.max, ALU.min

    banks = [Slot(ctx.enter_context(nc.psum_tensor(f"bank{i}", [P, 512], F32))) for i in range(8)]
    RA = Ring(banks)
    RS, RT, RO = Ring(banks[0:4]), Ring(banks[4:6]), Ring(banks[6:8])

    ident = sbuf("ident", [P, P])
    identb = sbuf("identb", [P, P], BF16)
    maskb = sbuf("maskb", [P, P], BF16)
    ones = sbuf("ones", [P, P])
    blk = sbuf("blk", [P, P])
    epsc = sbuf("epsc", [P, 1])
    vc = sbuf("vc", [P, NVEC])
    small = sbuf("small", [P, 256])
    stage = [Slot(sbuf(f"wstage{i}", [P, CAP])) for i in range(3)]
    whi = [Slot(sbuf(f"whi{i}", [P, CAP], F32R)) for i in range(3)]
    wlo = [Slot(sbuf(f"wlo{i}", [P, CAP], F32R)) for i in range(3)]
    RST, RHI, RLO = Ring(stage), Ring(whi), Ring(wlo)
    hhi = sbuf("hhi", [P, 8, T], F32R)
    hlo = sbuf("hlo", [P, 8, T], F32R)
    xT = sbuf("xT", [P, 8, T])
    tmp = Ring([Slot(sbuf(f"tmp{i}", [P, T])) for i in range(5)])
    hold = Ring([Slot(sbuf(f"hold{i}", [P, T])) for i in range(1)])
    kmn = sbuf("kmn", [P, 2, 256])
    kmg = sbuf("kmg", [P, 2, 256])
    vmem = sbuf("vmem", [P, 2, 256])
    fb = sbuf("fb", [12, 1])
    sinT = sbuf("sinT", [P, 4, 16])
    cosT = sbuf("cosT", [P, 4, 16])

    s_stage = [sem(f"s_w{i}") for i in range(3)]
    s_x, s_c, s_m, s_u = sem("s_x"), sem("s_c"), sem("s_m"), sem("s_u")
    s_out = [sem("s_out0"), sem("s_out1")]

    def col(name, i=0, n=P):
        a = VECS[name][0] + i
        return vc[0:n, a:a + 1]

    mscope = ExitStack()
    xt = sbuf("xt", [P, 4, D], scope=mscope)
    yt = xT[:].rearrange("p a b -> p (a b)").rearrange("p (c n) -> p c n", c=4)
    iscope = ExitStack()
    memt = sbuf("memt", [P, 2, D], scope=iscope)
    l_mem = dma(memt[:], d["mem_2"].rearrange("a (c p) n -> p (a c) n", p=P), s_m)
    l_vc = dma(vc[:], d["vecs"], s_c)
    l_fb = dma(fb[:], d["fox_b_f_2"].rearrange("a n -> n a"), s_c)
    l_c = l_fb

    offs, at = [], 0
    for (_, _, _, _, kt, _, n) in chunks:
        offs.append(at)
        at += P * kt * n

    class W:
        pass

    state = {"next": 0, "loaded": 0, "split": 0}
    staged, ready = {}, {}

    def load(i):
        _, _, _, _, kt, _, n = chunks[i]
        w = kt * n
        s, free = RST.take()
        k = (RST.i - 1) % 3
        src = d["wts"][offs[i]:offs[i] + P * w].rearrange("(p w) -> p w", p=P)
        staged[i] = (s, dma(s.t[:, 0:w], src, s_stage[k], free))

    def split(i):
        _, _, _, _, kt, _, n = chunks[i]
        w = kt * n
        s, l = staged.pop(i)
        hi, f1 = RHI.take()
        lo, f2 = RLO.take()
        a = acopy(hi.t[:, 0:w], s.t[:, 0:w], l, f1)
        b = tt(lo.t[:, 0:w], s.t[:, 0:w], hi.t[:, 0:w].bitcast(F32), SUB, a, f2)
        s.done(b)
        o = W()
        o.hi = hi.t[:, 0:w].rearrange("p (k n) -> p k n", k=kt)
        o.lo = lo.t[:, 0:w].rearrange("p (k n) -> p k n", k=kt)
        o.rdy = b
        o.done = lambda h: (hi.done(h), lo.done(h))
        ready[i] = o

    def weights(key):
        i = state["next"]
        state["next"] += 1
        assert chunks[i][0] == key, (chunks[i], key)
        while state["loaded"] < min(len(chunks), i + 3):
            load(state["loaded"])
            state["loaded"] += 1
            while state["split"] < min(state["loaded"], i + 2):
                split(state["split"])
                state["split"] += 1
        while state["split"] < min(state["loaded"], i + 2):
            split(state["split"])
            state["split"] += 1
        return ready.pop(i)

    for _ in range(3):
        load(state["loaded"])
        state["loaded"] += 1
    l_x = dma(xt[:], d["x"].rearrange("a (c p) n -> p (a c) n", p=P), s_x)

    table("natural_log_exp_and_others")
    c0 = mset(ident[:], 0.0)
    c_id = sel(ident[:], [[-1, P]], ALU.not_equal, 1.0, 0, 1, c0)
    c1 = mset(identb[:], 0.0)
    c_idb = sel(identb[:], [[-1, P]], ALU.not_equal, 1.0, 0, 1, c1)
    c2 = mset(maskb[:], 0.0)
    c_mk = sel(maskb[:], [[-1, P]], ALU.is_ge, NEG, 0, 1, c2)
    c_1 = mset(ones[:], 1.0)
    c3 = mset(blk[:], 0.0)
    c4 = mset(blk[0:64, 0:64], 1.0, c3)
    c5 = mset(blk[64:128, 64:128], 1.0, c3)
    c_e = mset(epsc[:], EPS)
    C = [c_id, c_idb, c_mk, c_1, c4, c5, c_e]

    def mm3(o, lh, ll, rh, rl, start, stop, *deps):
        mm(o, lh, rh, start, False, *deps)
        mm(o, lh, rl, False, False)
        return mm(o, ll, rh, False, stop)

    def fm_tile(key, xh, xl, kt, n, *deps):
        w = weights(key)
        b, free = RA.take()
        for k in range(kt):
            h = mm3(b.t[:, 0:n], w.hi[:, k, :], w.lo[:, k, :], xh[:, k, 0:n], xl[:, k, 0:n],
                    k == 0, k == kt - 1, w.rdy, free, deps)
        w.done(h)
        return b, h

    def tm_group(key, xh, xl, tiles, cols, *deps):
        bs = [RA.take() for _ in range(tiles)]
        hs = [None] * tiles
        for half in range(2):
            w = weights(key)
            for c in range(tiles):
                for k in range(4):
                    kk = 4 * half + k
                    hs[c] = mm3(bs[c][0].t[:, 0:cols], xh[:, kk, c * P:(c + 1) * P], xl[:, kk, c * P:(c + 1) * P],
                                w.hi[:, k, :], w.lo[:, k, :], kk == 0, kk == 7, w.rdy, bs[c][1], deps)
            w.done(hs[tiles - 1])
        return [(bs[c][0], hs[c]) for c in range(tiles)]

    flip = [0]

    def evac(o, i, *deps):
        flip[0] += 1
        return acopy(o, i, *deps) if flip[0] % 2 else cp(o, i, *deps)

    def split_bank(b, h, hi, lo, scale=None):
        n = hi.shape[-1]
        if scale is None:
            a = acopy(hi, b.t[:, 0:n], h)
            z = tt(lo, b.t[:, 0:n], hi.bitcast(F32), SUB, a)
        else:
            a = act(hi, b.t[:, 0:n], ACT.Identity, h, scale=scale)
            z = stt(lo, b.t[:, 0:n], scale, hi.bitcast(F32), MUL, SUB, a)
        b.done(z)
        return z

    def rstd_of(o, i, n, *deps):
        a = act(o, i, ACT.Ln, *deps, scale=1.0 / n, bias=epsc[0:i.shape[0], :])
        return act(o, o, ACT.Exp, a, scale=-0.5)

    def token_rms(src, tiles, at, *deps):
        t, free = tmp.take()
        t2, free2 = tmp.take()
        sc = small[:, at:at + 2 * tiles]
        last = None
        for c in range(tiles):
            for hf in range(2):
                last = act((t, t2)[hf].t[:], src[:, c, hf * 512:(hf + 1) * 512], ACT.Square, *deps, free, free2, last,
                           acc=sc[:, 2 * c + hf:2 * c + hf + 1])
        t.done(last)
        t2.done(last)
        a = tt(small[:, at + 16:at + 16 + tiles], small[:, at:at + 2 * tiles:2], small[:, at + 1:at + 2 * tiles:2], ADD, last)
        return rstd_of(small[:, at + 16:at + 16 + tiles], small[:, at + 16:at + 16 + tiles], D, a), at + 16

    def transpose_tokens(src, tiles, ready_, dst):
        r = None
        for kt in range(8):
            b, free = RA.take()
            for c in range(tiles):
                h = tr(b.t[:, c * P:(c + 1) * P], src[:, c, kt * P:(kt + 1) * P], ident[:], ready_, free, C)
            r = dst(kt, b, h)
        return r

    r, at_ = token_rms(memt, 2, 0, l_mem, C)
    for c in range(2):
        r2 = ts(memt[:, c, :], memt[:, c, :], small[:, at_ + c:at_ + c + 1], None, MUL, None, r, l_c)
    mh = hhi[:].rearrange("p a b -> p (a b)")[:, 0:2048].rearrange("p (k n) -> p k n", k=8)
    ml = hlo[:].rearrange("p a b -> p (a b)")[:, 0:2048].rearrange("p (k n) -> p k n", k=8)
    mr = transpose_tokens(memt, 2, r2, lambda kt, b, h: split_bank(b, h, mh[:, kt, :], ml[:, kt, :], col("mem_norm", kt)))
    for m in range(2):
        b, h = fm_tile("memk", mh, ml, 8, 256, mr)
        t, free = tmp.take()
        a = act(t.t[:, 0:256], b.t[:, 0:256], ACT.Square, h, free)
        b2, free = RA.take()
        g = mm(b2.t[:, 0:256], blk[:], t.t[:, 0:256], True, True, a, free, C)
        t2, free = tmp.take()
        a = rstd_of(t2.t[:, 0:256], b2.t[:, 0:256], 64, g, free)
        z = tt(kmn[:, m, :], b.t[:, 0:256], t2.t[:, 0:256], MUL, a)
        t.done(g)
        b2.done(a)
        b.done(z)
        t2.done(z)
    for c, (b, h) in enumerate(tm_group("memv", mh, ml, 2, 256, mr)):
        z = evac(vmem[:, c, :], b.t[:, 0:256], h)
        b.done(z)
    q.barrier()
    iscope.close()

    xs = ExitStack()
    xn = sbuf("xn", [P, 4, D], scope=xs)
    r, at_ = token_rms(xt, 4, 0, l_x, C)
    for c in range(4):
        r2 = ts(xn[:, c, :], xt[:, c, :], small[:, at_ + c:at_ + c + 1], None, MUL, None, r)
    hr = transpose_tokens(xn, 4, r2, lambda kt, b, h: split_bank(b, h, hhi[:, kt, :], hlo[:, kt, :], col("norm_g", kt)))
    q.barrier()
    xs.close()

    def attention(name, nh, qT, kT, v, width, causal, dst, bias=None, head_start=None, nj=None):
        sc = ExitStack()
        pr = tmp
        pt = Ring([Slot(sbuf(f"{name}_pt{i}", [P, T], scope=sc)) for i in range(2)])
        st = Ring([Slot(sbuf(f"{name}_s{i}", [P, T], scope=sc)) for i in range(2)]) if bias else None
        mx = sbuf(f"{name}_mx", [P, nh, 4], scope=sc)
        rs = sbuf(f"{name}_rs", [P, nh, 4], scope=sc)
        items = [(h, i) for h in range(nh) for i in range(4)]
        S, PR, PT, O = {}, {}, {}, {}
        fin = []

        def score(t):
            h, i = items[t]
            if i == 0 and head_start:
                head_start(h)
            n = width(i)
            b, free = RS.take()
            (qa, qh), (ka, kh) = qT(h, i), kT(h, n)
            g = mm(b.t[:, 0:n], qa, ka, True, not causal, qh, kh, free)
            if causal:
                g = mm(b.t[:, n - P:n], identb[:], maskb[:], False, True, C)
            S[t] = (b, g, n)

        def soft(t):
            h, i = items[t]
            b, g, n = S.pop(t)
            p_, free = pr.take()
            m = mx[:, h, i:i + 1]
            if bias:
                s_, f2 = st.take()
                ba, bh = bias(h, i, n)
                z = q.op("dve", lambda e: e.tensor_tensor_reduce(s_.t[:, 0:n], b.t[:, 0:n], ba, 1.0, -3e38, ADD,
                                                                 MAX, m), (g, bh, f2))
                b.done(z)
                z = ts(m, m, -1.0, None, MUL, None, z)
                a = act(p_.t[:, 0:n], s_.t[:, 0:n], ACT.Exp, z, free, bias=m, acc=rs[:, h, i:i + 1])
                s_.done(a)
            else:
                z = red(m, b.t[:, 0:n], MAX, g, negate=True)
                a = act(p_.t[:, 0:n], b.t[:, 0:n], ACT.Exp, z, free, bias=m, acc=rs[:, h, i:i + 1])
                b.done(a)
            PR[t] = (p_, a, n)

        def turn(t):
            p_, a, n = PR.pop(t)
            b, free = RT.take()
            for j in range(n // P):
                g = tr(b.t[:, j * P:(j + 1) * P], p_.t[:, j * P:(j + 1) * P], ident[:], a, free)
            p_.done(g)
            s_, f2 = pt.take()
            z = evac(s_.t[:, 0:n], b.t[:, 0:n], g, f2)
            b.done(z)
            PT[t] = (s_, z, n)

        def pv(t):
            h, i = items[t]
            s_, z, n = PT.pop(t)
            if t % 8 == 0:
                O[t // 8] = RO.take()
            b, free = O[t // 8]
            o = b.t[:, ((t % 8) * 64):((t % 8) * 64) + 64]
            for j in range(n // P):
                va, vh = v(h, j)
                g = mm(o, s_.t[:, j * P:(j + 1) * P], va, j == 0, j == n // P - 1, z, vh, free)
            s_.done(g)
            if t % 8 == 7:
                h0 = h - 1
                rr = rs[:, h0:h0 + 2, :]
                a = recip(rr, rr, g)
                for ii in range(4):
                    ov = b.t[:, :].rearrange("p (h i n) -> p h i n", h=2, i=4)[:, :, ii, :]
                    z = tt(dst(h0, ii), ov, rr[:, :, ii:ii + 1].to_broadcast([P, 2, 64]), MUL, a)
                b.done(z)
                fin.append(z)

        N = len(items)
        for t in range(N + 3):
            if t < N:
                score(t)
            if 1 <= t <= N:
                soft(t - 1)
            if 2 <= t <= N + 1:
                turn(t - 2)
            if t >= 3:
                pv(t - 3)
        return sc, fin

    def sigmoid_den(o, i, *deps):
        a = act(o, i, ACT.Exp, *deps, scale=-1.0)
        return ts(o, o, 1.0, None, ADD, None, a)

    def log_sigmoid(o, i, rows, n, *deps):
        t, free = tmp.take()
        tt_ = t.t[0:rows, 0:n]
        a = act(tt_, i, ACT.Abs, *deps, free)
        a = act(tt_, tt_, ACT.Exp, a, scale=-1.0)
        a = act(tt_, tt_, ACT.Ln, a, bias=1.0)
        z = stt(o, i, 0.0, tt_, MIN, SUB, a)
        t.done(z)
        return z

    s1 = ExitStack()
    aqT = sbuf("aqT", [P, 3, T], scope=s1)
    akT = sbuf("akT", [P, 3, T], scope=s1)
    av = sbuf("av", [P, 4, 384], scope=s1)
    ag = sbuf("ag", [P, 4, 384], scope=s1)
    ge = sbuf("ge", [P, 4, 384], scope=s1)
    U = sbuf("U", [P, 6, 512], scope=s1)
    bar = q.last()
    for hh in range(6):
        src = d["rel_ext"][hh:hh + 1, 1:513]
        skew = bass.AP(tensor=src.tensor, offset=src.offset, ap=[[1, P], [1, 512]])
        l_u = dma(U[:, hh, :], skew, s_u, bar)
    u_ok = mset(U[0:64, :, 0:64], NEG, l_u)
    q_, k_ = [], []
    for m in range(3):
        b, h = fm_tile("aq", hhi, hlo, 8, T, hr)
        z = act(aqT[:, m, :], b.t[:], ACT.Identity, h, scale=0.125)
        b.done(z)
        q_.append(z)
    for m in range(3):
        b, h = fm_tile("ak", hhi, hlo, 8, T)
        z = cp(akT[:, m, :], b.t[:], h)
        b.done(z)
        k_.append(z)
    v_ = []
    for c, (b, h) in enumerate(tm_group("av", hhi, hlo, 4, 384)):
        z = evac(av[:, c, :], b.t[:, 0:384], h)
        b.done(z)
        v_.append(z)
    for c, (b, h) in enumerate(tm_group("ag", hhi, hlo, 4, 384)):
        a = act(ge[:, c, :], b.t[:, 0:384], ACT.Exp, h, scale=-1.0)
        z = cp(ag[:, c, :], b.t[:, 0:384], a)
        b.done(z)
    z = ts(ge[:], ge[:], 1.0, None, ADD, None, a)
    z = recip(ge[:], ge[:], z)
    g_ok = tt(ag[:], ag[:], ge[:], MUL, z)

    def half(h):
        return slice(64 * (h % 2), 64 * (h % 2) + 64)

    def u_bias(h, i, n):
        base = U[:, h, n - 1:n]
        return bass.AP(tensor=base.tensor, offset=base.offset, ap=[base.ap[0], [-1, n]]), u_ok

    sc, fin = attention(
        "att", 6,
        lambda h, i: (aqT[half(h), h // 2, i * P:(i + 1) * P], q_[h // 2]),
        lambda h, n: (akT[half(h), h // 2, 0:n], k_[h // 2]),
        lambda h, j: (av[:, j, h * 64:(h + 1) * 64], v_[j]),
        lambda i: P * (i + 1), False,
        lambda h0, i: yt[:, i, h0 * 64:h0 * 64 + 128].rearrange("p (h n) -> p h n", h=2), bias=u_bias)
    tt(yt[:, :, 0:384], yt[:, :, 0:384], ag[:], MUL, fin, g_ok)
    q.barrier()
    sc.close()
    s1.close()

    s2 = ExitStack()
    cqk = sbuf("cqk", [P, 6, T], scope=s2)
    mva = sbuf("mva", [P, 4, 6, 65], scope=s2)
    mo = sbuf("mo", [P, 4, 384], scope=s2)
    mg = sbuf("mg", [P, 4, 384], scope=s2)
    hm = sbuf("hm", [P, 4, 6, 64], scope=s2)
    gts = sbuf("gts", [12, T], scope=s2)
    fr = sbuf("fr", [6, T], scope=s2)
    lf = fr
    FF_ = sbuf("Fsum", [6, T], scope=s2)
    aj = sbuf("aj", [6, T], scope=s2)
    Am = sbuf("Am", [6, T], scope=s2)
    em = sbuf("em", [6, T], scope=s2)
    bg = sbuf("bg", [12, 1], scope=s2)
    acol = sbuf("acol", [P, 4, 6], scope=s2)
    ecol = sbuf("ecol", [P, 4, 6], scope=s2)
    gml = sbuf("gml", [P, 384], scope=s2)
    bar = q.last()
    l_g = dma(bg[:], d["b_gates"].rearrange("a n -> n a"), s_u, bar)
    l_g = dma(gml[:], d["ml_norm_g"][0:1, :].to_broadcast([P, 384]), s_u, bar)
    o6 = c_1
    onesv = mset(mva[:, :, :, 64:65], 1.0)
    cq_ = []
    for m in range(6):
        b, h = fm_tile("mqk", hhi, hlo, 8, T)
        t, free = tmp.take()
        x_ = t.t
        a = act(x_[:], b.t[:], ACT.Identity, h, free, l_c, scale=col("conv_w", 4 * m + 3))
        z = a
        for s in range(1, 4):
            z = stt(x_[:, s:T], b.t[:, 0:T - s], col("conv_w", 4 * m + 3 - s), x_[:, s:T], MUL, ADD, z)
        b.done(z)
        t2, free = tmp.take()
        z = sigmoid_den(t2.t[:], x_[:], z, free)
        z = recip(t2.t[:], t2.t[:], z)
        if m < 3:
            z = tt(cqk[:, m, :], x_[:], t2.t[:], MUL, z)
        else:
            z = stt(cqk[:, m, :], x_[:], 0.125, t2.t[:], MUL, MUL, z)
        t.done(z)
        t2.done(z)
        cq_.append(z)
    mv_ = []
    for c, (b, h) in enumerate(tm_group("mv", hhi, hlo, 4, 384)):
        z = evac(mva[:, c, :, 0:64], b.t[:, 0:384].rearrange("p (h n) -> p h n", h=6), h, onesv)
        b.done(z)
        mv_.append(z)
    mo_ = []
    for c, (b, h) in enumerate(tm_group("mo", hhi, hlo, 4, 384)):
        z = sigmoid_den(mo[:, c, :], b.t[:, 0:384], h)
        b.done(z)
        mo_.append(z)
    b, h = fm_tile("gate", hhi, hlo, 8, T)
    a = act(gts[:], b.t[0:12, :], ACT.Identity, h, l_g, bias=bg[:, 0:1])
    b.done(a)
    b, free = RA.take()
    g = mm(b.t[0:6, :], ident[0:12, 6:12], gts[:], True, True, a, free, C)
    a = acopy(fr[:], b.t[0:6, :], g)
    b.done(a)
    z = log_sigmoid(lf[:], fr[:], 6, T, a)
    z = q.op("dve", lambda e: e.tensor_tensor_scan(FF_[:], ones[0:6, 0:1].to_broadcast([6, T]), lf[:], 0.0, MUL, ADD), (z, o6))
    z = tt(aj[:], gts[0:6, :], FF_[:], SUB, z)
    z_a = z
    z = q.op("dve", lambda e: e.tensor_tensor_scan(Am[:], ones[0:6, 0:1].to_broadcast([6, T]), aj[:], 0.0, MUL, MAX), (z,))
    z_A = z
    z = tt(em[:], FF_[:], Am[:], ADD, z)
    z_e = act(em[:], em[:], ACT.Exp, z, scale=-1.0)
    b, free = RA.take()
    for c in range(4):
        tr(b.t[:, c * 6:c * 6 + 6], aj[:, c * P:(c + 1) * P], ident[0:6, 0:6], z_a, free)
    for c in range(4):
        g = tr(b.t[:, 24 + c * 6:24 + c * 6 + 6], em[:, c * P:(c + 1) * P], ident[0:6, 0:6], z_e)
    z = cp(acol[:].rearrange("p a b -> p (a b)"), b.t[:, 0:24], g)
    c_ok = cp(ecol[:].rearrange("p a b -> p (a b)"), b.t[:, 24:48], g)
    b.done(c_ok)
    mg_ = []
    for c, (b, h) in enumerate(tm_group("mg", hhi, hlo, 4, 384)):
        t, free = tmp.take()
        z = sigmoid_den(t.t[:, 0:384], b.t[:, 0:384], h, free)
        z = tt(mo[:, c, :], mo[:, c, :], t.t[:, 0:384], MUL, z, mo_[c])
        t.done(z)
        z = recip(mo[:, c, :], mo[:, c, :], z)
        z = tt(mg[:, c, :], b.t[:, 0:384], mo[:, c, :], MUL, z)
        b.done(z)
        mg_.append(z)

    dts = Ring([Slot(sbuf(f"dt{i}", [P, T], scope=s2)) for i in range(3)])
    scs = Ring([Slot(sbuf(f"scm{i}", [P, 1280], scope=s2)) for i in range(2)])
    mden = sbuf("mden", [P, 6, 4], scope=s2)
    OFF = [0, 512, 896, 1152]
    HS = {}

    def ml_decay(h):
        ab, free = RT.take()
        ga_ = mm(ab.t[:], ident[0:6, h:h + 1].to_broadcast([6, P]), Am[:], True, True, z_A, free, C)
        s_, f2 = scs.take()
        lasts = []
        for J in range(4):
            n = T - J * P
            dt_, free = dts.take()
            a = act(dt_.t[:, 0:n], ab.t[:, J * P:T], ACT.Exp, ga_, c_ok, free, scale=-1.0, bias=acol[:, J, h:h + 1])
            pz = sel(dt_.t[:, 0:P], [[1, P]], ALU.is_ge, 0.0, 0, -1, a)
            b, free = RS.take()
            g = mm(b.t[:, 0:n], cqk[half(h), 3 + h // 2, J * P:(J + 1) * P], cqk[half(h), h // 2, J * P:T],
                   True, True, cq_[h // 2], cq_[3 + h // 2], free)
            z = tt(s_.t[:, OFF[J]:OFF[J] + n], b.t[:, 0:n], dt_.t[:, 0:n], MUL, g, pz, a, f2)
            b.done(z)
            dt_.done(z)
            lasts.append(z)
        ab.done(a)
        HS[h] = (s_, lasts)

    def ml_out(h):
        s_, lasts = HS.pop(h)
        b, free = RO.take()
        for i in range(4):
            for J in range(i + 1):
                o = OFF[J] + (i - J) * P
                g = mm(b.t[:, i * 65:(i + 1) * 65], s_.t[:, o:o + P], mva[:, J, h, :], J == 0, J == i,
                       lasts[J], mv_[J], free)
        s_.done(g)
        ov = b.t[:, 0:260].rearrange("p (i n) -> p i n", i=4)
        a = act(mden[:, h, :].unsqueeze(2), ov[:, :, 64:65], ACT.Abs, g)
        z = tt(mden[:, h, :].unsqueeze(2), mden[:, h, :].unsqueeze(2), ecol[:, :, h:h + 1], MAX, a, c_ok)
        z = recip(mden[:, h, :], mden[:, h, :], z)
        z = tt(hm[:, :, h, :], ov[:, :, 0:64], mden[:, h, :].unsqueeze(2).to_broadcast([P, 4, 64]), MUL, z)
        b.done(z)
        return z

    ml_ok = []
    for h in range(7):
        if h < 6:
            ml_decay(h)
        if h > 0:
            ml_ok.append(ml_out(h - 1))

    def head_norm(hv, sq, rows, groups, n, *deps):
        a = act(sq, hv, ACT.Square, *deps)
        z = red(rows, sq, ADD, a)
        return rstd_of(rows, rows, n, z)

    hv = hm[:].rearrange("p i h n -> p (i h) n")
    sq = mo[:].rearrange("p i (h n) -> p (i h) n", h=6)
    a = head_norm(hv, sq, small[:, 32:56], 24, 64, ml_ok, mg_)
    z = tt(hv, hv, small[:, 32:56].unsqueeze(2).to_broadcast([P, 24, 64]), MUL, a)
    gb = gml[:].unsqueeze(1).to_broadcast([P, 4, 384])
    hf_ = hm[:].rearrange("p i h n -> p i (h n)")
    z2 = tt(mg[:], mg[:], gb, MUL, mg_, l_g)
    tt(yt[:, :, 384:768], hf_, mg[:], MUL, z, z2)
    q.barrier()
    s2.close()

    s3 = ExitStack()
    gq = sbuf("gq", [P, T], scope=s3)
    gk = sbuf("gk", [P, T], scope=s3)
    gv = sbuf("gv", [P, 4, 256], scope=s3)
    gg = sbuf("gg", [P, 4, 256], scope=s3)
    ge2 = sbuf("ge2", [P, 4, 256], scope=s3)
    gaT = sbuf("gaT", [16, T], scope=s3)
    wal = sbuf("wal", [16, P], scope=s3)
    pre = sbuf("pre", [P, T], scope=s3)
    bT = sbuf("bT", [P, T], scope=s3)
    ATT = sbuf("ATT", [P, 4, 4, P], scope=s3)
    AX_ = [sbuf(f"AX{J}", [P, 4, (3 - J) * P], scope=s3) for J in range(3)]
    msk = sbuf("msk", [P, 7, P], scope=s3)
    ggn = sbuf("ggn", [P, 256], scope=s3)
    hg = sbuf("hg", [P, 4, 4, 64], scope=s3)
    nref = sbuf("nref", [P, 3], scope=s3)
    kl = Ring([Slot(sbuf(f"kl{i}", [P, T], scope=s3)) for i in range(2)])
    ql = Ring([Slot(sbuf(f"ql{i}", [P, T], scope=s3)) for i in range(2)])
    bar = q.last()
    l_a = dma(wal[:], d["w_alpha"].rearrange("a r n -> (a r) n"), s_u, bar)
    l_a = dma(ggn[:], d["gla_norm_g"][0:1, :].to_broadcast([P, 256]), s_u, bar)
    z0 = mset(msk[:], 0.0)
    z1 = mset(ATT[:], 0.0)
    mk_ = []
    for li in range(7):
        s = 64 >> li
        nb = P // (2 * s)
        v4 = msk[:, li, :].rearrange("p (a b s) -> p a b s", a=nb, b=2)[:, :, 1, :]
        z = mset(v4, 1.0, z0)
        z = sel(v4, [[-2 * s, nb], [0, s]], ALU.is_ge, 0.0, 0, 1, z)
        z = sel(v4, [[2 * s, nb], [0, s]], ALU.is_ge, 0.0, s - 1, -1, z)
        mk_.append(z)
    b, h = fm_tile("gqk", hhi, hlo, 8, T)
    zq = act(gq[:], b.t[:], ACT.Identity, h, scale=32 ** -0.5)
    b.done(zq)
    b, h = fm_tile("gqk", hhi, hlo, 8, T)
    zk = cp(gk[:], b.t[:], h)
    b.done(zk)
    gv_ = []
    for c, (b, h) in enumerate(tm_group("gv", hhi, hlo, 4, 256)):
        z = evac(gv[:, c, :], b.t[:, 0:256], h)
        b.done(z)
        gv_.append(z)
    b, h = fm_tile("ga", hhi, hlo, 8, T)
    a = acopy(gaT[:], b.t[0:16, :], h)
    b.done(a)
    b, free = RA.take()
    g = mm(b.t[:], wal[:], gaT[:], True, True, a, free, l_a)
    a = act(pre[:], b.t[:], ACT.Identity, g, l_c, bias=col("b_alpha"))
    b.done(a)
    z = log_sigmoid(pre[:], pre[:], P, T, a)
    z = ts(pre[:], pre[:], 1.0 / 16.0, None, MUL, None, z)
    t, free = tmp.take()
    o_ = mset(t.t[:], 1.0, free)
    zb = q.op("dve", lambda e: e.tensor_tensor_scan(bT[:], t.t[:], pre[:], 0.0, MUL, ADD), (z, o_))
    t.done(zb)
    for c, (b, h) in enumerate(tm_group("gg", hhi, hlo, 4, 256)):
        a = act(ge2[:, c, :], b.t[:, 0:256], ACT.Exp, h, scale=-1.0)
        z = cp(gg[:, c, :], b.t[:, 0:256], a)
        b.done(z)
    z = ts(ge2[:], ge2[:], 1.0, None, ADD, None, a)
    z = recip(ge2[:], ge2[:], z)
    z = tt(gg[:], gg[:], ge2[:], MUL, z)
    gg_ok = tt(gg[:], gg[:], ggn[:].unsqueeze(1).to_broadcast([P, 4, 256]), MUL, z, l_a)

    at_ok = {}
    prev = {c: z1 for c in range(4)}
    for li in range(8):
        if li < 7:
            s = 64 >> li
            nb = T // (2 * s)
            t, free = tmp.take()
            bv = bT[:].rearrange("p (a s) -> p a s", s=2 * s)
            tv = t.t[:].rearrange("p (a s) -> p a s", s=2 * s)
            z = tt(tv, bv, bv[:, :, s - 1:s].to_broadcast([P, nb, 2 * s]), SUB, zb, free)
            a = act(t.t[:], t.t[:], ACT.Abs, z)
            a = act(t.t[:], t.t[:], ACT.Exp, a, scale=-1.0)
            (k2, f1), (q2, f2) = kl.take(), ql.take()
            zk2 = tt(k2.t[:], gk[:], t.t[:], MUL, a, zk, f1)
            zq2 = tt(q2.t[:], gq[:], t.t[:], MUL, a, zq, f2, eng="pool")
            t.done(zk2, zq2)
            K_, Q_, M_, mh_ = k2.t, q2.t, msk[:, li, :], mk_[li]
        else:
            K_, Q_, zk2, zq2, M_, mh_ = gk, gq, zk, zq, ident[:], None
        for h in range(4):
            b, free = RA.take()
            hp = slice(32 * h, 32 * h + 32)
            for c in range(4):
                g = mm(b.t[:, c * P:(c + 1) * P], K_[hp, c * P:(c + 1) * P], Q_[hp, c * P:(c + 1) * P], True, True,
                       zk2, zq2, free)
            mb = M_.bitcast(I32).unsqueeze(1).to_broadcast([P, 4, P])
            bv4 = b.t[:].rearrange("p (c n) -> p c n", c=4)
            z = q.op("dve", lambda e, h=h, mb=mb, bv4=bv4: e.copy_predicated(ATT[:, :, h, :], mb, bv4),
                     (g, mh_, prev[h]))
            b.done(z)
            prev[h] = z
        if li < 7:
            k2.done(g)
            q2.done(g)
    ax_ = {}
    for J in range(3):
        n = (3 - J) * P
        e_ = bT[:, J * P + 127:J * P + 128]
        zr = ts(nref[:, J:J + 1], e_, -1.0, None, MUL, None, zb)
        t, free = tmp.take()
        a1 = act(t.t[:, 0:P], bT[:, J * P:(J + 1) * P], ACT.Exp, zb, free, scale=-1.0, bias=e_)
        a2 = act(t.t[:, P:T - J * P], bT[:, (J + 1) * P:T], ACT.Exp, zr, bias=nref[:, J:J + 1])
        (k2, f1), (q2, f2) = kl.take(), ql.take()
        zk2 = tt(k2.t[:, 0:P], gk[:, J * P:(J + 1) * P], t.t[:, 0:P], MUL, a1, f1)
        zq2 = tt(q2.t[:, 0:n], gq[:, (J + 1) * P:T], t.t[:, P:T - J * P], MUL, a2, f2)
        t.done(zk2, zq2)
        for h in range(4):
            hp = slice(32 * h, 32 * h + 32)
            b, free = RA.take()
            g = mm(b.t[:, 0:n], k2.t[hp, 0:P], q2.t[hp, 0:n], True, True, zk2, zq2, free)
            z = evac(AX_[J][:, h, :], b.t[:, 0:n], g)
            b.done(z)
            ax_[J, h] = z
        k2.done(g)
        q2.done(g)
    gz = []
    for i in range(4):
        b, free = RA.take()
        for h in range(4):
            o = b.t[:, h * 64:(h + 1) * 64]
            for J in range(i):
                mm(o, AX_[J][:, h, (i - J - 1) * P:(i - J) * P], gv[:, J, h * 64:(h + 1) * 64], J == 0, False,
                   ax_[J, h], gv_[J], free)
            g = mm(o, ATT[:, i, h, :], gv[:, i, h * 64:(h + 1) * 64], i == 0, True, prev[h], gv_[i], free)
        z = evac(hg[:, i, :, :], b.t[:, 0:256].rearrange("p (h n) -> p h n", h=4), g)
        b.done(z)
        gz.append(z)
    hv = hg[:].rearrange("p i h n -> p (i h) n")
    sq = ge2[:].rearrange("p i (h n) -> p (i h) n", h=4)
    a = head_norm(hv, sq, small[:, 64:80], 16, 64, gz, gg_ok)
    z = tt(hv, hv, small[:, 64:80].unsqueeze(2).to_broadcast([P, 16, 64]), MUL, a)
    yz = tt(yt[:, :, 768:1024], hg[:].rearrange("p i h n -> p i (h n)"), gg[:], MUL, z)
    q.barrier()
    s3.close()

    def turn_y(y, *deps):
        return transpose_tokens(y, 4, deps, lambda kt, b, h: split_bank(b, h, hhi[:, kt, :], hlo[:, kt, :]))

    s4 = ExitStack()
    fgr = sbuf("fgr", [P, D], scope=s4)
    l_f = dma(fgr[:], d["final_g"].rearrange("(a n) -> a n", a=1).to_broadcast([P, D]), s_u, q.last())
    yr = turn_y(yt, yz)
    rs_ = []
    for g0 in (0, 384, 768):
        n = min(384, D - g0)
        for c, (b, h) in enumerate(tm_group("wo1", hhi, hlo, 4, n, yr)):
            z = tt(xt[:, c, g0:g0 + n], b.t[:, 0:n], xt[:, c, g0:g0 + n], ADD, h)
            b.done(z)
            rs_.append(z)
    r, at_ = token_rms(xt, 4, 96, rs_)
    for c in range(4):
        r2 = stt(xt[:, c, :], xt[:, c, :], small[:, at_ + c:at_ + c + 1], fgr[:], MUL, MUL, r, l_f)

    xz = []

    def to_x(kt, b, h):
        z = evac(xT[:, kt, :], b.t[:], h)
        b.done(z)
        xz.append(z)
        return z

    transpose_tokens(xt, 4, r2, to_x)
    q.barrier()
    s4.close()
    mscope.close()

    xlast = {"h": list(xz)}

    def fm_norm(gname, g0):
        b, free = RA.take()
        for k in range(8):
            t, f2 = tmp.take()
            a = act(t.t[:], xT[:, k, :], ACT.Square, xlast["h"], f2)
            g = mm(b.t[:], ones[:], t.t[:], k == 0, k == 7, a, free)
            t.done(g)
        rb, f2 = hold.take()
        a = rstd_of(rb.t[:], b.t[:], D, g, f2)
        b.done(a)
        for k in range(8):
            t, f2 = tmp.take()
            z = stt(t.t[:], xT[:, k, :], col(gname, g0 + k), rb.t[:], MUL, MUL, a, f2)
            a2 = acopy(hhi[:, k, :], t.t[:], z)
            z = tt(hlo[:, k, :], t.t[:], hhi[:, k, :].bitcast(F32), SUB, a2, eng="pool" if k % 2 else "dve")
            t.done(z)
            if k % 2 == 0:
                ze = z
        rb.done(ze, z)
        return [ze, z]

    def head_normed(key, dst, gcol, *deps):
        b, h = fm_tile(key, hhi, hlo, 8, T, *deps)
        t, free = tmp.take()
        a = act(t.t[:], b.t[:], ACT.Square, h, free)
        b2, free = RA.take()
        g = mm(b2.t[:], blk[:], t.t[:], True, True, a, free)
        t.done(g)
        t2, free = tmp.take()
        a = rstd_of(t2.t[:], b2.t[:], 64, g, free)
        b2.done(a)
        z = stt(dst, b.t[:], gcol, t2.t[:], MUL, MUL, a)
        b.done(z)
        t2.done(z)
        return z

    def out_and_ffn(l, y, yz, final):
        yr = turn_y(y, yz)
        hs = []
        for m in range(8):
            b, h = fm_tile("wo", hhi, hlo, 8, T, yr)
            z = tt(xT[:, m, :], b.t[:], xT[:, m, :], ADD, h)
            b.done(z)
            hs.append(z)
        xlast["h"] = hs
        q.barrier()

    def ffn(l, final, extra=None):
        hr = fm_norm("norm_ffn", 8 * l)
        table("silu_and_others")
        fs = ExitStack()
        ahi = sbuf(f"ahi{l}", [P, 11, T], F32R, scope=fs)
        alo = sbuf(f"alo{l}", [P, 11, T], F32R, scope=fs)
        cr = Ring([Slot(sbuf(f"cr{l}_{i}", [P, T], scope=fs)) for i in range(4)])
        ob = Ring([Slot(sbuf(f"ob{l}_{i}", [P, 4, P], scope=fs)) for i in range(2)]) if final else None
        if extra:
            extra(fs)
        dlast = None
        hs = [None] * 8

        def conv(b, h, ch):
            t, free = cr.take()
            cw = lambda j: col(f"cw{l}", 3 * ch + j)
            a = act(t.t[:], b.t[:], ACT.Identity, h, free, scale=cw(2), bias=col(f"cb{l}", ch))
            z = stt(t.t[:, 1:T], b.t[:, 0:T - 1], cw(1), t.t[:, 1:T], MUL, ADD, a)
            z = stt(t.t[:, 2:T], b.t[:, 0:T - 2], cw(0), t.t[:, 2:T], MUL, ADD, z)
            b.done(z)
            return t, z

        for half_ in range(2):
            fin = []
            for ct in range(11):
                ch = 11 * half_ + ct
                b, h = fm_tile("up", hhi, hlo, 8, T, hr)
                tg, zg = conv(b, h, ch)
                a = act(tg.t[:], tg.t[:], ACT.Silu, zg)
                b, h = fm_tile("up", hhi, hlo, 8, T, hr)
                tv, zv = conv(b, h, 22 + ch)
                z = tt(tg.t[:], tg.t[:], tv.t[:], MUL, a, zv, eng="pool")
                tv.done(z)
                a2 = acopy(ahi[:, ct, :], tg.t[:], z, dlast)
                z = tt(alo[:, ct, :], tg.t[:], ahi[:, ct, :].bitcast(F32), SUB, a2, eng="pool")
                tg.done(z)
                fin.append(z)
            for m in range(8):
                w = weights("down")
                b, free = RA.take()
                for k in range(11):
                    g = mm3(b.t[:], w.hi[:, k, :], w.lo[:, k, :], ahi[:, k, :], alo[:, k, :], k == 0, k == 10,
                            w.rdy, free, fin[k])
                w.done(g)
                z = tt(xT[:, m, :], b.t[:], xT[:, m, :], ADD, g, hs[m])
                b.done(z)
                hs[m] = z
                if final and half_ == 1:
                    b, free = RA.take()
                    for c in range(4):
                        g2 = tr(b.t[:, c * P:(c + 1) * P], xT[:, m, c * P:(c + 1) * P], ident[:], z, free)
                    o, free = ob.take()
                    z = evac(o.t[:], b.t[:].rearrange("p (c n) -> p c n", c=4), g2, free)
                    b.done(z)
                    dd = dma(out.rearrange("a (c p) n -> p (a c) n", p=P)[:, :, m * P:(m + 1) * P], o.t[:],
                             s_out[m % 2], z)
                    o.done(dd)
                    last_out[m % 2] = dd
            dlast = g
        xlast["h"] = hs
        q.barrier()
        fs.close()
        if not final:
            table("natural_log_exp_and_others")

    last_out = [None, None]

    L0 = ExitStack()
    hr = fm_norm("norm_mix", 0)
    y0 = sbuf("y0", [P, 4, D], scope=L0)
    fqT = sbuf("fqT", [P, 6, T], scope=L0)
    fkT = sbuf("fkT", [P, 6, T], scope=L0)
    fv = sbuf("fv", [P, 4, 768], scope=L0)
    mqT = sbuf("mqT", [P, 2, T], scope=L0)
    cum = sbuf("cum", [12, T], scope=L0)
    fpre = sbuf("fpre", [12, T], scope=L0)
    gs = sbuf("gs", [P, 4], scope=L0)
    zs = ts(gs[:, 0:1], col("fq"), 0.125, None, MUL, None, l_c)
    zs = ts(gs[:, 1:2], col("mq", 0), 0.125, None, MUL, None, l_c)
    fq_ = [head_normed("fqk", fqT[:, m, :], gs[:, 0:1], hr, zs) for m in range(6)]
    fk_ = [head_normed("fqk", fkT[:, m, :], col("fk")) for m in range(6)]
    fv_ = {}
    for g0 in (0, 384):
        for c, (b, h) in enumerate(tm_group("fv", hhi, hlo, 4, 384)):
            z = evac(fv[:, c, g0:g0 + 384], b.t[:, 0:384], h)
            b.done(z)
            fv_[c, g0 // 384] = z
    b, h = fm_tile("ff", hhi, hlo, 8, T)
    a = act(fpre[:], b.t[0:12, :], ACT.Identity, h, l_c, bias=fb[:, 0:1])
    b.done(a)
    z = log_sigmoid(fpre[:], fpre[:], 12, T, a)
    zc = q.op("dve", lambda e: e.tensor_tensor_scan(cum[:], ones[0:12, 0:1].to_broadcast([12, T]), fpre[:], 0.0, MUL, ADD), (z,))
    mq_ = [head_normed("fm", mqT[:, m, :], gs[:, 1:2]) for m in range(2)]

    ncr = Ring([Slot(sbuf(f"nc{i}", [P, T], scope=L0)) for i in range(2)])
    NC = {}

    def fox_head(h):
        if h >= 1 and h - 1 in NC:
            pass
        b, free = RT.take()
        g = mm(b.t[:], ident[0:12, h:h + 1].to_broadcast([12, P]), cum[:], True, True, zc, free)
        s_, f2 = ncr.take()
        a = act(s_.t[:], b.t[:], ACT.Identity, g, f2, scale=-1.0)
        b.done(a)
        NC[h] = (s_, a)

    def fox_bias(h, i, n):
        return NC[h][0].t[:, 0:n], NC[h][1]

    def fox_start(h):
        if h >= 2:
            NC[h - 2][0].done(q.end["dve"])
        fox_head(h)

    dst = lambda y, off: (lambda h0, i: y[:, i, off + h0 * 64:off + h0 * 64 + 128].rearrange("p (h n) -> p h n", h=2))
    sc, fin0 = attention(
        "fox", 12,
        lambda h, i: (fqT[half(h), h // 2, i * P:(i + 1) * P], fq_[h // 2]),
        lambda h, n: (fkT[half(h), h // 2, 0:n], fk_[h // 2]),
        lambda h, j: (fv[:, j, h * 64:(h + 1) * 64], fv_[j, h // 6]),
        lambda i: P * (i + 1), True, dst(y0, 0), bias=fox_bias, head_start=fox_start)
    q.barrier()
    sc.close()

    def mem_attention(l, y, mqT, mq_):
        kg = ts(kmg[:], kmn[:], col("mk", l), None, MUL, None, l_c)
        return attention(
            f"mem{l}", 4,
            lambda h, i: (mqT[half(h), h // 2, i * P:(i + 1) * P], mq_[h // 2]),
            lambda h, n: (kmg[half(h), h // 2, :], kg),
            lambda h, j: (vmem[:, j, h * 64:(h + 1) * 64], None),
            lambda i: 256, False, dst(y, 768))

    sc, fin1 = mem_attention(0, y0, mqT, mq_)
    out_and_ffn(0, y0, fin0 + fin1, False)
    sc.close()
    L0.close()

    def rope_tables(fs):
        pi_ = sbuf("posi", [P, 4], I32, scope=fs)
        pf = sbuf("posf", [P, 4], scope=fs)
        iv = sbuf("ivf", [P, 16], scope=fs)
        an = sbuf("ang", [P, 4, 16], scope=fs)
        kk = sbuf("kk", [P, 4, 16], scope=fs)
        r_ = sbuf("rr", [P, 2, 4, 16], scope=fs)
        l_p = dma(pi_[:], d["pos"], s_u, q.last())
        inv = np.float32(10000.0) ** (-np.arange(0, 32, 2, dtype=np.float32) / np.float32(32))
        for j in range(16):
            m = mset(iv[:, j:j + 1], float(np.float32(inv[j])))
        z = cp(pf[:], pi_[:], l_p)
        z = tt(an[:], pf[:].unsqueeze(2).to_broadcast([P, 4, 16]), iv[:].unsqueeze(1).to_broadcast([P, 4, 16]),
               MUL, z, m)
        magic = 12582912.0
        c1 = 6.28125
        c2 = float(np.float32(2 * np.pi - 6.28125) // np.float32(2 ** -20) * 2 ** -20)
        c3 = float(2 * np.pi - 6.28125 - c2)
        lim = 3.1415925
        zz = z
        for w, (quarter, shift, dst_) in enumerate(((0.0, 0.0, sinT), (0.25, float(np.pi / 2), cosT))):
            z = ts(kk[:], an[:], float(1 / (2 * np.pi)), quarter, MUL, ADD, zz)
            z = ts(kk[:], kk[:], magic, None, ADD, None, z)
            z = ts(kk[:], kk[:], -magic, None, ADD, None, z)
            z = stt(r_[:, w], kk[:], -c1, an[:], MUL, ADD, z)
            z = stt(r_[:, w], kk[:], -c2, r_[:, w], MUL, ADD, z)
            z = stt(r_[:, w], kk[:], -c3, r_[:, w], MUL, ADD, z)
            z = ts(r_[:, w], r_[:, w], shift, lim, ADD, MIN, z)
            z = ts(r_[:, w], r_[:, w], -lim, None, MAX, None, z)
            a = act(dst_[:], r_[:, w], ACT.Sin, z)
            zz = [zz, z]
        rope_ok.append(a)

    rope_ok = []
    ffn(0, False, rope_tables)

    L1 = ExitStack()
    hr = fm_norm("norm_mix", 8)
    y1 = sbuf("y1", [P, 4, D], scope=L1)
    qt = sbuf("qt", [P, 4, 12, 96], scope=L1)
    kt_ = sbuf("ktm", [P, 4, 12, 96], scope=L1)
    vt = sbuf("vt", [P, 4, 12, 64], scope=L1)
    mqT1 = sbuf("mqT1", [P, 2, T], scope=L1)
    gs1 = sbuf("gs1", [P, 1], scope=L1)
    gq96 = sbuf("gq96", [96, 2], scope=L1)
    l_q = dma(gq96[:, 0:1], d["mla_q_gain_2"].rearrange("a n -> n a"), s_u, q.last())
    l_q = dma(gq96[:, 1:2], d["mla_k_gain_2"].rearrange("a n -> n a"), s_u)
    Lt = ExitStack()
    lhi = sbuf("lhi", [P, 3, T], F32R, scope=Lt)
    llo = sbuf("llo", [P, 3, T], F32R, scope=Lt)
    krr = sbuf("krr", [P, 4, 32], scope=Lt)
    krt = sbuf("krt", [P, 4, 4, 16], scope=Lt)
    zs = ts(gs1[:], col("mq", 1), 0.125, None, MUL, None, l_c)
    zg = ts(gq96[:, 0:1], gq96[:, 0:1], 96 ** -0.5, None, MUL, None, l_q)

    def latent(tiles, key, n, gname, base, *deps):
        bs = []
        b2, f2 = RO.take()
        for m in range(tiles):
            b, h = fm_tile_s(key, *deps)
            t, free = tmp.take()
            a = act(t.t[:], b.t[:], ACT.Square, h, free)
            g = mm(b2.t[:], ones[:], t.t[:], m == 0, m == tiles - 1, a, f2)
            t.done(g)
            bs.append(b)
        rb, free = hold.take()
        a = rstd_of(rb.t[:], b2.t[:], n, g, free)
        b2.done(a)
        zl = []
        for m in range(tiles):
            t, free = tmp.take()
            z = stt(t.t[:], bs[m].t[:], col(gname, m), rb.t[:], MUL, MUL, a, free)
            bs[m].done(z)
            a2 = acopy(lhi[:, base + m, :], t.t[:], z)
            z = tt(llo[:, base + m, :], t.t[:], lhi[:, base + m, :].bitcast(F32), SUB, a2)
            t.done(z)
            zl.append(z)
        rb.done(zl[-1])
        return zl

    def fm_tile_s(key, *deps):
        w = weights(key)
        b, free = RS.take()
        for k in range(8):
            h = mm3(b.t[:], w.hi[:, k, :], w.lo[:, k, :], hhi[:, k, :], hlo[:, k, :], k == 0, k == 7, w.rdy, free, deps)
        w.done(h)
        return b, h

    ql_ = latent(2, "ql", 256, "qa", 0, hr)
    kvl_ = latent(1, "kvl", 128, "kva", 2)
    w = weights("kr")
    b, free = RA.take()
    for c in range(4):
        for k in range(8):
            g = mm3(b.t[:, c * 32:(c + 1) * 32], hhi[:, k, c * P:(c + 1) * P], hlo[:, k, c * P:(c + 1) * P],
                    w.hi[:, k, :], w.lo[:, k, :], k == 0, k == 7, w.rdy, free)
    w.done(g)
    z_kr = cp(krr[:].rearrange("p c n -> p (c n)"), b.t[:, 0:P], g)
    b.done(z_kr)
    mq_ = [head_normed("mm", mqT1[:, m, :], gs1[:, 0:1], zs) for m in range(2)]

    def rope(x1, x2, cc, ss, t4, *deps, eng="dve"):
        z1_ = tt(t4[0], x1, cc, MUL, *deps, eng=eng)
        z2_ = tt(t4[1], x2, ss, MUL, eng=eng)
        z3_ = tt(t4[2], x1, ss, MUL, eng=eng)
        z4_ = tt(t4[3], x2, cc, MUL, eng=eng)
        z5_ = tt(x1, t4[0], t4[1], SUB, z1_, z2_, z3_, eng=eng)
        return tt(x2, t4[2], t4[3], ADD, z3_, z4_, z5_, eng=eng)

    zk_ = rope(krr[:, :, 0:16], krr[:, :, 16:32], cosT[:], sinT[:], [krt[:, i] for i in range(4)], z_kr, rope_ok)
    zkr = []
    for c in range(4):
        zkr.append(cp(kt_[:, c, :, 64:96], krr[:, c, :].unsqueeze(1).to_broadcast([P, 12, 32]), zk_, eng="pool"))
    qz = []
    for j in range(3):
        w = weights("qup")
        for c in range(4):
            b, free = RA.take()
            for k in range(2):
                g = mm3(b.t[:, 0:384], lhi[:, k, c * P:(c + 1) * P], llo[:, k, c * P:(c + 1) * P],
                        w.hi[:, k, :], w.lo[:, k, :], k == 0, k == 1, w.rdy, free, ql_)
            z = evac(qt[:, c, 4 * j:4 * j + 4, :], b.t[:, 0:384].rearrange("p (h n) -> p h n", h=4), g)
            b.done(z)
            qz.append(z)
        w.done(g)
    kz = []
    for j in range(3):
        w = weights("kvup")
        for c in range(4):
            b, free = RA.take()
            g = mm3(b.t[:], lhi[:, 2, c * P:(c + 1) * P], llo[:, 2, c * P:(c + 1) * P],
                    w.hi[:, 0, :], w.lo[:, 0, :], True, True, w.rdy, free, kvl_)
            bv = b.t[:].rearrange("p (h n) -> p h n", h=4)
            a = acopy(kt_[:, c, 4 * j:4 * j + 4, 0:64], bv[:, :, 0:64], g)
            z = cp(vt[:, c, 4 * j:4 * j + 4, :], bv[:, :, 64:128], a)
            b.done(z)
            kz += [a, z]
        w.done(g)
    q.barrier()
    Lt.close()
    Lr = ExitStack()
    sqb = sbuf("sqb", [P, 12, 96], scope=Lr)
    r4 = [sbuf(f"r4{i}", [P, 12, 16], scope=Lr) for i in range(4)]
    r48 = sbuf("r48", [P, 2, 48], scope=Lr)
    prev_ = None
    nz = []
    for c in range(4):
        cb = cosT[:, c, :].unsqueeze(1).to_broadcast([P, 12, 16])
        sb_ = sinT[:, c, :].unsqueeze(1).to_broadcast([P, 12, 16])
        prev_ = rope(qt[:, c, :, 64:80], qt[:, c, :, 80:96], cb, sb_, [x[:] for x in r4], qz, prev_)
    zz = None
    for w_, src in enumerate((kt_, qt)):
        for c in range(4):
            a = act(sqb[:], src[:, c], ACT.Square, zz, kz, zkr, prev_)
            zz = red(r48[:, w_, 12 * c:12 * c + 12], sqb[:], ADD, a)
        a = rstd_of(r48[:, w_, :], r48[:, w_, :], 96, zz)
        for c in range(4):
            nz.append(tt(src[:, c], src[:, c], r48[:, w_, 12 * c:12 * c + 12].unsqueeze(2).to_broadcast([P, 12, 96]),
                         MUL, a, eng="pool" if c % 2 else "dve"))
    q.barrier()
    Lr.close()

    qk = ExitStack()
    qh_r = Ring([Slot(sbuf(f"qh{i}", [96, T], scope=qk)) for i in range(2)])
    kh_r = Ring([Slot(sbuf(f"kh{i}", [96, T], scope=qk)) for i in range(2)])
    QK = {}

    def mla_start(h):
        if h >= 2:
            lastpe = q.end["pe"]
            QK[h - 2][0].done(lastpe)
            QK[h - 2][2].done(lastpe)
        outs = []
        for src, ring, gi in ((qt, qh_r, 0), (kt_, kh_r, 1)):
            b, free = RT.take()
            for c in range(4):
                g = tr(b.t[0:96, c * P:(c + 1) * P], src[:, c, h, :], ident[:], free, nz)
            s_, f2 = ring.take()
            a = act(s_.t[:], b.t[0:96, :], ACT.Identity, g, f2, zg, l_q, scale=gq96[:, gi:gi + 1])
            b.done(a)
            outs += [s_, a]
        QK[h] = outs

    sc, fin0 = attention(
        "mla", 12,
        lambda h, i: (QK[h][0].t[:, i * P:(i + 1) * P], QK[h][1]),
        lambda h, n: (QK[h][2].t[:, 0:n], QK[h][3]),
        lambda h, j: (vt[:, j, h, :], None),
        lambda i: P * (i + 1), True, dst(y1, 0), head_start=mla_start)
    q.barrier()
    sc.close()
    qk.close()
    sc, fin1 = mem_attention(1, y1, mqT1, mq_)
    out_and_ffn(1, y1, fin0 + fin1, True)
    sc.close()
    L1.close()
    ffn(1, True)
    assert state["next"] == len(chunks)

    q.number()
    with nc.Block() as block:
        @block.sync
        def _(e):
            q.emit("sp", e, sems)
            for _, s, n in last_out:
                e.wait_ge(s, n)

        @block.scalar
        def _(e):
            q.emit("act", e, sems)

        @block.vector
        def _(e):
            q.emit("dve", e, sems)

        @block.gpsimd
        def _(e):
            q.emit("pool", e, sems)

        @block.tensor
        def _(e):
            q.emit("pe", e, sems)
    ctx.close()


def lay_out(inputs):
    a = {k: np.asarray(v) for k, v in inputs.items()}
    parts = []
    for _, name, l, k0, kt, c0, n in plan_chunks():
        w = a[name] if l is None else a[name][l]
        parts.append(w[k0:k0 + kt * P, c0:c0 + n].reshape(kt, P, n).transpose(1, 0, 2).reshape(-1))
    vec = np.zeros((P, NVEC), np.float32)

    def put(name, m):
        c, n = VECS[name]
        vec[:, c:c + n] = m

    put("norm_g", a["norm_g"][0].reshape(8, P).T)
    put("conv_w", a["conv_w"][0].reshape(4, 6, P).transpose(2, 1, 0).reshape(P, 24))
    put("norm_mix", a["norm_mix_2"].reshape(16, P).T)
    put("norm_ffn", a["norm_ffn_2"].reshape(16, P).T)
    put("mem_norm", a["mem_norm_2"].reshape(8, P).T)
    put("qa", a["mla_qa_norm_2"][0].reshape(2, P).T)
    put("kva", a["mla_kva_norm_2"].reshape(1, P).T)
    put("b_alpha", a["b_alpha"].reshape(1, P).T)
    put("fq", np.tile(a["fox_q_gain_2"][0], 2)[:, None])
    put("fk", np.tile(a["fox_k_gain_2"][0], 2)[:, None])
    put("mq", np.tile(a["mem_q_gain_2"], (1, 2)).T)
    put("mk", np.tile(a["mem_k_gain_2"], (1, 2)).T)
    for l in range(2):
        put(f"cw{l}", a["ffn_conv_w_2"][l].reshape(3, 44, P).transpose(2, 1, 0).reshape(P, 132))
        put(f"cb{l}", a["ffn_conv_b_2"][l].reshape(44, P).T)
    rel = a["rel_bias"][0]
    out = {"pos": a["positions_2"].reshape(4, P).T, "wts": np.concatenate(parts), "vecs": vec,
           "rel_ext": np.concatenate([rel, np.repeat(rel[:, 256:257], 640 - 257, axis=1)], axis=1)}
    for k in ("x", "mem_2", "fox_b_f_2", "b_gates", "ml_norm_g", "gla_norm_g", "w_alpha", "final_g",
              "mla_q_gain_2", "mla_k_gain_2"):
        out[k] = a[k]
    return {k: np.ascontiguousarray(v) for k, v in out.items()}


def kernel(**inputs):
    import concourse.bacc as bacc
    from concourse.bass_utils import run_bass_kernel_spmd

    nc = bacc.Bacc("TRN2", target_bir_lowering=False, num_devices=1)
    arrays = lay_out(inputs)
    d = {k: nc.dram_tensor(f"in_{k}", v.shape, mybir.dt.from_np(v.dtype), kind="ExternalInput").ap()
         for k, v in arrays.items()}
    out = nc.dram_tensor("out_0", (1, T, D), F32, kind="ExternalOutput").ap()
    build(nc, d, out)
    r = run_bass_kernel_spmd(nc, [{f"in_{k}": v for k, v in arrays.items()}], core_ids=[0])
    return r.results[0]["out_0"]
```

```python
from contextlib import ExitStack

import numpy as np
import concourse.bass as bass
from concourse import mybir

F32 = mybir.dt.float32
F32R = mybir.dt.float32r
BF16 = mybir.dt.bfloat16
I32 = mybir.dt.int32
ALU = mybir.AluOpType
ACT = mybir.ActivationFunctionType
AX = mybir.AxisListType.X
P = 128
T = 512
D = 1024
EPS = 1e-6
NEG = -1e30
FF = 2816
CAP = 1536


def plan_chunks():
    out = []

    def fm(key, name, l, kt, c0, cols):
        for c in range(c0, c0 + cols, P):
            out.append((key, name, l, 0, kt, c, P))

    def tm(key, name, l, c0, cols, step=384):
        for c in range(c0, c0 + cols, step):
            n = min(step, c0 + cols - c)
            for half in range(2):
                out.append((key, name, l, half * 512, 4, c, n))

    fm("memk", "w_mem_kv_2", None, 8, 0, 256)
    tm("memv", "w_mem_kv_2", None, 256, 256)
    fm("aq", "w_in", 0, 8, 0, 384)
    fm("ak", "w_in", 0, 8, 384, 384)
    tm("av", "w_in", 0, 768, 384)
    tm("ag", "w_in", 0, 1152, 384)
    fm("mqk", "w_in", 0, 8, 1536, 768)
    tm("mv", "w_in", 0, 2304, 384)
    tm("mo", "w_in", 0, 2688, 384)
    fm("gate", "w_in", 0, 8, 3072, 128)
    tm("mg", "w_in", 0, 3084, 384)
    fm("ga", "w_in", 0, 8, 3980, 128)
    fm("gqk", "w_in", 0, 8, 3468, 256)
    tm("gv", "w_in", 0, 3724, 256)
    tm("gg", "w_in", 0, 3996, 256)
    tm("wo1", "w_out", 0, 0, 1024)

    def tail(l):
        fm("wo", "w_out_2", l, 8, 0, 1024)
        for half in range(2):
            for ct in range(11):
                c = (11 * half + ct) * P
                fm("up", "ffn_w_up_2", l, 8, c, P)
                fm("up", "ffn_w_up_2", l, 8, FF + c, P)
            for m in range(8):
                out.append(("down", "ffn_w_down_2", l, half * 1408, 11, m * P, P))

    fm("ff", "fox_w_in_2", 0, 8, 2304, 128)
    fm("fm", "fox_w_in_2", 0, 8, 2316, 256)
    fm("fqk", "fox_w_in_2", 0, 8, 0, 1536)
    tm("fv", "fox_w_in_2", 0, 1536, 768)
    tail(0)
    fm("ql", "mla_w_in_2", 0, 8, 0, 256)
    fm("kvl", "mla_w_in_2", 0, 8, 256, 128)
    out.append(("kr", "mla_w_in_2", 0, 0, 8, 384, 32))
    fm("mm", "mla_w_in_2", 0, 8, 416, 256)
    for j in range(3):
        out.append(("qup", "mla_w_q_up_2", 0, 0, 2, 384 * j, 384))
        out.append(("kvup", "mla_w_kv_up_2", 0, 0, 1, 512 * j, 512))
    tail(1)
    return out


VECS = {}


def _vecs():
    at = 0
    for name, n in (("norm_g", 8), ("conv_w", 24), ("norm_mix", 16), ("norm_ffn", 16), ("mem_norm", 8),
                    ("qa", 2), ("kva", 1), ("b_alpha", 1), ("fq", 1), ("fk", 1), ("mq", 2), ("mk", 2),
                    ("cw0", 132), ("cb0", 44), ("cw1", 132), ("cb1", 44)):
        VECS[name] = (at, n)
        at += n
    return at


NVEC = _vecs()


class Handle:
    __slots__ = ("eng", "used", "val")

    def __init__(self, eng):
        self.eng, self.used, self.val = eng, False, 0


class Queues:

    ENG = ("pe", "act", "dve", "pool", "sp")

    def __init__(self):
        self.q = {e: [] for e in self.ENG}
        self.held = {e: [] for e in self.ENG}
        self.end = {}

    def op(self, eng, fn, deps):
        h = Handle(eng)
        flat = list(self.held[eng])
        self.held[eng] = []
        stack = list(deps)
        while stack:
            d = stack.pop()
            if d is None:
                continue
            if isinstance(d, (list, tuple)) and not (len(d) == 3 and d[0] == "dma"):
                stack.extend(d)
                continue
            if isinstance(d, Handle):
                d.used = True
            flat.append(d)
        if eng == "pool" and self.q[eng]:
            self.q[eng][-1][2].used = True
            flat.append(self.q[eng][-1][2])
        self.q[eng].append((fn, flat, h))
        self.end[eng] = h
        return h

    def last(self):
        return [self.end[e] for e in ("pe", "act", "dve", "pool") if e in self.end]

    def barrier(self):
        now = self.last()
        for h in now:
            h.used = True
        for e in ("act", "dve", "pool"):
            self.held[e] = self.held[e] + now
        return now

    def number(self):
        for e in self.ENG:
            n = 0
            for _, _, h in self.q[e]:
                if h.used:
                    n += 1
                    h.val = n

    def emit(self, eng, e, sems):
        seen = {}
        for fn, deps, h in self.q[eng]:
            need = {}
            for d in deps:
                s, v = (sems[d.eng], d.val) if isinstance(d, Handle) else (d[1], d[2])
                k = id(s)
                if v > seen.get(k, 0) and v > need.get(k, (None, 0))[1]:
                    need[k] = (s, v)
            for k, (s, v) in need.items():
                e.wait_ge(s, v)
                seen[k] = v
            ins = fn(e)
            if h.used:
                ins.then_inc(sems[eng], 1)


class Slot:

    def __init__(self, t):
        self.t, self.free = t, []

    def take(self):
        f, self.free = self.free, None
        assert f is not None, "slot in use"
        return f

    def done(self, *hs):
        self.free = list(hs)


class Ring:
    def __init__(self, slots):
        self.s, self.i = slots, 0

    def take(self):
        s = self.s[self.i % len(self.s)]
        self.i += 1
        return s, s.take()


def build(nc, d, out):
    q = Queues()
    ctx = ExitStack()
    chunks = plan_chunks()

    def sem(n):
        return ctx.enter_context(nc.semaphore(n))

    def sbuf(name, shape, dt=F32, scope=None):
        return (scope or ctx).enter_context(nc.sbuf_tensor(name, shape, dt))

    sems = {e: sem("s_" + e) for e in Queues.ENG}

    def mm(o, lhsT, rhs, start, stop, *deps):
        return q.op("pe", lambda e: e.matmul(o, lhsT, rhs, start=start, stop=stop), deps)

    def mmx(o, lhsT, rhs, start, stop, *deps):
        return q.op("pe", lambda e: e.matmul(o, lhsT, rhs, start=start, stop=stop, skip_group_check=True), deps)

    def tr(o, i, ident, *deps):
        return q.op("pe", lambda e: e.transpose(o, i, ident), deps)

    def act(o, i, f, *deps, bias=0.0, scale=1.0, acc=None):
        if acc is None:
            return q.op("act", lambda e: e.activation(o, i, f, bias=bias, scale=scale), deps)
        return q.op("act", lambda e: e.activation(o, i, f, bias=bias, scale=scale, accum_out=acc), deps)

    def acopy(o, i, *deps):
        return q.op("act", lambda e: e.copy(o, i), deps)

    def tt(o, a, b, op, *deps, eng="dve"):
        return q.op(eng, lambda e: e.tensor_tensor(o, a, b, op), deps)

    def ts(o, a, s1, s2, op0, op1, *deps, eng="dve"):
        if op1 is None:
            return q.op(eng, lambda e: e.tensor_scalar(o, a, s1, None, op0), deps)
        return q.op(eng, lambda e: e.tensor_scalar(o, a, s1, s2, op0, op1), deps)

    def stt(o, a, s, b, op0, op1, *deps, eng="dve"):
        return q.op(eng, lambda e: e.scalar_tensor_tensor(out=o, in0=a, scalar=s, in1=b, op0=op0, op1=op1), deps)

    def cp(o, i, *deps, eng="dve"):
        return q.op(eng, lambda e: e.tensor_copy(o, i), deps)

    def recip(o, i, *deps):
        return q.op("dve", lambda e: e.reciprocal(o, i), deps)

    def red(o, i, op, *deps, negate=None):
        return q.op("dve", lambda e: e.tensor_reduce(o, i, AX, op, negate=negate), deps)

    def mset(ap, v, *deps, eng="pool"):
        return q.op(eng, lambda e: e.memset(ap, v), deps)

    def sel(ap, pattern, cmp, fill, base, cm, *deps):
        return q.op("pool", lambda e: e.affine_select(out=ap, in_=ap, pattern=pattern, compare_op=cmp, fill=fill,
                                                       base=base, channel_multiplier=cm), deps)

    dcount = {}

    def dma(o, i, s, *deps):
        n = dcount[id(s)] = dcount.get(id(s), 0) + 16
        q.op("sp", lambda e: e.dma_start(o, i).then_inc(s, 16), deps)
        return ("dma", s, n)

    def table(name):
        end = q.end.get("act")
        q.op("act", lambda e: e.preload_act_table_set(name), ())
        if end is not None:
            q.end["act"] = end

    MUL, ADD, SUB, MAX, MIN = ALU.mult, ALU.add, ALU.subtract, ALU.max, ALU.min

    banks = [Slot(ctx.enter_context(nc.psum_tensor(f"bank{i}", [P, 512], F32))) for i in range(8)]
    RA = Ring(banks[0:7])
    stat = banks[7]
    RS, RT, RO = Ring(banks[0:4]), Ring(banks[4:6]), Ring(banks[6:8])

    ident = sbuf("ident", [P, P])
    identb = sbuf("identb", [P, P], BF16)
    maskb = sbuf("maskb", [P, P], BF16)
    ones = sbuf("ones", [P, P])
    blk = sbuf("blk", [P, P])
    epsc = sbuf("epsc", [P, 1])
    vc = sbuf("vc", [P, NVEC])
    small = sbuf("small", [P, 256])
    stage = [Slot(sbuf(f"wstage{i}", [P, CAP])) for i in range(3)]
    whi = [Slot(sbuf(f"whi{i}", [P, CAP], F32R)) for i in range(3)]
    wlo = [Slot(sbuf(f"wlo{i}", [P, CAP], F32R)) for i in range(3)]
    RST, RHI, RLO = Ring(stage), Ring(whi), Ring(wlo)
    hhi = sbuf("hhi", [P, 8, T], F32R)
    hlo = sbuf("hlo", [P, 8, T], F32R)
    xT = sbuf("xT", [P, 8, T])
    tmp = Ring([Slot(sbuf(f"tmp{i}", [P, T])) for i in range(5)])
    hold = Ring([Slot(sbuf(f"hold{i}", [P, T])) for i in range(1)])
    kmn = sbuf("kmn", [P, 2, 256])
    kmg = sbuf("kmg", [P, 2, 256])
    vmem = sbuf("vmem", [P, 2, 256])
    fb = sbuf("fb", [12, 1])
    sinT = sbuf("sinT", [P, 4, 16])
    cosT = sbuf("cosT", [P, 4, 16])

    s_stage = [sem(f"s_w{i}") for i in range(3)]
    s_x, s_c, s_m, s_u = sem("s_x"), sem("s_c"), sem("s_m"), sem("s_u")
    s_out = [sem("s_out0"), sem("s_out1")]

    def col(name, i=0, n=P):
        a = VECS[name][0] + i
        return vc[0:n, a:a + 1]

    mscope = ExitStack()
    xt = sbuf("xt", [P, 4, D], scope=mscope)
    yt = xT[:].rearrange("p a b -> p (a b)").rearrange("p (c n) -> p c n", c=4)
    iscope = ExitStack()
    memt = sbuf("memt", [P, 2, D], scope=iscope)
    l_mem = dma(memt[:], d["mem_2"].rearrange("a (c p) n -> p (a c) n", p=P), s_m)
    l_vc = dma(vc[:], d["vecs"], s_c)
    l_fb = dma(fb[:], d["fox_b_f_2"].rearrange("a n -> n a"), s_c)
    l_c = l_fb

    offs, at = [], 0
    for (_, _, _, _, kt, _, n) in chunks:
        offs.append(at)
        at += P * kt * n

    class W:
        pass

    state = {"next": 0, "loaded": 0, "split": 0}
    staged, ready = {}, {}

    def load(i):
        _, _, _, _, kt, _, n = chunks[i]
        w = kt * n
        s, free = RST.take()
        k = (RST.i - 1) % 3
        src = d["wts"][offs[i]:offs[i] + P * w].rearrange("(p w) -> p w", p=P)
        staged[i] = (s, dma(s.t[:, 0:w], src, s_stage[k], free))

    def split(i):
        _, _, _, _, kt, _, n = chunks[i]
        w = kt * n
        s, l = staged.pop(i)
        hi, f1 = RHI.take()
        lo, f2 = RLO.take()
        a = acopy(hi.t[:, 0:w], s.t[:, 0:w], l, f1)
        b = tt(lo.t[:, 0:w], s.t[:, 0:w], hi.t[:, 0:w].bitcast(F32), SUB, a, f2)
        s.done(b)
        o = W()
        o.hi = hi.t[:, 0:w].rearrange("p (k n) -> p k n", k=kt)
        o.lo = lo.t[:, 0:w].rearrange("p (k n) -> p k n", k=kt)
        o.rdy = b
        o.done = lambda h: (hi.done(h), lo.done(h))
        ready[i] = o

    def ahead(i):
        while True:
            n = state["split"]
            if state["loaded"] < min(len(chunks), n + 3):
                load(state["loaded"])
                state["loaded"] += 1
            elif n < len(chunks) and n <= i + 2 and RHI.s[RHI.i % len(RHI.s)].free is not None:
                split(n)
                state["split"] += 1
            else:
                return

    def weights(key):
        i = state["next"]
        state["next"] += 1
        assert chunks[i][0] == key, (chunks[i], key)
        ahead(i)
        return ready.pop(i)

    ahead(-1)
    l_x = dma(xt[:], d["x"].rearrange("a (c p) n -> p (a c) n", p=P), s_x)

    table("natural_log_exp_and_others")
    c0 = mset(ident[:], 0.0)
    c_id = sel(ident[:], [[-1, P]], ALU.not_equal, 1.0, 0, 1, c0)
    c1 = mset(identb[:], 0.0)
    c_idb = sel(identb[:], [[-1, P]], ALU.not_equal, 1.0, 0, 1, c1)
    c2 = mset(maskb[:], 0.0)
    c_mk = sel(maskb[:], [[-1, P]], ALU.is_ge, NEG, 0, 1, c2)
    c_1 = mset(ones[:], 1.0)
    c3 = mset(blk[:], 0.0)
    c4 = mset(blk[0:64, 0:64], 1.0, c3)
    c5 = mset(blk[64:128, 64:128], 1.0, c3)
    c_e = mset(epsc[:], EPS)
    C = [c_id, c_idb, c_mk, c_1, c4, c5, c_e]

    def mm3(o, lh, ll, rh, rl, start, stop, *deps):
        mm(o, lh, rh, start, False, *deps)
        mm(o, lh, rl, False, False)
        return mm(o, ll, rh, False, stop)

    def at(dep, k):
        return dep[k] if isinstance(dep, list) else dep

    def fm_tile(key, xh, xl, kt, n, dep=None, ring=None):
        if early:
            return early.pop(0)
        w = weights(key)
        b, free = (ring or RA).take()
        for k in range(kt):
            h = mm3(b.t[:, 0:n], w.hi[:, k, :], w.lo[:, k, :], xh[:, k, 0:n], xl[:, k, 0:n],
                    k == 0, k == kt - 1, w.rdy, free, at(dep, k))
        w.done(h)
        return b, h

    early = []

    def fm_first(keys, xh, xl, kt, n, dep, ring=None):
        w2 = [weights(key) for key in keys]
        bs = [(ring or RA).take() for _ in w2]
        for k in range(kt):
            for w, (b, free) in zip(w2, bs):
                h = mm3(b.t[:, 0:n], w.hi[:, k, :], w.lo[:, k, :], xh[:, k, 0:n], xl[:, k, 0:n],
                        k == 0, k == kt - 1, w.rdy, free, at(dep, k))
                if k == kt - 1:
                    w.done(h)
                    early.append((b, h))

    def tm_group(key, xh, xl, tiles, cols, dep=None):
        w2 = [weights(key), weights(key)]
        for c in range(tiles):
            b, free = RA.take()
            for kk in range(8):
                w = w2[kk // 4]
                g = mm3(b.t[:, 0:cols], xh[:, kk, c * P:(c + 1) * P], xl[:, kk, c * P:(c + 1) * P],
                        w.hi[:, kk % 4, :], w.lo[:, kk % 4, :], kk == 0, kk == 7, w.rdy, free, at(dep, kk))
            if c == tiles - 1:
                w2[0].done(g)
                w2[1].done(g)
            yield b, g

    flip = [0]

    def evac(o, i, *deps):
        flip[0] += 1
        return acopy(o, i, *deps) if flip[0] % 2 else cp(o, i, *deps)

    def split_bank(b, h, hi, lo, scale=None):
        n = hi.shape[-1]
        if scale is None:
            a = acopy(hi, b.t[:, 0:n], h)
            z = tt(lo, b.t[:, 0:n], hi.bitcast(F32), SUB, a)
        else:
            a = act(hi, b.t[:, 0:n], ACT.Identity, h, scale=scale)
            z = stt(lo, b.t[:, 0:n], scale, hi.bitcast(F32), MUL, SUB, a)
        b.done(z)
        return z

    def rstd_of(o, i, n, *deps):
        a = act(o, i, ACT.Ln, *deps, scale=1.0 / n, bias=epsc[0:i.shape[0], :])
        return act(o, o, ACT.Exp, a, scale=-0.5)

    def token_rms(src, tiles, at, *deps):
        t, free = tmp.take()
        t2, free2 = tmp.take()
        sc = small[:, at:at + 2 * tiles]
        last = None
        for c in range(tiles):
            for hf in range(2):
                last = act((t, t2)[hf].t[:], src[:, c, hf * 512:(hf + 1) * 512], ACT.Square, *deps, free, free2, last,
                           acc=sc[:, 2 * c + hf:2 * c + hf + 1])
        t.done(last)
        t2.done(last)
        a = tt(small[:, at + 16:at + 16 + tiles], small[:, at:at + 2 * tiles:2], small[:, at + 1:at + 2 * tiles:2], ADD, last)
        return rstd_of(small[:, at + 16:at + 16 + tiles], small[:, at + 16:at + 16 + tiles], D, a), at + 16

    def transpose_tokens(src, tiles, ready_, dst, kts=range(8)):
        r = []
        for kt in kts:
            b, free = RA.take()
            for c in range(tiles):
                h = tr(b.t[:, c * P:(c + 1) * P], src[:, c, kt * P:(kt + 1) * P], ident[:], ready_, free, C)
            r.append(dst(kt, b, h))
        return r

    r, at_ = token_rms(memt, 2, 160, l_mem, C)
    for c in range(2):
        r2 = ts(memt[:, c, :], memt[:, c, :], small[:, at_ + c:at_ + c + 1], None, MUL, None, r, l_c)
    mh = hhi[:].rearrange("p a b -> p (a b)")[:, 0:2048].rearrange("p (k n) -> p k n", k=8)
    ml = hlo[:].rearrange("p a b -> p (a b)")[:, 0:2048].rearrange("p (k n) -> p k n", k=8)
    mr = transpose_tokens(memt, 2, r2, lambda kt, b, h: split_bank(b, h, mh[:, kt, :], ml[:, kt, :], col("mem_norm", kt)))
    r, at_ = token_rms(xt, 4, 0, l_x, C)
    for c in range(4):
        xr2 = ts(yt[:, c, :], xt[:, c, :], small[:, at_ + c:at_ + c + 1], None, MUL, None, r)
    for m in range(2):
        b, h = fm_tile("memk", mh, ml, 8, 256, mr)
        t, free = tmp.take()
        a = act(t.t[:, 0:256], b.t[:, 0:256], ACT.Square, h, free)
        b2, free = RA.take()
        g = mm(b2.t[:, 0:256], blk[:], t.t[:, 0:256], True, True, a, free, C)
        t2, free = tmp.take()
        a = rstd_of(t2.t[:, 0:256], b2.t[:, 0:256], 64, g, free)
        z = tt(kmn[:, m, :], b.t[:, 0:256], t2.t[:, 0:256], MUL, a)
        t.done(g)
        b2.done(a)
        b.done(z)
        t2.done(z)
    for c, (b, h) in enumerate(tm_group("memv", mh, ml, 2, 256, mr)):
        z = evac(vmem[:, c, :], b.t[:, 0:256], h)
        b.done(z)
    ahead(state["next"])
    hr = transpose_tokens(yt, 4, xr2, lambda kt, b, h: split_bank(b, h, hhi[:, kt, :], hlo[:, kt, :], col("norm_g", kt)))
    q.barrier()
    iscope.close()

    class Head:

        def __init__(self, q, k, v, width, causal=False, bias=None, prep=None, low=None, add=None):
            self.low, self.add = low, add
            self.q, self.k, self.v, self.width = q, k, v, width
            self.causal, self.bias, self.prep = causal, bias, prep

    def attention(name, heads, dst, post=None, side=None):
        sc = ExitStack()
        nh = len(heads)
        pt = Ring([Slot(sbuf(f"{name}_pt{i}", [P, T], scope=sc)) for i in range(3)])
        biased = any(h.bias for h in heads)
        st = Ring([Slot(sbuf(f"{name}_s{i}", [P, T], scope=sc)) for i in range(2)]) if biased else None
        mx = sbuf(f"{name}_mx", [P, nh, 4], scope=sc)
        rs = sbuf(f"{name}_rs", [P, nh, 4], scope=sc)
        items = [(h, i) for h in range(nh) for i in (3, 0, 2, 1)]
        S, PR, PT, O = {}, {}, {}, {}
        fin = []

        def score(t):
            h, i = items[t]
            n = heads[h].width(i)
            b, free = RS.take()
            (qa, qh), (ka, kh) = heads[h].q(i), heads[h].k(n)
            hd = heads[h]
            last_ = not hd.causal and not hd.low and not hd.add
            g = mm(b.t[:, 0:n], qa, ka, True, last_, qh, kh, free)
            if hd.low:
                ql_, kl_ = hd.low(i, n)
                mm(b.t[:, 0:n], qa, kl_, False, False)
                g = mm(b.t[:, 0:n], ql_, ka, False, not hd.causal and not hd.add)
            if hd.add:
                sa, ca, *dep = hd.add(n)
                g = mm(b.t[:, 0:n], sa, ca, False, not hd.causal, dep)
            if heads[h].causal:
                g = mm(b.t[:, n - P:n], identb[:], maskb[:], False, True, C)
            S[t] = (b, g, n)

        def soft(t):
            h, i = items[t]
            b, g, n = S.pop(t)
            p_, free = tmp.take()
            m = mx[:, h, i:i + 1]
            if heads[h].bias:
                s_, f2 = st.take()
                ba, bh = heads[h].bias(i, n)
                z = q.op("dve", lambda e: e.tensor_tensor_reduce(s_.t[:, 0:n], b.t[:, 0:n], ba, 1.0, -3e38, ADD,
                                                                 MAX, m), (g, bh, f2))
                b.done(z)
                z = ts(m, m, -1.0, None, MUL, None, z)
                a = act(p_.t[:, 0:n], s_.t[:, 0:n], ACT.Exp, z, free, bias=m, acc=rs[:, h, i:i + 1])
                s_.done(a)
            else:
                z = red(m, b.t[:, 0:n], MAX, g, negate=True)
                a = act(p_.t[:, 0:n], b.t[:, 0:n], ACT.Exp, z, free, bias=m, acc=rs[:, h, i:i + 1])
                b.done(a)
            PR[t] = (p_, a, n)

        def turn(t):
            p_, a, n = PR.pop(t)
            b, free = RT.take()
            for j in range(n // P):
                g = tr(b.t[:, j * P:(j + 1) * P], p_.t[:, j * P:(j + 1) * P], ident[:], a, free)
            p_.done(g)
            s_, f2 = pt.take()
            z = cp(s_.t[:, 0:n], b.t[:, 0:n], g, f2)
            b.done(z)
            PT[t] = (s_, z, n)

        def pv(t):
            h, i = items[t]
            s_, z, n = PT.pop(t)
            if t % 8 == 0:
                O[t // 8] = RO.take()
            b, free = O[t // 8]
            o = b.t[:, ((h % 2) * 4 + i) * 64:((h % 2) * 4 + i) * 64 + 64]
            for j in range(n // P):
                va, vh = heads[h].v(j)
                g = mm(o, s_.t[:, j * P:(j + 1) * P], va, j == 0, j == n // P - 1, z, vh, free)
            s_.done(g)
            if t % 8 == 7:
                h0 = h - 1
                rr = rs[:, h0:h0 + 2, :]
                a = recip(rr, rr, g)
                o_, f3 = dst(t // 8)
                for ii in range(4):
                    ov = b.t[:, :].rearrange("p (h i n) -> p h i n", h=2, i=4)[:, :, ii, :]
                    z = tt(o_(ii), ov, rr[:, :, ii:ii + 1].to_broadcast([P, 2, 64]), MUL, a, f3)
                b.done(z)
                fin.append(z)

        N = len(items)
        for t in range(-2, N + 8):
            if (t + 2) % 4 == 0 and t + 2 < N and heads[(t + 2) // 4].prep:
                heads[(t + 2) // 4].prep()
            if 0 <= t < N:
                score(t)
            if 1 <= t <= N:
                soft(t - 1)
            if 3 <= t <= N + 2:
                turn(t - 3)
            if 5 <= t <= N + 4:
                pv(t - 5)
            if side:
                side(t)
            if post and t >= 14 and (t - 14) % 8 == 0 and (t - 14) // 8 < len(fin):
                post((t - 14) // 8, fin[(t - 14) // 8])
        return sc, fin

    def sigmoid_den(o, i, *deps):
        a = act(o, i, ACT.Exp, *deps, scale=-1.0)
        return ts(o, o, 1.0, None, ADD, None, a)

    def log_sigmoid(o, i, rows, n, *deps):
        t, free = tmp.take()
        tt_ = t.t[0:rows, 0:n]
        a = act(tt_, i, ACT.Abs, *deps, free)
        a = act(tt_, tt_, ACT.Exp, a, scale=-1.0)
        a = act(tt_, tt_, ACT.Ln, a, bias=1.0)
        z = stt(o, i, 0.0, tt_, MIN, SUB, a)
        t.done(z)
        return z

    s1 = ExitStack()
    aqT = sbuf("aqT", [P, 3, T], scope=s1)
    akT = sbuf("akT", [P, 3, T], scope=s1)
    av = sbuf("av", [P, 4, 384], scope=s1)
    ag = sbuf("ag", [P, 4, 384], scope=s1)
    ge = sbuf("ge", [P, 4, 384], scope=s1)
    U = sbuf("U", [P, 6, 512], scope=s1)
    bar = q.last()
    for hh in range(6):
        src = d["rel_ext"][hh:hh + 1, 1:513]
        skew = bass.AP(tensor=src.tensor, offset=src.offset, ap=[[1, P], [1, 512]])
        l_u = dma(U[:, hh, :], skew, s_u, bar)
    u_ok = mset(U[0:64, :, 0:64], NEG, l_u)
    q_, k_ = [], []
    fm_first(("aq", "aq"), hhi, hlo, 8, T, hr)
    for m in range(3):
        b, h = fm_tile("aq", hhi, hlo, 8, T, hr)
        z = act(aqT[:, m, :], b.t[:], ACT.Identity, h, scale=0.125)
        b.done(z)
        q_.append(z)
    for m in range(3):
        b, h = fm_tile("ak", hhi, hlo, 8, T)
        z = cp(akT[:, m, :], b.t[:], h)
        b.done(z)
        k_.append(z)
    v_ = []
    for c, (b, h) in enumerate(tm_group("av", hhi, hlo, 4, 384)):
        z = evac(av[:, c, :], b.t[:, 0:384], h)
        b.done(z)
        v_.append(z)
    for c, (b, h) in enumerate(tm_group("ag", hhi, hlo, 4, 384)):
        a = act(ge[:, c, :], b.t[:, 0:384], ACT.Exp, h, scale=-1.0)
        z = cp(ag[:, c, :], b.t[:, 0:384], a)
        b.done(z)
    ag_last = [a, z]

    def gate_part(c):
        def go():
            z = ts(ge[:, c], ge[:, c], 1.0, None, ADD, None, ag_last, eng="pool")
            z = recip(ge[:, c], ge[:, c], z)
            g_ok.append(tt(ag[:, c], ag[:, c], ge[:, c], MUL, z, eng="pool"))
        return go

    g_ok = []

    def half(h):
        return slice(64 * (h % 2), 64 * (h % 2) + 64)

    def u_bias(h, i, n):
        base = U[:, h, n - 1:n]
        return bass.AP(tensor=base.tensor, offset=base.offset, ap=[base.ap[0], [-1, n]]), u_ok

    def att_head(h):
        return Head(lambda i: (aqT[half(h), h // 2, i * P:(i + 1) * P], q_[h // 2]),
                    lambda n: (akT[half(h), h // 2, 0:n], k_[h // 2]),
                    lambda j: (av[:, j, h * 64:(h + 1) * 64], v_[j]),
                    lambda i: P * (i + 1), bias=lambda i, n: u_bias(h, i, n),
                    prep=gate_part(h - 1) if 1 <= h <= 4 else None)

    sc, fin = attention("att", [att_head(h) for h in range(6)],
                        lambda g: (lambda i: yt[:, i, g * P:(g + 1) * P].rearrange("p (h n) -> p h n", h=2), None))
    ya = tt(yt[:, :, 0:384], yt[:, :, 0:384], ag[:], MUL, fin, g_ok)
    q.barrier()
    sc.close()
    s1.close()

    s2 = ExitStack()
    cqk = sbuf("cqk", [P, 6, T], scope=s2)
    mva = sbuf("mva", [P, 4, 6, 65], scope=s2)
    mo = sbuf("mo", [P, 4, 384], scope=s2)
    mg = sbuf("mg", [P, 4, 384], scope=s2)
    hm = sbuf("hm", [P, 4, 6, 64], scope=s2)
    gts = sbuf("gts", [12, T], scope=s2)
    fr = sbuf("fr", [6, T], scope=s2)
    lf = fr
    FF_ = sbuf("Fsum", [6, T], scope=s2)
    aj = sbuf("aj", [6, T], scope=s2)
    Am = sbuf("Am", [6, T], scope=s2)
    em = sbuf("em", [6, T], scope=s2)
    bg = sbuf("bg", [12, 1], scope=s2)
    acol = sbuf("acol", [P, 4, 6], scope=s2)
    ecol = sbuf("ecol", [P, 4, 6], scope=s2)
    gml = sbuf("gml", [P, 384], scope=s2)
    bar = q.last()
    l_g = dma(bg[:], d["b_gates"].rearrange("a n -> n a"), s_u, bar)
    l_g = dma(gml[:], d["ml_norm_g"][0:1, :].to_broadcast([P, 384]), s_u, bar)
    o6 = c_1
    onesv = mset(mva[:, :, :, 64:65], 1.0)
    cq_, late = [], []
    for m in range(6):
        b, h = fm_tile("mqk", hhi, hlo, 8, T)
        t, free = tmp.take()
        x_ = t.t
        a = act(x_[:], b.t[:], ACT.Identity, h, free, l_c, scale=col("conv_w", 4 * m + 3))
        z = a
        for s in range(1, 4):
            z = stt(x_[:, s:T], b.t[:, 0:T - s], col("conv_w", 4 * m + 3 - s), x_[:, s:T], MUL, ADD, z)
        b.done(z)
        t2, free = tmp.take()
        a = act(t2.t[:], x_[:], ACT.Exp, z, free, scale=-1.0)
        z = ts(t2.t[:], t2.t[:], 1.0, None, ADD, None, a, eng="pool")

        def finish(m=m, x_=x_, t=t, t2=t2, z=z):
            z = recip(t2.t[:], t2.t[:], z)
            if m < 3:
                z = tt(cqk[:, m, :], x_[:], t2.t[:], MUL, z, eng="pool")
            else:
                z = stt(cqk[:, m, :], x_[:], 0.125, t2.t[:], MUL, MUL, z)
            t.done(z)
            t2.done(z)
            cq_.append(z)

        if late:
            late.pop()()
        late.append(finish)
    late.pop()()
    mv_ = []
    for c, (b, h) in enumerate(tm_group("mv", hhi, hlo, 4, 384)):
        z = evac(mva[:, c, :, 0:64], b.t[:, 0:384].rearrange("p (h n) -> p h n", h=6), h, onesv)
        b.done(z)
        mv_.append(z)
    mo_ = []
    for c, (b, h) in enumerate(tm_group("mo", hhi, hlo, 4, 384)):
        z = sigmoid_den(mo[:, c, :], b.t[:, 0:384], h)
        b.done(z)
        mo_.append(z)
    b, h = fm_tile("gate", hhi, hlo, 8, T)
    a = act(gts[:], b.t[0:12, :], ACT.Identity, h, l_g, bias=bg[:, 0:1])
    b.done(a)
    b, free = RA.take()
    g = mm(b.t[0:6, :], ident[0:12, 6:12], gts[:], True, True, a, free, C)
    a = acopy(fr[:], b.t[0:6, :], g)
    b.done(a)
    z = log_sigmoid(lf[:], fr[:], 6, T, a)
    z = q.op("dve", lambda e: e.tensor_tensor_scan(FF_[:], ones[0:6, 0:1].to_broadcast([6, T]), lf[:], 0.0, MUL, ADD), (z, o6))
    z = tt(aj[:], gts[0:6, :], FF_[:], SUB, z)
    z_a = z
    z = q.op("dve", lambda e: e.tensor_tensor_scan(Am[:], ones[0:6, 0:1].to_broadcast([6, T]), aj[:], 0.0, MUL, MAX), (z,))
    z_A = z
    z = tt(em[:], FF_[:], Am[:], ADD, z)
    z_e = act(em[:], em[:], ACT.Exp, z, scale=-1.0)
    b, free = RA.take()
    for c in range(4):
        tr(b.t[:, c * 6:c * 6 + 6], aj[:, c * P:(c + 1) * P], ident[0:6, 0:6], z_a, free)
    for c in range(4):
        g = tr(b.t[:, 24 + c * 6:24 + c * 6 + 6], em[:, c * P:(c + 1) * P], ident[0:6, 0:6], z_e)
    z = cp(acol[:].rearrange("p a b -> p (a b)"), b.t[:, 0:24], g)
    c_ok = cp(ecol[:].rearrange("p a b -> p (a b)"), b.t[:, 24:48], g)
    b.done(c_ok)
    mg_ = []
    for c, (b, h) in enumerate(tm_group("mg", hhi, hlo, 4, 384)):
        t, free = tmp.take()
        z = sigmoid_den(t.t[:, 0:384], b.t[:, 0:384], h, free)
        z = tt(mo[:, c, :], mo[:, c, :], t.t[:, 0:384], MUL, z, mo_[c])
        t.done(z)
        z = recip(mo[:, c, :], mo[:, c, :], z)
        z = tt(mg[:, c, :], b.t[:, 0:384], mo[:, c, :], MUL, z)
        b.done(z)
        mg_.append(z)

    dts = Ring([Slot(sbuf(f"dt{i}", [P, T], scope=s2)) for i in range(3)])
    scs = Ring([Slot(sbuf(f"scm{i}", [P, 1280], scope=s2)) for i in range(2)])
    mden = sbuf("mden", [P, 6, 4], scope=s2)
    OFF = [0, 512, 896, 1152]
    HS = {}

    def ml_decay(h):
        ab, free = RT.take()
        ga_ = mm(ab.t[:], ident[0:6, h:h + 1].to_broadcast([6, P]), Am[:], True, True, z_A, free, C)
        s_, f2 = scs.take()
        lasts = []
        for J in range(4):
            n = T - J * P
            dt_, free = dts.take()
            a = act(dt_.t[:, 0:n], ab.t[:, J * P:T], ACT.Exp, ga_, c_ok, free, scale=-1.0, bias=acol[:, J, h:h + 1])
            pz = sel(dt_.t[:, 0:P], [[1, P]], ALU.is_ge, 0.0, 0, -1, a)
            b, free = RS.take()
            g = mm(b.t[:, 0:n], cqk[half(h), 3 + h // 2, J * P:(J + 1) * P], cqk[half(h), h // 2, J * P:T],
                   True, True, cq_[h // 2], cq_[3 + h // 2], free)
            z = tt(s_.t[:, OFF[J]:OFF[J] + n], b.t[:, 0:n], dt_.t[:, 0:n], MUL, g, pz, a, f2)
            b.done(z)
            dt_.done(z)
            lasts.append(z)
        ab.done(a)
        HS[h] = (s_, lasts)

    def ml_out(h):
        s_, lasts = HS.pop(h)
        b, free = RO.take()
        for i in range(4):
            for J in range(i + 1):
                o = OFF[J] + (i - J) * P
                g = mm(b.t[:, i * 65:(i + 1) * 65], s_.t[:, o:o + P], mva[:, J, h, :], J == 0, J == i,
                       lasts[J], mv_[J], free)
        s_.done(g)
        ov = b.t[:, 0:260].rearrange("p (i n) -> p i n", i=4)
        a = act(mden[:, h, :].unsqueeze(2), ov[:, :, 64:65], ACT.Abs, g)
        z = tt(mden[:, h, :].unsqueeze(2), mden[:, h, :].unsqueeze(2), ecol[:, :, h:h + 1], MAX, a, c_ok)
        z = recip(mden[:, h, :], mden[:, h, :], z)
        z = tt(hm[:, :, h, :], ov[:, :, 0:64], mden[:, h, :].unsqueeze(2).to_broadcast([P, 4, 64]), MUL, z)
        b.done(z)
        return z

    ml_ok = []
    for h in range(7):
        if h < 6:
            ml_decay(h)
        if h > 0:
            ml_ok.append(ml_out(h - 1))

    def head_norm(hv, sq, rows, groups, n, *deps):
        a = act(sq, hv, ACT.Square, *deps)
        z = red(rows, sq, ADD, a)
        return rstd_of(rows, rows, n, z)

    hv = hm[:].rearrange("p i h n -> p (i h) n")
    sq = mo[:].rearrange("p i (h n) -> p (i h) n", h=6)
    a = head_norm(hv, sq, small[:, 32:56], 24, 64, ml_ok, mg_)
    z = tt(hv, hv, small[:, 32:56].unsqueeze(2).to_broadcast([P, 24, 64]), MUL, a)
    gb = gml[:].unsqueeze(1).to_broadcast([P, 4, 384])
    hf_ = hm[:].rearrange("p i h n -> p i (h n)")
    z2 = tt(mg[:], mg[:], gb, MUL, mg_, l_g)
    ym = [tt(yt[:, :, 384:768], hf_, mg[:], MUL, z, z2), ya]
    q.barrier()
    s2.close()

    def turn_y(y, kts, *deps):
        return transpose_tokens(y, 4, deps, lambda kt, b, h: split_bank(b, h, hhi[:, kt, :], hlo[:, kt, :]), kts)

    s3 = ExitStack()
    gq = sbuf("gq", [P, T], scope=s3)
    gk = sbuf("gk", [P, T], scope=s3)
    gv = sbuf("gv", [P, 4, 256], scope=s3)
    gg = sbuf("gg", [P, 4, 256], scope=s3)
    ge2 = sbuf("ge2", [P, 4, 256], scope=s3)
    gaT = sbuf("gaT", [16, T], scope=s3)
    wal = sbuf("wal", [16, P], scope=s3)
    pre = sbuf("pre", [P, T], scope=s3)
    bT = sbuf("bT", [P, T], scope=s3)
    ATT = sbuf("ATT", [P, 4, 4, P], scope=s3)
    AX_ = [sbuf(f"AX{J}", [P, 4, (3 - J) * P], scope=s3) for J in range(3)]
    msk = sbuf("msk", [P, 7, P], scope=s3)
    ggn = sbuf("ggn", [P, 256], scope=s3)
    hg = sbuf("hg", [P, 4, 4, 64], scope=s3)
    nref = sbuf("nref", [P, 3], scope=s3)
    kl = Ring([Slot(sbuf(f"kl{i}", [P, T], scope=s3)) for i in range(2)])
    ql = Ring([Slot(sbuf(f"ql{i}", [P, T], scope=s3)) for i in range(2)])
    bar = q.last()
    l_a = dma(wal[:], d["w_alpha"].rearrange("a r n -> (a r) n"), s_u, bar)
    l_a = dma(ggn[:], d["gla_norm_g"][0:1, :].to_broadcast([P, 256]), s_u, bar)
    z0 = mset(msk[:], 0.0)
    z1 = mset(ATT[:], 0.0)
    mk_ = []
    for li in range(7):
        s = 64 >> li
        nb = P // (2 * s)
        v4 = msk[:, li, :].rearrange("p (a b s) -> p a b s", a=nb, b=2)[:, :, 1, :]
        z = mset(v4, 1.0, z0)
        z = sel(v4, [[-2 * s, nb], [0, s]], ALU.is_ge, 0.0, 0, 1, z)
        z = sel(v4, [[2 * s, nb], [0, s]], ALU.is_ge, 0.0, s - 1, -1, z)
        mk_.append(z)
    b, h = fm_tile("ga", hhi, hlo, 8, T)
    a = acopy(gaT[:], b.t[0:16, :], h)
    b.done(a)
    b, h = fm_tile("gqk", hhi, hlo, 8, T)
    zq = act(gq[:], b.t[:], ACT.Identity, h, scale=32 ** -0.5)
    b.done(zq)
    b, free = RA.take()
    g = mm(b.t[:], wal[:], gaT[:], True, True, a, free, l_a)
    a = act(pre[:], b.t[:], ACT.Identity, g, l_c, bias=col("b_alpha"))
    b.done(a)
    b, h = fm_tile("gqk", hhi, hlo, 8, T)
    zk = cp(gk[:], b.t[:], h)
    b.done(zk)
    z = log_sigmoid(pre[:], pre[:], P, T, a)
    z = ts(pre[:], pre[:], 1.0 / 16.0, None, MUL, None, z)
    zb = q.op("dve", lambda e: e.tensor_tensor_scan(bT[:], ones[:, 0:1].to_broadcast([P, T]), pre[:], 0.0, MUL,
                                                    ADD), (z, c_1))
    LV = {}

    def level(li):
        if li == 7:
            LV[li] = (gk, gq, zk, zq, None, None)
            return
        t, free = tmp.take()
        (k2, f1), (q2, f2) = kl.take(), ql.take()
        if li < 7:
            s = 64 >> li
            nb = T // (2 * s)
            bv = bT[:].rearrange("p (a s) -> p a s", s=2 * s)
            tv = t.t[:].rearrange("p (a s) -> p a s", s=2 * s)
            z = tt(tv, bv, bv[:, :, s - 1:s].to_broadcast([P, nb, 2 * s]), SUB, zb, free)
            a = act(t.t[:], t.t[:], ACT.Abs, z)
            a = act(t.t[:], t.t[:], ACT.Exp, a, scale=-1.0)
            zk2 = tt(k2.t[:], gk[:], t.t[:], MUL, a, zk, f1)
            zq2 = tt(q2.t[:], gq[:], t.t[:], MUL, a, zq, f2, eng="pool")
        else:
            J = li - 8
            n = (3 - J) * P
            e_ = bT[:, J * P + 127:J * P + 128]
            zr = ts(nref[:, J:J + 1], e_, -1.0, None, MUL, None, zb)
            a1 = act(t.t[:, 0:P], bT[:, J * P:(J + 1) * P], ACT.Exp, zb, free, scale=-1.0, bias=e_)
            a2 = act(t.t[:, P:T - J * P], bT[:, (J + 1) * P:T], ACT.Exp, zr, bias=nref[:, J:J + 1])
            zk2 = tt(k2.t[:, 0:P], gk[:, J * P:(J + 1) * P], t.t[:, 0:P], MUL, a1, f1)
            zq2 = tt(q2.t[:, 0:n], gq[:, (J + 1) * P:T], t.t[:, P:T - J * P], MUL, a2, f2)
        t.done(zk2, zq2)
        LV[li] = (k2.t, q2.t, zk2, zq2, k2, q2)

    level(8)
    level(9)
    gv_ = []
    for c, (b, h) in enumerate(tm_group("gv", hhi, hlo, 4, 256)):
        z = evac(gv[:, c, :], b.t[:, 0:256], h)
        b.done(z)
        gv_.append(z)
    for c, (b, h) in enumerate(tm_group("gg", hhi, hlo, 4, 256)):
        a = act(ge2[:, c, :], b.t[:, 0:256], ACT.Exp, h, scale=-1.0)
        z = cp(gg[:, c, :], b.t[:, 0:256], a)
        b.done(z)
    gg_last = [a, z]
    yr = turn_y(yt, range(0, 6), ym)

    def gg_gate():
        z = ts(ge2[:], ge2[:], 1.0, None, ADD, None, gg_last, eng="pool")
        z = recip(ge2[:], ge2[:], z)
        z = tt(gg[:], gg[:], ge2[:], MUL, z, eng="pool")
        return tt(gg[:], gg[:], ggn[:].unsqueeze(1).to_broadcast([P, 4, 256]), MUL, z, l_a, eng="pool")

    ax_ = {}
    prev = {h: z1 for h in range(4)}
    order = [8, 9, 10, 0, 1, 2, 3, 4, 5, 6, 7]
    for at_i, li in enumerate(order):
        K_, Q_, zk2, zq2, k2, q2 = LV.pop(li)
        bs = []
        for h in range(4):
            b, free = RA.take()
            hp = slice(32 * h, 32 * h + 32)
            if li >= 8:
                n = (11 - li) * P
                g = mm(b.t[:, 0:n], K_[hp, 0:P], Q_[hp, 0:n], True, True, zk2, zq2, free)
            else:
                for c in range(4):
                    g = mm(b.t[:, c * P:(c + 1) * P], K_[hp, c * P:(c + 1) * P], Q_[hp, c * P:(c + 1) * P], True,
                           True, zk2, zq2, free)
            bs.append((b, g))
        if k2 is not None:
            k2.done(g)
            q2.done(g)
        if at_i + 2 < len(order):
            level(order[at_i + 2])
        for h, (b, g) in enumerate(bs):
            if li >= 8:
                z = evac(AX_[li - 8][:, h, :], b.t[:, 0:n], g)
                ax_[li - 8, h] = z
            else:
                mb = (msk[:, li, :] if li < 7 else ident[:]).bitcast(I32).unsqueeze(1).to_broadcast([P, 4, P])
                bv4 = b.t[:].rearrange("p (c n) -> p c n", c=4)
                z = q.op("dve", lambda e, h=h, mb=mb, bv4=bv4: e.copy_predicated(ATT[:, :, h, :], mb, bv4),
                         (g, mk_[li] if li < 7 else None, prev[h]))
                prev[h] = z
            b.done(z)
        if at_i == 4:
            gg_ok = gg_gate()
    gz = []
    for i in range(4):
        b, free = RA.take()
        for h in range(4):
            o = b.t[:, h * 64:(h + 1) * 64]
            for J in range(i):
                mm(o, AX_[J][:, h, (i - J - 1) * P:(i - J) * P], gv[:, J, h * 64:(h + 1) * 64], J == 0, False,
                   ax_[J, h], gv_[J], free)
            g = mm(o, ATT[:, i, h, :], gv[:, i, h * 64:(h + 1) * 64], i == 0, True, prev[h], gv_[i], free)
        z = evac(hg[:, i, :, :], b.t[:, 0:256].rearrange("p (h n) -> p h n", h=4), g)
        b.done(z)
        gz.append(z)
    hv = hg[:].rearrange("p i h n -> p (i h) n")
    sq = ge2[:].rearrange("p i (h n) -> p (i h) n", h=4)
    a = head_norm(hv, sq, small[:, 64:80], 16, 64, gz, gg_ok)
    z = tt(hv, hv, small[:, 64:80].unsqueeze(2).to_broadcast([P, 16, 64]), MUL, a)
    yz = tt(yt[:, :, 768:1024], hg[:].rearrange("p i h n -> p i (h n)"), gg[:], MUL, z)
    q.barrier()
    s3.close()

    xlast = {"h": [None] * 8}
    stats = {"pend": []}

    def stat_begin():
        stats["b"], stats["free"] = stat, stat.take()
        stats["n"] = 0

    def stat_add(k, dep):
        t, f2 = tmp.take()
        stats["pend"].append((t, act(t.t[:], xT[:, k, :], ACT.Square, dep, f2)))

    def stat_sum():
        for t, a in stats["pend"]:
            stats["g"] = mm(stat.t[:], ones[:], t.t[:], stats["n"] == 0, stats["n"] == 7, a, stats["free"])
            stats["n"] += 1
            t.done(stats["g"])
        stats["pend"] = []

    def fm_norm(gname, g0):
        stat_sum()
        ahead(state["next"])
        assert stats["n"] == 8
        rb, f2 = hold.take()
        a = rstd_of(rb.t[:], stat.t[:], D, stats["g"], f2)
        stat.done(a)
        out_ = []
        for k in range(8):
            t, f2 = tmp.take()
            z0_ = stt(t.t[:], xT[:, k, :], col(gname, g0 + k), rb.t[:], MUL, MUL, a, f2, xlast["h"][k])
            a2 = acopy(hhi[:, k, :], t.t[:], z0_)
            z = tt(hlo[:, k, :], t.t[:], hhi[:, k, :].bitcast(F32), SUB, a2, eng="pool" if k % 2 else "dve")
            t.done(z)
            out_.append(z)
        rb.done(z0_)
        return out_

    s4 = ExitStack()
    fgr = sbuf("fgr", [P, D], scope=s4)
    l_f = dma(fgr[:], d["final_g"].rearrange("(a n) -> a n", a=1).to_broadcast([P, D]), s_u, q.last())
    yr = yr + turn_y(yt, range(6, 8), yz)
    rs_ = []
    sqs = small[:, 96:112].rearrange("p (c g) -> p c g", c=4)
    zs_ = mset(sqs, 0.0, q.last())
    for gi, g0 in enumerate((0, 384, 768)):
        n = min(384, D - g0)
        for c, (b, h) in enumerate(tm_group("wo1", hhi, hlo, 4, n, yr)):
            z = tt(xt[:, c, g0:g0 + n], b.t[:, 0:n], xt[:, c, g0:g0 + n], ADD, h)
            b.done(z)
            t, free = tmp.take()
            a = act(t.t[:, 0:n], xt[:, c, g0:g0 + n], ACT.Square, z, free, zs_, acc=sqs[:, c, gi:gi + 1])
            t.done(a)
            rs_.append(a)
    z = red(small[:, 112:116], sqs, ADD, rs_)
    r = rstd_of(small[:, 112:116], small[:, 112:116], D, z)
    at_ = 112
    for c in range(4):
        r2 = stt(xt[:, c, :], xt[:, c, :], small[:, at_ + c:at_ + c + 1], fgr[:], MUL, MUL, r, l_f)

    xz = []

    def to_x(kt, b, h):
        z = evac(xT[:, kt, :], b.t[:], h)
        b.done(z)
        stat_sum()
        stat_add(kt, z)
        xz.append(z)
        return z

    stat_begin()
    ahead(state["next"])
    transpose_tokens(xt, 4, r2, to_x)
    xlast["h"] = xz
    hr = fm_norm("norm_mix", 0)
    q.barrier()
    s4.close()
    mscope.close()


    def head_normed(key, dst, gcol, dep=None, gdep=None):
        b, h = fm_tile(key, hhi, hlo, 8, T, dep)
        t, free = tmp.take()
        a = act(t.t[:], b.t[:], ACT.Square, h, free)
        yield None
        b2, free = RA.take()
        g = mm(b2.t[:], blk[:], t.t[:], True, True, a, free)
        t.done(g)
        t2, free = tmp.take()
        a = rstd_of(t2.t[:], b2.t[:], 64, g, free)
        b2.done(a)
        if type(dst) is not tuple:
            z = stt(dst, b.t[:], gcol, t2.t[:], MUL, MUL, a, gdep)
            b.done(z)
        else:
            z = stt(t2.t[:], b.t[:], gcol, t2.t[:], MUL, MUL, a, gdep)
            b.done(z)
            a = acopy(dst[0], t2.t[:], z)
            z = tt(dst[1], t2.t[:], dst[0].bitcast(F32), SUB, a, eng="pool")
        t2.done(z)
        yield z

    def head_normed_all(jobs):
        out_, before = [], None
        for j in jobs:
            g = head_normed(*j)
            next(g)
            if before:
                out_.append(next(before))
            before = g
        out_.append(next(before))
        return out_

    def turned_outputs(l, scope):
        yr = Ring([Slot(sbuf(f"y{l}_{i}", [P, 4, P], scope=scope)) for i in range(2)])
        res, used = [None] * 8, {}

        def dst(g):
            s_, free = yr.take()
            used[g] = s_
            return lambda i: s_.t[:, i, :].rearrange("p (h n) -> p h n", h=2), free

        def post(g0, z):
            kt = (g0 + 6) % 8
            b, free = RT.take()
            for c in range(4):
                g = tr(b.t[:, c * P:(c + 1) * P], used[g0].t[:, c, :], ident[:], z, free)
            used[g0].done(g)
            res[kt] = split_bank(b, g, hhi[:, kt, :], hlo[:, kt, :])
        return res, dst, post

    def out_product(l, yr):
        hs = []
        stat_begin()
        for m in range(8):
            b, h = fm_tile("wo", hhi, hlo, 8, T, yr)
            stat_sum()
            z = tt(xT[:, m, :], b.t[:], xT[:, m, :], ADD, h)
            b.done(z)
            stat_add(m, z)
            hs.append(z)
        xlast["h"] = hs
        q.barrier()

    def ffn(l, final, extra=None):
        hr = fm_norm("norm_ffn", 8 * l)
        table("silu_and_others")
        fs = ExitStack()
        ahi = sbuf(f"ahi{l}", [P, 11, T], F32R, scope=fs)
        alo = sbuf(f"alo{l}", [P, 11, T], F32R, scope=fs)
        cr = Ring([Slot(sbuf(f"cr{l}_{i}", [P, T], scope=fs)) for i in range(4)])
        ob = Ring([Slot(sbuf(f"ob{l}_{i}", [P, 4, P], scope=fs)) for i in range(2)]) if final else None
        if extra:
            extra(fs)
        dlast = None
        hs = [None] * 8

        def conv(b, h, ch):
            t, free = cr.take()
            cw = lambda j: col(f"cw{l}", 3 * ch + j)
            a = act(t.t[:], b.t[:], ACT.Identity, h, free, scale=cw(2), bias=col(f"cb{l}", ch))
            z = stt(t.t[:, 1:T], b.t[:, 0:T - 1], cw(1), t.t[:, 1:T], MUL, ADD, a)
            z = stt(t.t[:, 2:T], b.t[:, 0:T - 2], cw(0), t.t[:, 2:T], MUL, ADD, z)
            b.done(z)
            return t, z

        def gate(ct, tg, zg, tv, zv):
            a = act(tg.t[:], tg.t[:], ACT.Silu, zg)
            z = tt(tg.t[:], tg.t[:], tv.t[:], MUL, a, zv, eng="pool")
            tv.done(z)
            yield None
            a2 = acopy(ahi[:, ct, :], tg.t[:], z, dlast)
            z = tt(alo[:, ct, :], tg.t[:], ahi[:, ct, :].bitcast(F32), SUB, a2, eng="pool")
            tg.done(z)
            yield z

        store = []

        def put_out(m, z):
            b, free = RA.take()
            for c in range(4):
                g2 = tr(b.t[:, c * P:(c + 1) * P], xT[:, m, c * P:(c + 1) * P], ident[:], z, free)
            o, free = ob.take()
            z = evac(o.t[:], b.t[:].rearrange("p (c n) -> p c n", c=4), g2, free)
            b.done(z)
            dd = dma(out.rearrange("a (c p) n -> p (a c) n", p=P)[:, :, m * P:(m + 1) * P], o.t[:], s_out[m % 2], z)
            o.done(dd)
            last_out[m % 2] = dd

        fm_first(("up", "up"), hhi, hlo, 8, T, hr)
        for half_ in range(2):
            fin = []
            behind = None
            for ct in range(11):
                ch = 11 * half_ + ct
                b, h = fm_tile("up", hhi, hlo, 8, T, hr)
                if behind:
                    next(behind)
                tg, zg = conv(b, h, ch)
                b, h = fm_tile("up", hhi, hlo, 8, T, hr)
                if behind:
                    fin.append(next(behind))
                tv, zv = conv(b, h, 22 + ch)
                behind = gate(ct, tg, zg, tv, zv)
            next(behind)
            fin.append(next(behind))
            if half_ == 1 and not final:
                stat_begin()
            for m in range(8):
                w = weights("down")
                b, free = RA.take()
                for k in range(11):
                    g = mm3(b.t[:], w.hi[:, k, :], w.lo[:, k, :], ahi[:, k, :], alo[:, k, :], k == 0, k == 10,
                            w.rdy, free, fin[k])
                w.done(g)
                if half_ == 1 and not final:
                    stat_sum()
                z = tt(xT[:, m, :], b.t[:], xT[:, m, :], ADD, g, hs[m])
                b.done(z)
                hs[m] = z
                if half_ == 1 and not final:
                    stat_add(m, z)
                if final and half_ == 1:
                    store.append((m, z))
                if final and half_ == 1 and m > 0:
                    put_out(*store.pop(0))
            if store:
                put_out(*store.pop(0))
            dlast = g

        xlast["h"] = hs
        if not final:
            table("natural_log_exp_and_others")
        nhr = fm_norm("norm_mix", 8) if not final else None
        q.barrier()
        fs.close()
        return nhr

    last_out = [None, None]

    L0 = ExitStack()
    fqh, fql, fkh, fkl = [sbuf(n, [P, 6, T], F32R, scope=L0) for n in ("fqh", "fql", "fkh", "fkl")]
    fv = sbuf("fv", [P, 4, 768], scope=L0)
    mqT = sbuf("mqT", [P, 2, T], scope=L0)
    cum = sbuf("cum", [12, T], scope=L0)
    fpre = sbuf("fpre", [12, T], scope=L0)
    gs = sbuf("gs", [P, 4], scope=L0)
    zs = ts(gs[:, 0:1], col("fq"), 0.125, None, MUL, None, l_c)
    zs = ts(gs[:, 1:2], col("mq", 0), 0.125, None, MUL, None, l_c)
    fm_first(("ff", "fm"), hhi, hlo, 8, T, hr)
    b, h = fm_tile("ff", hhi, hlo, 8, T)
    a = act(fpre[:], b.t[0:12, :], ACT.Identity, h, l_c, bias=fb[:, 0:1])
    b.done(a)
    z = log_sigmoid(fpre[:], fpre[:], 12, T, a)
    zc = q.op("dve", lambda e: e.tensor_tensor_scan(cum[:], ones[0:12, 0:1].to_broadcast([12, T]), fpre[:], 0.0, MUL, ADD), (z,))
    cb = sbuf("cb", [P, T], BF16, scope=L0)
    cres = sbuf("cres", [12, T], scope=L0)
    selb = sbuf("selb", [P, 12], BF16, scope=L0)
    zm = mset(cb[:], 0.0, q.last())
    z = cp(cb[0:12, :], cum[:], zc, zm)
    z = tt(cres[:], cum[:], cb[0:12, :], SUB, z)
    z = cp(cb[32:44, :], cres[:], z)
    z = tt(cres[:], cres[:], cb[32:44, :], SUB, z)
    z_cb = cp(cb[64:76, :], cres[:], z)
    z = stt(selb[:], identb[:, 0:12], -1.0, identb[:, 32:44], MUL, SUB, C)
    z_sel = tt(selb[:], selb[:], identb[:, 64:76], SUB, z)

    fqk_ = head_normed_all([("fm", mqT[:, m, :], gs[:, 1:2]) for m in range(2)]
                           + [("fqk", (fqh[:, m, :], fql[:, m, :]), gs[:, 0:1], hr, zs) for m in range(6)]
                           + [("fqk", (fkh[:, m, :], fkl[:, m, :]), col("fk")) for m in range(6)])
    mq_, fqk_ = fqk_[0:2], fqk_[2:]
    fq_, fk_ = fqk_[0:6], fqk_[6:12]
    fv_ = {}
    for g0 in (0, 384):
        for c, (b, h) in enumerate(tm_group("fv", hhi, hlo, 4, 384)):
            z = evac(fv[:, c, g0:g0 + 384], b.t[:, 0:384], h)
            b.done(z)
            fv_[c, g0 // 384] = z
    def fox_h(h):
        hf, m = half(h), h // 2
        return Head(lambda i: (fqh[hf, m, i * P:(i + 1) * P], fq_[m]),
                    lambda n: (fkh[hf, m, 0:n], fk_[m]),
                    lambda j: (fv[:, j, h * 64:(h + 1) * 64], fv_[j, h // 6]),
                    lambda i: P * (i + 1), True,
                    low=lambda i, n: (fql[hf, m, i * P:(i + 1) * P], fkl[hf, m, 0:n]),
                    add=lambda n: (selb[0:76, h:h + 1].to_broadcast([76, P]), cb[0:76, 0:n], z_cb, z_sel))

    def mem_heads(l, mqT, mq_):
        kg = ts(kmg[:], kmn[:], col("mk", l), None, MUL, None, l_c)
        return [Head(lambda i, h=h: (mqT[half(h), h // 2, i * P:(i + 1) * P], mq_[h // 2]),
                     lambda n, h=h: (kmg[half(h), h // 2, :], kg),
                     lambda j, h=h: (vmem[:, j, h * 64:(h + 1) * 64], None),
                     lambda i: 256) for h in range(4)]

    yr, dst, post = turned_outputs(0, L0)
    sc, _ = attention("fox", mem_heads(0, mqT, mq_) + [fox_h(h) for h in range(12)], dst, post)
    out_product(0, yr)
    sc.close()
    L0.close()

    def rope_tables(fs):
        pi_ = sbuf("posi", [P, 4], I32, scope=fs)
        pf = sbuf("posf", [P, 4], scope=fs)
        iv = sbuf("ivf", [P, 16], scope=fs)
        an = sbuf("ang", [P, 4, 16], scope=fs)
        kk = sbuf("kk", [P, 4, 16], scope=fs)
        r_ = sbuf("rr", [P, 2, 4, 16], scope=fs)
        l_p = dma(pi_[:], d["pos"], s_u, q.last())
        inv = np.float32(10000.0) ** (-np.arange(0, 32, 2, dtype=np.float32) / np.float32(32))
        for j in range(16):
            m = mset(iv[:, j:j + 1], float(np.float32(inv[j])))
        z = cp(pf[:], pi_[:], l_p)
        z = tt(an[:], pf[:].unsqueeze(2).to_broadcast([P, 4, 16]), iv[:].unsqueeze(1).to_broadcast([P, 4, 16]),
               MUL, z, m)
        magic = 12582912.0
        c1 = 6.28125
        c2 = float(np.float32(2 * np.pi - 6.28125) // np.float32(2 ** -20) * 2 ** -20)
        c3 = float(2 * np.pi - 6.28125 - c2)
        lim = 3.1415925
        zz = z
        for w, (quarter, shift, dst_) in enumerate(((0.0, 0.0, sinT), (0.25, float(np.pi / 2), cosT))):
            z = ts(kk[:], an[:], float(1 / (2 * np.pi)), quarter, MUL, ADD, zz)
            z = ts(kk[:], kk[:], magic, None, ADD, None, z)
            z = ts(kk[:], kk[:], -magic, None, ADD, None, z)
            z = stt(r_[:, w], kk[:], -c1, an[:], MUL, ADD, z)
            z = stt(r_[:, w], kk[:], -c2, r_[:, w], MUL, ADD, z)
            z = stt(r_[:, w], kk[:], -c3, r_[:, w], MUL, ADD, z)
            z = ts(r_[:, w], r_[:, w], shift, lim, ADD, MIN, z)
            z = ts(r_[:, w], r_[:, w], -lim, None, MAX, None, z)
            a = act(dst_[:], r_[:, w], ACT.Sin, z)
            zz = [zz, z]
        rope_ok.append(a)

    rope_ok = []
    hr = ffn(0, False, rope_tables)

    L1 = ExitStack()
    grp = [Slot((sbuf(f"qt{i}", [P, 4, 4, 96], scope=L1), sbuf(f"kt{i}", [P, 4, 4, 96], scope=L1)))
           for i in range(2)]
    vts = [sbuf(f"vt{i}", [P, 4, 4, 64], scope=L1) for i in range(3)]
    mqT1 = sbuf("mqT1", [P, 2, T], scope=L1)
    gs1 = sbuf("gs1", [P, 1], scope=L1)
    gq96 = sbuf("gq96", [96, 2], scope=L1)
    l_q = dma(gq96[:, 0:1], d["mla_q_gain_2"].rearrange("a n -> n a"), s_u, q.last())
    l_q = dma(gq96[:, 1:2], d["mla_k_gain_2"].rearrange("a n -> n a"), s_u)
    lhi = sbuf("lhi", [P, 3, T], F32R, scope=L1)
    llo = sbuf("llo", [P, 3, T], F32R, scope=L1)
    krr = sbuf("krr", [P, 4, 32], scope=L1)
    krt = sbuf("krt", [P, 4, 4, 16], scope=L1)
    zs = ts(gs1[:], col("mq", 1), 0.125, None, MUL, None, l_c)
    zg = ts(gq96[:, 0:1], gq96[:, 0:1], 96 ** -0.5, None, MUL, None, l_q)

    def latent(tiles, key, n, gname, base, dep=None):
        bs = []
        b2, f2 = RO.take()
        for m in range(tiles):
            b, h = fm_tile(key, hhi, hlo, 8, T, dep, RS)
            t, free = tmp.take()
            a = act(t.t[:], b.t[:], ACT.Square, h, free)
            g = mm(b2.t[:], ones[:], t.t[:], m == 0, m == tiles - 1, a, f2)
            t.done(g)
            bs.append(b)
        rb, free = hold.take()
        a = rstd_of(rb.t[:], b2.t[:], n, g, free)
        b2.done(a)
        zl = []
        for m in range(tiles):
            t, free = tmp.take()
            z = stt(t.t[:], bs[m].t[:], col(gname, m), rb.t[:], MUL, MUL, a, free)
            bs[m].done(z)
            a2 = acopy(lhi[:, base + m, :], t.t[:], z)
            z = tt(llo[:, base + m, :], t.t[:], lhi[:, base + m, :].bitcast(F32), SUB, a2)
            t.done(z)
            zl.append(z)
        rb.done(zl[-1])
        return zl

    fm_first(("ql", "ql"), hhi, hlo, 8, T, hr, RS)
    ql_ = latent(2, "ql", 256, "qa", 0, hr)
    kvl_ = latent(1, "kvl", 128, "kva", 2)
    w = weights("kr")
    b, free = RA.take()
    for k in range(8):
        g = mm3(b.t[0:32, :], w.hi[:, k, :], w.lo[:, k, :], hhi[:, k, :], hlo[:, k, :], k == 0, k == 7, w.rdy, free)
    w.done(g)
    t, free = tmp.take()
    z = cp(t.t[0:32, :], b.t[0:32, :], g, free)
    b.done(z)
    b, free = RA.take()
    for c in range(4):
        g = tr(b.t[:, c * 32:(c + 1) * 32], t.t[0:32, c * P:(c + 1) * P], ident[0:32, 0:32], z, free)
    t.done(g)
    z_kr = cp(krr[:].rearrange("p c n -> p (c n)"), b.t[:, 0:P], g)
    b.done(z_kr)
    mq_ = head_normed_all([("mm", mqT1[:, m, :], gs1[:, 0:1], None, zs) for m in range(2)])

    def rope(x1, x2, cc, ss, t4, *deps, eng="dve"):
        z1_ = tt(t4[0], x1, cc, MUL, *deps, eng=eng)
        z2_ = tt(t4[1], x2, ss, MUL, eng=eng)
        z3_ = tt(t4[2], x1, ss, MUL, eng=eng)
        z4_ = tt(t4[3], x2, cc, MUL, eng=eng)
        z5_ = tt(x1, t4[0], t4[1], SUB, z1_, z2_, z3_, eng=eng)
        return tt(x2, t4[2], t4[3], ADD, z3_, z4_, z5_, eng=eng)

    zk_ = rope(krr[:, :, 0:16], krr[:, :, 16:32], cosT[:], sinT[:], [krt[:, i] for i in range(4)], z_kr, rope_ok)
    sqb = sbuf("sqb", [P, 4, 4, 96], scope=L1)
    r4 = [sbuf(f"r4{i}", [P, 4, 4, 16], scope=L1) for i in range(4)]
    r16 = sbuf("r16", [P, 6, 16], scope=L1)
    GR = {}

    def mla_group(j, ring):
        st_ = {}
        cb_ = cosT[:].unsqueeze(2).to_broadcast([P, 4, 4, 16])
        sb_ = sinT[:].unsqueeze(2).to_broadcast([P, 4, 4, 16])
        vt = vts[j]
        rq, rk = r16[:, 2 * j, :], r16[:, 2 * j + 1, :]

        def begin():
            s_ = grp[j % 2]
            st_["free"] = s_.take()
            st_["q"], st_["k"] = s_.t
            st_["zr"] = cp(s_.t[1][:, :, :, 64:96], krr[:].unsqueeze(2).to_broadcast([P, 4, 4, 32]), zk_,
                           st_["free"], eng="pool")
            st_["qz"], st_["kz"] = [], []
            GR[j] = [s_, [], st_["kz"]]

        def q_tile(c):
            if c == 0:
                begin()
                st_["w"] = weights("qup")
            w = st_["w"]
            b, free = ring.take()
            for k in range(2):
                g = mm3(b.t[:, 0:384], lhi[:, k, c * P:(c + 1) * P], llo[:, k, c * P:(c + 1) * P],
                        w.hi[:, k, :], w.lo[:, k, :], k == 0, k == 1, w.rdy, free, ql_)
            z = evac(st_["q"][:, c], b.t[:, 0:384].rearrange("p (h n) -> p h n", h=4), g, st_["free"])
            b.done(z)
            st_["qz"].append(z)
            if c == 3:
                w.done(g)

        def kv_tile(c):
            if c == 0:
                st_["w"] = weights("kvup")
            w = st_["w"]
            b, free = ring.take()
            g = mm3(b.t[:], lhi[:, 2, c * P:(c + 1) * P], llo[:, 2, c * P:(c + 1) * P],
                    w.hi[:, 0, :], w.lo[:, 0, :], True, True, w.rdy, free, kvl_)
            bv = b.t[:].rearrange("p (h n) -> p h n", h=4)
            a = acopy(st_["k"][:, c, :, 0:64], bv[:, :, 0:64], g, st_["free"])
            z = cp(vt[:, c], bv[:, :, 64:128], a, st_["free"])
            b.done(z)
            st_["kz"] += [a, z]
            if c == 3:
                w.done(g)

        def turn_1():
            x1, x2 = st_["q"][:, :, :, 64:80], st_["q"][:, :, :, 80:96]
            st_["a"] = [tt(r4[0][:], x1, cb_, MUL, st_["qz"], rope_ok, q.end["dve"]), tt(r4[1][:], x2, sb_, MUL)]

        def turn_2():
            x1, x2 = st_["q"][:, :, :, 64:80], st_["q"][:, :, :, 80:96]
            st_["a"] += [tt(r4[2][:], x1, sb_, MUL), tt(r4[3][:], x2, cb_, MUL)]

        def turn_3():
            x1, x2 = st_["q"][:, :, :, 64:80], st_["q"][:, :, :, 80:96]
            z = tt(x1, r4[0][:], r4[1][:], SUB, st_["a"])
            st_["qr"] = [z, tt(x2, r4[2][:], r4[3][:], ADD, st_["a"])]

        def square(x, *deps):
            st_["sq"] = act(sqb[:], x[:], ACT.Square, deps, q.end["dve"])

        def sums(rr):
            st_["sum"] = red(rr, sqb[:].rearrange("p c h n -> p (c h) n"), ADD, st_["sq"])

        def scale(x, rr):
            sr = x[:].rearrange("p c h n -> p (c h) n")
            a = rstd_of(rr, rr, 96, st_["sum"])
            GR[j][1].append(tt(sr, sr, rr.unsqueeze(2).to_broadcast([P, 16, 96]), MUL, a, eng="pool"))

        return [lambda: q_tile(0), lambda: q_tile(1), lambda: q_tile(2), lambda: q_tile(3),
                lambda: (kv_tile(0), turn_1()), lambda: (kv_tile(1), turn_2()), lambda: (kv_tile(2), turn_3()),
                lambda: (kv_tile(3), square(st_["q"], st_["qr"])),
                lambda: sums(rq), lambda: (scale(st_["q"], rq), square(st_["k"], st_["kz"], st_["zr"])),
                lambda: sums(rk), lambda: scale(st_["k"], rk)]

    qh_r = Ring([Slot(sbuf(f"qh{i}", [96, T], scope=L1)) for i in range(2)])
    kh_r = Ring([Slot(sbuf(f"kh{i}", [96, T], scope=L1)) for i in range(2)])
    QK = {}

    steps = mla_group(0, RA)
    for f in steps[0:8]:
        f()
    side_ = {t - 1: f for t, f in enumerate(steps[8:])}
    side_.update({12 + t: f for t, f in enumerate(mla_group(1, RT))})
    side_[26] = lambda: GR[0][0].done(q.end["pe"])
    side_.update({27 + t: f for t, f in enumerate(mla_group(2, RT))})

    def side(t):
        if t in side_:
            side_[t]()

    def mla_start(h):
        if h >= 2:
            QK[h - 2][0].done(q.end["pe"])
            QK[h - 2][2].done(q.end["pe"])
        s_, nz = GR[h // 4][0:2]
        outs = []
        for src, ring, gi in ((s_.t[0], qh_r, 0), (s_.t[1], kh_r, 1)):
            b, free = RT.take()
            for c in range(4):
                g = tr(b.t[0:96, c * P:(c + 1) * P], src[:, c, h % 4, :], ident[:], free, nz)
            o_, f2 = ring.take()
            a = act(o_.t[:], b.t[0:96, :], ACT.Identity, g, f2, zg, l_q, scale=gq96[:, gi:gi + 1])
            b.done(a)
            outs += [o_, a]
        QK[h] = outs

    def mla_h(h):
        return Head(lambda i: (QK[h][0].t[:, i * P:(i + 1) * P], QK[h][1]),
                    lambda n: (QK[h][2].t[:, 0:n], QK[h][3]),
                    lambda j: (vts[h // 4][:, j, h % 4, :], GR[h // 4][2]),
                    lambda i: P * (i + 1), True, prep=lambda: mla_start(h))

    yr, dst, post = turned_outputs(1, L1)
    sc, _ = attention("mla", mem_heads(1, mqT1, mq_) + [mla_h(h) for h in range(12)], dst, post, side)
    out_product(1, yr)
    sc.close()
    L1.close()
    ffn(1, True)
    assert state["next"] == len(chunks)

    q.number()
    with nc.Block() as block:
        @block.sync
        def _(e):
            q.emit("sp", e, sems)
            for _, s, n in last_out:
                e.wait_ge(s, n)

        @block.scalar
        def _(e):
            q.emit("act", e, sems)

        @block.vector
        def _(e):
            q.emit("dve", e, sems)

        @block.gpsimd
        def _(e):
            q.emit("pool", e, sems)

        @block.tensor
        def _(e):
            q.emit("pe", e, sems)
    ctx.close()


def lay_out(inputs):
    a = {k: np.asarray(v) for k, v in inputs.items()}
    parts = []
    for _, name, l, k0, kt, c0, n in plan_chunks():
        w = a[name] if l is None else a[name][l]
        parts.append(w[k0:k0 + kt * P, c0:c0 + n].reshape(kt, P, n).transpose(1, 0, 2).reshape(-1))
    vec = np.zeros((P, NVEC), np.float32)

    def put(name, m):
        c, n = VECS[name]
        vec[:, c:c + n] = m

    put("norm_g", a["norm_g"][0].reshape(8, P).T)
    put("conv_w", a["conv_w"][0].reshape(4, 6, P).transpose(2, 1, 0).reshape(P, 24))
    put("norm_mix", a["norm_mix_2"].reshape(16, P).T)
    put("norm_ffn", a["norm_ffn_2"].reshape(16, P).T)
    put("mem_norm", a["mem_norm_2"].reshape(8, P).T)
    put("qa", a["mla_qa_norm_2"][0].reshape(2, P).T)
    put("kva", a["mla_kva_norm_2"].reshape(1, P).T)
    put("b_alpha", a["b_alpha"].reshape(1, P).T)
    put("fq", np.tile(a["fox_q_gain_2"][0], 2)[:, None])
    put("fk", np.tile(a["fox_k_gain_2"][0], 2)[:, None])
    put("mq", np.tile(a["mem_q_gain_2"], (1, 2)).T)
    put("mk", np.tile(a["mem_k_gain_2"], (1, 2)).T)
    for l in range(2):
        put(f"cw{l}", a["ffn_conv_w_2"][l].reshape(3, 44, P).transpose(2, 1, 0).reshape(P, 132))
        put(f"cb{l}", a["ffn_conv_b_2"][l].reshape(44, P).T)
    rel = a["rel_bias"][0]
    out = {"pos": a["positions_2"].reshape(4, P).T, "wts": np.concatenate(parts), "vecs": vec,
           "rel_ext": np.concatenate([rel, np.repeat(rel[:, 256:257], 640 - 257, axis=1)], axis=1)}
    for k in ("x", "mem_2", "fox_b_f_2", "b_gates", "ml_norm_g", "gla_norm_g", "w_alpha", "final_g",
              "mla_q_gain_2", "mla_k_gain_2"):
        out[k] = a[k]
    return {k: np.ascontiguousarray(v) for k, v in out.items()}


def kernel(**inputs):
    import concourse.bacc as bacc
    from concourse.bass_utils import run_bass_kernel_spmd

    nc = bacc.Bacc("TRN2", target_bir_lowering=False, num_devices=1)
    arrays = lay_out(inputs)
    d = {k: nc.dram_tensor(f"in_{k}", v.shape, mybir.dt.from_np(v.dtype), kind="ExternalInput").ap()
         for k, v in arrays.items()}
    out = nc.dram_tensor("out_0", (1, T, D), F32, kind="ExternalOutput").ap()
    build(nc, d, out)
    r = run_bass_kernel_spmd(nc, [{f"in_{k}": v for k, v in arrays.items()}], core_ids=[0])
    return r.results[0]["out_0"]
```

```python
from contextlib import ExitStack

import numpy as np
import concourse.bass as bass
from concourse import mybir

F32 = mybir.dt.float32
F32R = mybir.dt.float32r
BF16 = mybir.dt.bfloat16
I32 = mybir.dt.int32
ALU = mybir.AluOpType
ACT = mybir.ActivationFunctionType
AX = mybir.AxisListType.X
P = 128
T = 512
D = 1024
EPS = 1e-6
NEG = -1e30
FF = 2816
CAP = 1536


def plan_chunks():
    out = []

    def fm(key, name, l, kt, c0, cols):
        for c in range(c0, c0 + cols, P):
            out.append((key, name, l, 0, kt, c, P))

    def tm(key, name, l, c0, cols, step=384):
        for c in range(c0, c0 + cols, step):
            n = min(step, c0 + cols - c)
            for half in range(2):
                out.append((key, name, l, half * 512, 4, c, n))

    fm("memk", "w_mem_kv_2", None, 8, 0, 256)
    tm("memv", "w_mem_kv_2", None, 256, 256)
    fm("aq", "w_in", 0, 8, 0, 384)
    fm("ak", "w_in", 0, 8, 384, 384)
    tm("ag", "w_in", 0, 1152, 384)
    tm("av", "w_in", 0, 768, 384)
    out.append(("gate", "gates", None, 0, 8, 0, 48))
    tm("mo", "w_in", 0, 2688, 384)
    fm("mqk", "w_in", 0, 8, 1536, 768)
    tm("mg", "w_in", 0, 3084, 384)
    tm("mv", "w_in", 0, 2304, 384)
    tm("gg", "w_in", 0, 3996, 256)
    fm("gqk", "w_in", 0, 8, 3468, 256)
    tm("gv", "w_in", 0, 3724, 256)
    tm("wo1", "w_out", 0, 0, 1024)

    def tail(l):
        fm("wo", "w_out_2", l, 8, 0, 1024)
        for half in range(2):
            for ct in range(11):
                c = (11 * half + ct) * P
                fm("up", "ffn_w_up_2", l, 8, c, P)
                fm("up", "ffn_w_up_2", l, 8, FF + c, P)
            for m in range(8):
                out.append(("down", "ffn_w_down_2", l, half * 1408, 11, m * P, P))

    fm("ff", "fox_w_in_2", 0, 8, 2304, 128)
    fm("fm", "fox_w_in_2", 0, 8, 2316, 256)
    fm("fqk", "fox_w_in_2", 0, 8, 0, 1536)
    tm("fv", "fox_w_in_2", 0, 1536, 768)
    tail(0)
    fm("ql", "mla_w_in_2", 0, 8, 0, 256)
    fm("kvl", "mla_w_in_2", 0, 8, 256, 128)
    out.append(("kr", "mla_w_in_2", 0, 0, 8, 384, 32))
    fm("mm", "mla_w_in_2", 0, 8, 416, 256)
    for j in range(3):
        out.append(("qup", "mla_w_q_up_2", 0, 0, 2, 384 * j, 384))
        out.append(("kvup", "mla_w_kv_up_2", 0, 0, 1, 512 * j, 512))
    tail(1)
    return out


VECS = {}


def _vecs():
    at = 0
    for name, n in (("norm_g", 8), ("conv_w", 24), ("norm_mix", 16), ("norm_ffn", 16), ("mem_norm", 8),
                    ("qa", 2), ("kva", 1), ("b_alpha", 1), ("fq", 1), ("fk", 1), ("mq", 2), ("mk", 2),
                    ("cw0", 132), ("cb0", 44), ("cw1", 132), ("cb1", 44)):
        VECS[name] = (at, n)
        at += n
    return at


NVEC = _vecs()


class Handle:
    __slots__ = ("eng", "used", "val")

    def __init__(self, eng):
        self.eng, self.used, self.val = eng, False, 0


class Queues:

    ENG = ("pe", "act", "dve", "pool", "sp")

    def __init__(self):
        self.q = {e: [] for e in self.ENG}
        self.held = {e: [] for e in self.ENG}
        self.end = {}

    def op(self, eng, fn, deps):
        h = Handle(eng)
        flat = list(self.held[eng])
        self.held[eng] = []
        stack = list(deps)
        while stack:
            d = stack.pop()
            if d is None:
                continue
            if isinstance(d, (list, tuple)) and not (len(d) == 3 and d[0] == "dma"):
                stack.extend(d)
                continue
            if isinstance(d, Handle):
                d.used = True
            flat.append(d)
        if eng == "pool" and self.q[eng]:
            self.q[eng][-1][2].used = True
            flat.append(self.q[eng][-1][2])
        self.q[eng].append((fn, flat, h))
        self.end[eng] = h
        return h

    def last(self):
        return [self.end[e] for e in ("pe", "act", "dve", "pool") if e in self.end]

    def barrier(self):
        now = self.last()
        for h in now:
            h.used = True
        for e in ("act", "dve", "pool"):
            self.held[e] = self.held[e] + now
        return now

    def number(self):
        for e in self.ENG:
            n = 0
            for _, _, h in self.q[e]:
                if h.used:
                    n += 1
                    h.val = n

    def emit(self, eng, e, sems):
        seen = {}
        for fn, deps, h in self.q[eng]:
            need = {}
            for d in deps:
                s, v = (sems[d.eng], d.val) if isinstance(d, Handle) else (d[1], d[2])
                k = id(s)
                if v > seen.get(k, 0) and v > need.get(k, (None, 0))[1]:
                    need[k] = (s, v)
            for k, (s, v) in need.items():
                e.wait_ge(s, v)
                seen[k] = v
            ins = fn(e)
            if h.used:
                ins.then_inc(sems[eng], 1)


class Slot:

    def __init__(self, t):
        self.t, self.free = t, []

    def take(self):
        f, self.free = self.free, None
        assert f is not None, "slot in use"
        return f

    def done(self, *hs):
        self.free = list(hs)


class Ring:
    def __init__(self, slots):
        self.s, self.i = slots, 0

    def take(self):
        s = self.s[self.i % len(self.s)]
        self.i += 1
        return s, s.take()


def build(nc, d, out):
    q = Queues()
    ctx = ExitStack()
    chunks = plan_chunks()

    def sem(n):
        return ctx.enter_context(nc.semaphore(n))

    def sbuf(name, shape, dt=F32, scope=None):
        return (scope or ctx).enter_context(nc.sbuf_tensor(name, shape, dt))

    sems = {e: sem("s_" + e) for e in Queues.ENG}

    def mm(o, lhsT, rhs, start, stop, *deps):
        return q.op("pe", lambda e: e.matmul(o, lhsT, rhs, start=start, stop=stop), deps)

    def mmx(o, lhsT, rhs, start, stop, *deps):
        return q.op("pe", lambda e: e.matmul(o, lhsT, rhs, start=start, stop=stop, skip_group_check=True), deps)

    def tr(o, i, ident, *deps):
        return q.op("pe", lambda e: e.transpose(o, i, ident), deps)

    def act(o, i, f, *deps, bias=0.0, scale=1.0, acc=None):
        if acc is None:
            return q.op("act", lambda e: e.activation(o, i, f, bias=bias, scale=scale), deps)
        return q.op("act", lambda e: e.activation(o, i, f, bias=bias, scale=scale, accum_out=acc), deps)

    def acopy(o, i, *deps):
        return q.op("act", lambda e: e.copy(o, i), deps)

    def tt(o, a, b, op, *deps, eng="dve"):
        return q.op(eng, lambda e: e.tensor_tensor(o, a, b, op), deps)

    def ts(o, a, s1, s2, op0, op1, *deps, eng="dve"):
        if op1 is None:
            return q.op(eng, lambda e: e.tensor_scalar(o, a, s1, None, op0), deps)
        return q.op(eng, lambda e: e.tensor_scalar(o, a, s1, s2, op0, op1), deps)

    def stt(o, a, s, b, op0, op1, *deps, eng="dve"):
        return q.op(eng, lambda e: e.scalar_tensor_tensor(out=o, in0=a, scalar=s, in1=b, op0=op0, op1=op1), deps)

    def cp(o, i, *deps, eng="dve"):
        return q.op(eng, lambda e: e.tensor_copy(o, i), deps)

    def recip(o, i, *deps):
        return q.op("dve", lambda e: e.reciprocal(o, i), deps)

    def red(o, i, op, *deps, negate=None):
        return q.op("dve", lambda e: e.tensor_reduce(o, i, AX, op, negate=negate), deps)

    def mset(ap, v, *deps, eng="pool"):
        return q.op(eng, lambda e: e.memset(ap, v), deps)

    def sel(ap, pattern, cmp, fill, base, cm, *deps):
        return q.op("pool", lambda e: e.affine_select(out=ap, in_=ap, pattern=pattern, compare_op=cmp, fill=fill,
                                                       base=base, channel_multiplier=cm), deps)

    dcount = {}

    def dma(o, i, s, *deps):
        n = dcount[id(s)] = dcount.get(id(s), 0) + 16
        q.op("sp", lambda e: e.dma_start(o, i).then_inc(s, 16), deps)
        return ("dma", s, n)

    def table(name):
        end = q.end.get("act")
        q.op("act", lambda e: e.preload_act_table_set(name), ())
        if end is not None:
            q.end["act"] = end

    MUL, ADD, SUB, MAX, MIN = ALU.mult, ALU.add, ALU.subtract, ALU.max, ALU.min

    banks = [Slot(ctx.enter_context(nc.psum_tensor(f"bank{i}", [P, 512], F32))) for i in range(8)]
    RA = Ring(banks[0:7])
    stat = banks[7]
    RS, RT, RO = Ring(banks[0:4]), Ring(banks[4:6]), Ring(banks[6:8])

    ident = sbuf("ident", [P, P])
    identb = sbuf("identb", [P, P], BF16)
    maskb = sbuf("maskb", [P, P], BF16)
    ones = sbuf("ones", [P, P])
    blk = sbuf("blk", [P, P])
    onesr = sbuf("onesr", [P, P], F32R)
    blkr = sbuf("blkr", [P, P], F32R)
    epsc = sbuf("epsc", [P, 1])
    vc = sbuf("vc", [P, NVEC])
    small = sbuf("small", [P, 256])
    stage = [Slot(sbuf(f"wstage{i}", [P, CAP])) for i in range(3)]
    whi = [Slot(sbuf(f"whi{i}", [P, CAP], F32R)) for i in range(3)]
    wlo = [Slot(sbuf(f"wlo{i}", [P, CAP], F32R)) for i in range(3)]
    RST, RHI, RLO = Ring(stage), Ring(whi), Ring(wlo)
    hhi = sbuf("hhi", [P, 8, T], F32R)
    hlo = sbuf("hlo", [P, 8, T], F32R)
    xT = sbuf("xT", [P, 8, T])
    tmp = Ring([Slot(sbuf(f"tmp{i}", [P, T])) for i in range(5)])
    hold = Ring([Slot(sbuf(f"hold{i}", [P, T])) for i in range(1)])
    kmn = sbuf("kmn", [P, 2, 256])
    kmg = sbuf("kmg", [P, 2, 256])
    vmem = sbuf("vmem", [P, 2, 256])
    fb = sbuf("fb", [12, 1])
    sinT = sbuf("sinT", [P, 4, 16])
    cosT = sbuf("cosT", [P, 4, 16])

    s_stage = [sem(f"s_w{i}") for i in range(3)]
    s_c, s_u = sem("s_c"), sem("s_u")
    s_x = [sem(f"s_x{c}") for c in range(4)]
    s_mem = [sem("s_mem0"), sem("s_mem1")]
    s_out = [sem("s_out0"), sem("s_out1")]

    def col(name, i=0, n=P):
        a = VECS[name][0] + i
        return vc[0:n, a:a + 1]

    mscope = ExitStack()
    xt = sbuf("xt", [P, 4, D], scope=mscope)
    yt = xT[:].rearrange("p a b -> p (a b)").rearrange("p (c n) -> p c n", c=4)
    bT = sbuf("bT", [P, T], scope=mscope)
    iscope = ExitStack()
    memt = sbuf("memt", [P, 2, D], scope=iscope)
    l_mem = [dma(memt[:, c, :], d["mem_2"].rearrange("a (c p) n -> p (a c) n", p=P)[:, c, :], s_mem[c])
             for c in range(2)]
    l_vc = dma(vc[:], d["vecs"], s_c)
    l_fb = dma(fb[:], d["fox_b_f_2"].rearrange("a n -> n a"), s_c)
    l_c = l_fb

    offs, at = [], 0
    for (_, _, _, _, kt, _, n) in chunks:
        offs.append(at)
        at += P * kt * n

    class W:
        pass

    state = {"next": 0, "loaded": 0, "split": 0}
    staged, ready = {}, {}

    def load(i):
        _, _, _, _, kt, _, n = chunks[i]
        w = kt * n
        s, free = RST.take()
        k = (RST.i - 1) % 3
        src = d["wts"][offs[i]:offs[i] + P * w].rearrange("(p w) -> p w", p=P)
        staged[i] = (s, dma(s.t[:, 0:w], src, s_stage[k], free))

    def split(i):
        _, _, _, _, kt, _, n = chunks[i]
        w = kt * n
        s, l = staged.pop(i)
        hi, f1 = RHI.take()
        lo, f2 = RLO.take()
        a = acopy(hi.t[:, 0:w], s.t[:, 0:w], l, f1)
        b = tt(lo.t[:, 0:w], s.t[:, 0:w], hi.t[:, 0:w].bitcast(F32), SUB, a, f2)
        s.done(b)
        o = W()
        o.hi = hi.t[:, 0:w].rearrange("p (k n) -> p k n", k=kt)
        o.lo = lo.t[:, 0:w].rearrange("p (k n) -> p k n", k=kt)
        o.rdy = b
        o.done = lambda h: (hi.done(h), lo.done(h))
        ready[i] = o

    def ahead(i):
        while True:
            n = state["split"]
            if state["loaded"] < min(len(chunks), n + 3):
                load(state["loaded"])
                state["loaded"] += 1
            elif n < len(chunks) and n <= i + 2 and RHI.s[RHI.i % len(RHI.s)].free is not None:
                split(n)
                state["split"] += 1
            else:
                return

    def weights(key):
        i = state["next"]
        state["next"] += 1
        assert chunks[i][0] == key, (chunks[i], key)
        ahead(i)
        return ready.pop(i)

    def load_next():
        load(state["loaded"])
        state["loaded"] += 1

    for _ in range(3):
        load_next()
    l_x = [dma(xt[:, c, :], d["x"].rearrange("a (c p) n -> p (a c) n", p=P)[:, c, :], s_x[c]) for c in range(4)]

    table("natural_log_exp_and_others")
    c0 = mset(ident[:], 0.0)
    c_id = sel(ident[:], [[-1, P]], ALU.not_equal, 1.0, 0, 1, c0)
    c1 = mset(identb[:], 0.0)
    c_idb = sel(identb[:], [[-1, P]], ALU.not_equal, 1.0, 0, 1, c1)
    c2 = mset(maskb[:], 0.0)
    c_mk = sel(maskb[:], [[-1, P]], ALU.is_ge, NEG, 0, 1, c2)
    c_1 = mset(ones[:], 1.0)
    c3 = mset(blk[:], 0.0)
    c4 = mset(blk[0:64, 0:64], 1.0, c3)
    c5 = mset(blk[64:128, 64:128], 1.0, c3)
    c_e = mset(epsc[:], EPS)
    C = [c_id, c_idb, c_mk, c_1, c4, c5, c_e]

    c_r = [cp(onesr[:], ones[:], c_1), cp(blkr[:], blk[:], c4, c5)]

    sq_ring = {"now": None}

    def part_ring(name, n, scope, *free):
        sq_ring["now"] = r = Ring([Slot([sbuf(f"{name}{i}{p}", [P, T], F32R, scope=scope) for p in "hl"])
                                   for i in range(n)])
        for s_ in r.s:
            s_.done(*free)

    def squares(src, *deps, whole=False):
        t, f1 = tmp.take()
        a = act(t.t[:], src, ACT.Square, *deps, f1)
        if whole or sq_ring["now"] is None:
            return t, a
        pr, f2 = sq_ring["now"].take()
        a = acopy(pr.t[0][:], t.t[:], a, f2)
        z = tt(pr.t[1][:], t.t[:], pr.t[0][:].bitcast(F32), SUB, a, eng="pool")
        t.done(z)
        return pr, z

    def sum_parts(o, pair, parts, start, stop, *deps):
        s_, z = parts
        if type(s_.t) is not list:
            g = mm(o, pair[0][:], s_.t[:], start, stop, z, *deps)
        else:
            mm(o, pair[1][:], s_.t[0][:], start, False, z, c_r, *deps)
            g = mm(o, pair[1][:], s_.t[1][:], False, stop)
        s_.done(g)
        return g

    def mm3(o, lh, ll, rh, rl, start, stop, *deps):
        mm(o, lh, rh, start, False, *deps)
        mm(o, lh, rl, False, False)
        return mm(o, ll, rh, False, stop)

    def at(dep, k):
        return dep[k] if isinstance(dep, list) else dep

    def fm_tile(key, xh, xl, kt, n, dep=None, ring=None, rows=P):
        if early:
            return early.pop(0)
        w = weights(key)
        b, free = (ring or RA).take()
        for k in range(kt):
            h = mm3(b.t[0:rows, 0:n], w.hi[:, k, :], w.lo[:, k, :], xh[:, k, 0:n], xl[:, k, 0:n],
                    k == 0, k == kt - 1, w.rdy, free, at(dep, k))
        w.done(h)
        return b, h

    early = []

    def fm_first(keys, xh, xl, kt, n, dep, ring=None):
        w2 = [weights(key) for key in keys]
        bs = [(ring or RA).take() for _ in w2]
        for k in range(kt):
            for w, (b, free) in zip(w2, bs):
                z_hi, z_lo = at(dep, k)
                o = b.t[:, 0:n]
                mm(o, w.hi[:, k, :], xh[:, k, 0:n], k == 0, False, w.rdy, free, z_hi)
                mm(o, w.lo[:, k, :], xh[:, k, 0:n], False, False)
                h = mm(o, w.hi[:, k, :], xl[:, k, 0:n], False, k == kt - 1, z_lo)
                if k == kt - 1:
                    w.done(h)
                    early.append((b, h))

    def tm_group(key, xh, xl, tiles, cols, dep=None, mid=None):
        w, bs = weights(key), []
        for c in range(tiles):
            b, free = RA.take()
            bs.append(b)
            for k in range(4):
                g = mm3(b.t[:, 0:cols], xh[:, k, c * P:(c + 1) * P], xl[:, k, c * P:(c + 1) * P],
                        w.hi[:, k, :], w.lo[:, k, :], k == 0, False, w.rdy, free, at(dep, k))
        w.done(g)
        if mid:
            mid()
        w = weights(key)
        for c, b in enumerate(bs):
            for k in range(4):
                g = mm3(b.t[:, 0:cols], xh[:, k + 4, c * P:(c + 1) * P], xl[:, k + 4, c * P:(c + 1) * P],
                        w.hi[:, k, :], w.lo[:, k, :], False, k == 3, w.rdy, at(dep, k + 4))
            if c == tiles - 1:
                w.done(g)
            yield b, g

    flip = [0]

    def evac(o, i, *deps):
        flip[0] += 1
        return acopy(o, i, *deps) if flip[0] % 2 else cp(o, i, *deps)

    def split_bank(b, h, hi, lo, scale=None):
        n = hi.shape[-1]
        if scale is None:
            a = acopy(hi, b.t[:, 0:n], h)
            z = tt(lo, b.t[:, 0:n], hi.bitcast(F32), SUB, a)
        else:
            a = act(hi, b.t[:, 0:n], ACT.Identity, h, scale=scale)
            z = stt(lo, b.t[:, 0:n], scale, hi.bitcast(F32), MUL, SUB, a)
        b.done(z)
        return a, z

    def rstd_of(o, i, n, *deps):
        a = act(o, i, ACT.Ln, *deps, scale=1.0 / n, bias=epsc[0:i.shape[0], :])
        return act(o, o, ACT.Exp, a, scale=-0.5)

    def token_rms(src, tiles, at, loads, *deps):
        t, free = tmp.take()
        t2, free2 = tmp.take()
        sc = small[:, at:at + 2 * tiles]
        last = None
        for c in range(tiles):
            for hf in range(2):
                last = act((t, t2)[hf].t[:], src[:, c, hf * 512:(hf + 1) * 512], ACT.Square, loads[c], *deps, free, free2, last,
                           acc=sc[:, 2 * c + hf:2 * c + hf + 1])
        t.done(last)
        t2.done(last)
        a = tt(small[:, at + 16:at + 16 + tiles], small[:, at:at + 2 * tiles:2], small[:, at + 1:at + 2 * tiles:2], ADD, last)
        return rstd_of(small[:, at + 16:at + 16 + tiles], small[:, at + 16:at + 16 + tiles], D, a), at + 16

    def transpose_tokens(src, tiles, ready_, dst, kts=range(8)):
        r = []
        for kt in kts:
            b, free = RA.take()
            for c in range(tiles):
                h = tr(b.t[:, c * P:(c + 1) * P], src[:, c, kt * P:(kt + 1) * P], ident[:], at(ready_, kt), free, C)
            r.append(dst(kt, b, h))
        return r

    r, at_ = token_rms(memt, 2, 160, l_mem, C)
    for c in range(2):
        r2 = ts(memt[:, c, :], memt[:, c, :], small[:, at_ + c:at_ + c + 1], None, MUL, None, r, l_c)
    mh = hhi[:].rearrange("p a b -> p (a b)")[:, 0:2048].rearrange("p (k n) -> p k n", k=8)
    ml = hlo[:].rearrange("p a b -> p (a b)")[:, 0:2048].rearrange("p (k n) -> p k n", k=8)
    ahead(-1)
    mr = transpose_tokens(memt, 2, r2, lambda kt, b, h: split_bank(b, h, mh[:, kt, :], ml[:, kt, :], col("mem_norm", kt)))
    fm_first(("memk", "memk"), mh, ml, 8, 256, mr)
    r, at_ = token_rms(xt, 4, 0, l_x, C)
    for c in range(4):
        xr2 = ts(yt[:, c, :], xt[:, c, :], small[:, at_ + c:at_ + c + 1], None, MUL, None, r)
    mk = []
    for m in range(2):
        b, h = fm_tile("memk", mh, ml, 8, 256)
        t, free = tmp.take()
        mk.append((m, b, t, act(t.t[:, 0:256], b.t[:, 0:256], ACT.Square, h, free)))

    def mem_norm():
        for m, b, t, a in mk:
            b2, free = RA.take()
            g = mm(b2.t[:, 0:256], blk[:], t.t[:, 0:256], True, True, a, free, C)
            t.done(g)
            t2, free = tmp.take()
            a = rstd_of(t2.t[:, 0:256], b2.t[:, 0:256], 64, g, free)
            b2.done(a)
            z = tt(kmn[:, m, :], b.t[:, 0:256], t2.t[:, 0:256], MUL, a)
            b.done(z)
            t2.done(z)

    for c, (b, h) in enumerate(tm_group("memv", mh, ml, 2, 256, mr, mem_norm)):
        z = evac(vmem[:, c, :], b.t[:, 0:256], h)
        b.done(z)
    ahead(state["next"])
    hr = transpose_tokens(yt, 4, xr2, lambda kt, b, h: split_bank(b, h, hhi[:, kt, :], hlo[:, kt, :], col("norm_g", kt)))
    q.barrier()
    iscope.close()

    class Head:

        def __init__(self, q, k, v, width, causal=False, bias=None, prep=None, low=None, add=None):
            self.low, self.add = low, add
            self.q, self.k, self.v, self.width = q, k, v, width
            self.causal, self.bias, self.prep = causal, bias, prep

    def attention(name, heads, dst, post=None, side=None, free=()):
        sc = ExitStack()
        nh = len(heads)
        pt = Ring([Slot(sbuf(f"{name}_pt{i}", [P, T], scope=sc)) for i in range(3)])
        for s_ in pt.s:
            s_.done(*free)
        biased = any(h.bias for h in heads)
        st = Ring([Slot(sbuf(f"{name}_s{i}", [P, T], scope=sc)) for i in range(2)]) if biased else None
        mx = sbuf(f"{name}_mx", [P, nh, 4], scope=sc)
        rs = sbuf(f"{name}_rs", [P, nh, 4], scope=sc)
        items = [(h, i) for h in range(nh) for i in (0, 1, 2, 3)]
        S, PR, PT, O = {}, {}, {}, {}
        fin = []

        def score(t):
            h, i = items[t]
            n = heads[h].width(i)
            b, free = RS.take()
            (qa, qh), (ka, kh) = heads[h].q(i), heads[h].k(n)
            hd = heads[h]
            last_ = not hd.causal and not hd.low and not hd.add
            g = mm(b.t[:, 0:n], qa, ka, True, last_, qh, kh, free)
            if hd.low:
                ql_, kl_ = hd.low(i, n)
                mm(b.t[:, 0:n], qa, kl_, False, False)
                g = mm(b.t[:, 0:n], ql_, ka, False, not hd.causal and not hd.add)
            if hd.add:
                sa, ca, *dep = hd.add(n)
                g = mm(b.t[:, 0:n], sa, ca, False, not hd.causal, dep)
            if heads[h].causal:
                g = mm(b.t[:, n - P:n], identb[:], maskb[:], False, True, C)
            S[t] = (b, g, n)

        def soft(t):
            h, i = items[t]
            b, g, n = S.pop(t)
            p_, free = tmp.take()
            m = mx[:, h, i:i + 1]
            if heads[h].bias:
                s_, f2 = st.take()
                ba, bh = heads[h].bias(i, n)
                z = q.op("dve", lambda e: e.tensor_tensor_reduce(s_.t[:, 0:n], b.t[:, 0:n], ba, 1.0, -3e38, ADD,
                                                                 MAX, m), (g, bh, f2))
                b.done(z)
                z = ts(m, m, -1.0, None, MUL, None, z)
                a = act(p_.t[:, 0:n], s_.t[:, 0:n], ACT.Exp, z, free, bias=m, acc=rs[:, h, i:i + 1])
                s_.done(a)
            else:
                z = red(m, b.t[:, 0:n], MAX, g, negate=True)
                a = act(p_.t[:, 0:n], b.t[:, 0:n], ACT.Exp, z, free, bias=m, acc=rs[:, h, i:i + 1])
                b.done(a)
            PR[t] = (p_, a, n)

        def turn(t):
            p_, a, n = PR.pop(t)
            b, free = RT.take()
            for j in range(n // P):
                g = tr(b.t[:, j * P:(j + 1) * P], p_.t[:, j * P:(j + 1) * P], ident[:], a, free)
            p_.done(g)
            s_, f2 = pt.take()
            z = (acopy if biased else cp)(s_.t[:, 0:n], b.t[:, 0:n], g, f2)
            b.done(z)
            PT[t] = (s_, z, n)

        def pv(t):
            h, i = items[t]
            s_, z, n = PT.pop(t)
            if t % 8 == 0:
                O[t // 8] = RO.take()
            b, free = O[t // 8]
            o = b.t[:, ((h % 2) * 4 + i) * 64:((h % 2) * 4 + i) * 64 + 64]
            for j in range(n // P):
                va, vh = heads[h].v(j)
                g = mm(o, s_.t[:, j * P:(j + 1) * P], va, j == 0, j == n // P - 1, z, vh, free)
            s_.done(g)
            if t % 8 == 7:
                h0 = h - 1
                rr = rs[:, h0:h0 + 2, :]
                a = recip(rr, rr, g)
                o_, f3 = dst(t // 8)
                for ii in range(4):
                    ov = b.t[:, :].rearrange("p (h i n) -> p h i n", h=2, i=4)[:, :, ii, :]
                    z = tt(o_(ii), ov, rr[:, :, ii:ii + 1].to_broadcast([P, 2, 64]), MUL, a, f3)
                b.done(z)
                fin.append(z)

        N = len(items)
        for t in range(-2, N + 8):
            if (t + 2) % 4 == 0 and t + 2 < N and heads[(t + 2) // 4].prep:
                heads[(t + 2) // 4].prep()
            if 0 <= t < N:
                score(t)
            if 1 <= t <= N:
                soft(t - 1)
            if 3 <= t <= N + 2:
                turn(t - 3)
            if 5 <= t <= N + 4:
                pv(t - 5)
            if side:
                side(t)
            if post and t >= 14 and (t - 14) % 8 == 0 and (t - 14) // 8 < len(fin):
                post((t - 14) // 8, fin[(t - 14) // 8])
        return sc, fin

    def sigmoid_den(o, i, *deps):
        a = act(o, i, ACT.Exp, *deps, scale=-1.0)
        return ts(o, o, 1.0, None, ADD, None, a)

    def log_sigmoid(o, i, rows, n, *deps):
        t, free = tmp.take()
        tt_ = t.t[0:rows, 0:n]
        a = act(tt_, i, ACT.Abs, *deps, free)
        a = act(tt_, tt_, ACT.Exp, a, scale=-1.0)
        a = act(tt_, tt_, ACT.Ln, a, bias=1.0)
        z = stt(o, i, 0.0, tt_, MIN, SUB, a)
        t.done(z)
        return z

    s1 = ExitStack()
    aqh, aql, akh, akl = [sbuf(n, [P, 3, T], F32R, scope=s1) for n in ("aqh", "aql", "akh", "akl")]
    av = sbuf("av", [P, 4, 384], scope=s1)
    ag = sbuf("ag", [P, 4, 384], scope=s1)
    U = sbuf("U", [P, 6, 512], scope=s1)
    bar = q.last()
    for hh in range(6):
        src = d["rel_ext"][hh:hh + 1, 1:513]
        skew = bass.AP(tensor=src.tensor, offset=src.offset, ap=[[1, P], [1, 512]])
        l_u = dma(U[:, hh, :], skew, s_u, bar)
    u_ok = mset(U[0:64, :, 0:64], NEG, l_u)
    q_, k_ = [], []
    fm_first(("aq", "aq"), hhi, hlo, 8, T, hr)
    for m in range(3):
        b, h = fm_tile("aq", hhi, hlo, 8, T, hr)
        q_.append(split_bank(b, h, aqh[:, m, :], aql[:, m, :], 0.125))
    for m in range(3):
        b, h = fm_tile("ak", hhi, hlo, 8, T)
        k_.append(split_bank(b, h, akh[:, m, :], akl[:, m, :]))
    table("silu_and_others")
    g_ok = []
    for c, (b, h) in enumerate(tm_group("ag", hhi, hlo, 4, 384)):
        a = act(ag[:, c, :], b.t[:, 0:384], ACT.Silu, h)
        b.done(a)
        g_ok.append(a)
    table("natural_log_exp_and_others")
    v_ = []
    for c, (b, h) in enumerate(tm_group("av", hhi, hlo, 4, 384)):
        z = evac(av[:, c, :], b.t[:, 0:384], h)
        b.done(z)
        v_.append(z)
    def half(h):
        return slice(64 * (h % 2), 64 * (h % 2) + 64)

    def u_bias(h, i, n):
        base = U[:, h, n - 1:n]
        return bass.AP(tensor=base.tensor, offset=base.offset, ap=[base.ap[0], [-1, n]]), u_ok

    def att_head(h):
        hf, m = half(h), h // 2
        return Head(lambda i: (aqh[hf, m, i * P:(i + 1) * P], q_[m]),
                    lambda n: (akh[hf, m, 0:n], k_[m]),
                    lambda j: (av[:, j, h * 64:(h + 1) * 64], v_[j]),
                    lambda i: P * (i + 1), bias=lambda i, n: u_bias(h, i, n),
                    low=lambda i, n: (aql[hf, m, i * P:(i + 1) * P], akl[hf, m, 0:n]))

    sc, fin = attention("att", [att_head(h) for h in range(6)],
                        lambda g: (lambda i: yt[:, i, g * P:(g + 1) * P].rearrange("p (h n) -> p h n", h=2), None))
    ya = tt(yt[:, :, 0:384], yt[:, :, 0:384], ag[:], MUL, fin, g_ok)
    q.barrier()
    sc.close()
    s1.close()

    s2 = ExitStack()
    cqk = sbuf("cqk", [P, 6, T], scope=s2)
    mva = sbuf("mva", [P, 4, 6, 65], scope=s2)
    mo = sbuf("mo", [P, 4, 384], scope=s2)
    mg = sbuf("mg", [P, 4, 384], scope=s2)
    hm = sbuf("hm", [P, 4, 6, 64], scope=s2)
    gts = sbuf("gts", [70, T], scope=s2)
    wal = sbuf("wal", [48, P], scope=s2)
    fr = sbuf("fr", [6, T], scope=s2)
    lf = fr
    FF_ = sbuf("Fsum", [6, T], scope=s2)
    aj = sbuf("aj", [6, T], scope=s2)
    Am = gts[64:70, :]
    em = FF_
    bg = sbuf("bg", [12, 1], scope=s2)
    acol = sbuf("acol", [P, 4, 6], scope=s2)
    ecol = sbuf("ecol", [P, 4, 6], scope=s2)
    gml = sbuf("gml", [P, 384], scope=s2)
    bar = q.last()
    l_g = dma(bg[:], d["b_gates"].rearrange("a n -> n a"), s_u, bar)
    l_g = dma(gml[:], d["ml_norm_g"][0:1, :].to_broadcast([P, 384]), s_u, bar)
    l_g = dma(wal[32:48, :], d["w_alpha"].rearrange("a r n -> (a r) n"), s_u, bar)
    o6 = c_1
    onesv = mset(mva[:, :, :, 64:65], 1.0)
    b, h = fm_tile("gate", hhi, hlo, 8, T, rows=48)
    a = act(gts[0:12, :], b.t[0:12, :], ACT.Identity, h, l_g, bias=bg[:, 0:1])
    a_ga = acopy(gts[32:48, :], b.t[32:48, :], h)
    b.done(a_ga)
    mo_ = []

    def gate_rows():
        b, free = RA.take()
        g = mm(b.t[0:6, :], ident[0:12, 6:12], gts[0:12, :], True, True, a, free, C)
        b2, free = RA.take()
        g2 = mm(b2.t[:], wal[32:48, :], gts[32:48, :], True, True, a_ga, free, l_g)
        z = acopy(fr[:], b.t[0:6, :], g)
        b.done(z)
        t, free = tmp.take()
        z2 = act(t.t[:], b2.t[:], ACT.Identity, g2, free, l_c, bias=col("b_alpha"))
        b2.done(z2)
        pend.extend([z, t, z2])

    pend = []
    for c, (b, h) in enumerate(tm_group("mo", hhi, hlo, 4, 384, mid=gate_rows)):
        a = act(mo[:, c, :], b.t[:, 0:384], ACT.Exp, h, scale=-1.0)
        b.done(a)
        mo_.append(ts(mo[:, c, :], mo[:, c, :], 1.0, None, ADD, None, a, eng="pool"))
    z, t_al, z2 = pend
    al_ = t_al.t[:]
    z = log_sigmoid(lf[:], fr[:], 6, T, z)
    z = q.op("dve", lambda e: e.tensor_tensor_scan(FF_[:], ones[0:6, 0:1].to_broadcast([6, T]), lf[:], 0.0, MUL, ADD), (z, o6))
    z = tt(aj[:], gts[0:6, :], FF_[:], SUB, z)
    z_a = z
    z = q.op("dve", lambda e: e.tensor_tensor_scan(Am, ones[0:6, 0:1].to_broadcast([6, T]), aj[:], 0.0, MUL, MAX), (z,))
    z_A = z
    z = tt(em[:], FF_[:], Am, ADD, z)
    z_e = act(em[:], em[:], ACT.Exp, z, scale=-1.0)
    z = log_sigmoid(al_, al_, P, T, z2)
    z = ts(al_, al_, 1.0 / 16.0, None, MUL, None, z)
    zb = q.op("dve", lambda e: e.tensor_tensor_scan(bT[:], ones[:, 0:1].to_broadcast([P, T]), al_, 0.0, MUL,
                                                    ADD), (z, c_1))
    t_al.done(zb)
    table("silu_and_others")
    cq_ = []
    for m in range(6):
        b, h = fm_tile("mqk", hhi, hlo, 8, T)
        t, free = tmp.take()
        x_ = t.t
        z = act(x_[:], b.t[:], ACT.Identity, h, free, l_c, scale=col("conv_w", 4 * m + 3))
        for s in range(1, 4):
            z = stt(x_[:, s:T], b.t[:, 0:T - s], col("conv_w", 4 * m + 3 - s), x_[:, s:T], MUL, ADD, z)
        b.done(z)
        a = act(cqk[:, m, :], x_[:], ACT.Silu, z)
        t.done(a)
        cq_.append(a)
    mg_ = []
    for c, (b, h) in enumerate(tm_group("mg", hhi, hlo, 4, 384)):
        a = act(mg[:, c, :], b.t[:, 0:384], ACT.Silu, h)
        b.done(a)
        mg_.append(tt(mg[:, c, :], mg[:, c, :], gml[:], MUL, a, l_g, eng="pool"))
    b, free = RA.take()
    for c in range(4):
        tr(b.t[:, c * 6:c * 6 + 6], aj[:, c * P:(c + 1) * P], ident[0:6, 0:6], z_a, free)
    for c in range(4):
        g = tr(b.t[:, 24 + c * 6:24 + c * 6 + 6], em[:, c * P:(c + 1) * P], ident[0:6, 0:6], z_e)
    z = cp(acol[:].rearrange("p a b -> p (a b)"), b.t[:, 0:24], g)
    c_ok = cp(ecol[:].rearrange("p a b -> p (a b)"), b.t[:, 24:48], g)
    b.done(c_ok)
    table("natural_log_exp_and_others")
    mv_ = []
    for c, (b, h) in enumerate(tm_group("mv", hhi, hlo, 4, 384)):
        z = evac(mva[:, c, :, 0:64], b.t[:, 0:384].rearrange("p (h n) -> p h n", h=6), h, onesv)
        b.done(z)
        mv_.append(z)

    dts = Ring([Slot(sbuf(f"dt{i}", [P, T], scope=s2)) for i in range(3)])
    scs = Ring([Slot(sbuf(f"scm{i}", [P, 1280], scope=s2)) for i in range(2)])
    mden = sbuf("mden", [P, 6, 4], scope=s2)
    OFF = [0, 512, 896, 1152]
    HS = {}

    def ml_decay(h):
        ab, free = RT.take()
        ga_ = mm(ab.t[:], ident[64:70, 64 + h:65 + h].to_broadcast([6, P]), Am, True, True, z_A, free, C)
        s_, f2 = scs.take()
        lasts = []
        for J in range(4):
            n = T - J * P
            dt_, free = dts.take()
            a = act(dt_.t[:, 0:n], ab.t[:, J * P:T], ACT.Exp, ga_, c_ok, free, scale=-1.0, bias=acol[:, J, h:h + 1])
            pz = sel(dt_.t[:, 0:P], [[1, P]], ALU.is_ge, 0.0, 0, -1, a)
            b, free = RS.take()
            g = mm(b.t[:, 0:n], cqk[half(h), 3 + h // 2, J * P:(J + 1) * P], cqk[half(h), h // 2, J * P:T],
                   True, True, cq_[h // 2], cq_[3 + h // 2], free)
            z = stt(s_.t[:, OFF[J]:OFF[J] + n], b.t[:, 0:n], 0.125, dt_.t[:, 0:n], MUL, MUL, g, pz, a, f2)
            b.done(z)
            dt_.done(z)
            lasts.append(z)
        ab.done(a)
        HS[h] = (s_, lasts)

    def ml_out(h):
        s_, lasts = HS.pop(h)
        b, free = RO.take()
        for i in range(4):
            for J in range(i + 1):
                o = OFF[J] + (i - J) * P
                g = mm(b.t[:, i * 65:(i + 1) * 65], s_.t[:, o:o + P], mva[:, J, h, :], J == 0, J == i,
                       lasts[J], mv_[J], free)
        s_.done(g)
        ov = b.t[:, 0:260].rearrange("p (i n) -> p i n", i=4)
        a = act(mden[:, h, :].unsqueeze(2), ov[:, :, 64:65], ACT.Abs, g)
        z = tt(mden[:, h, :].unsqueeze(2), mden[:, h, :].unsqueeze(2), ecol[:, :, h:h + 1], MAX, a, c_ok)
        z = recip(mden[:, h, :], mden[:, h, :], z)
        z = tt(hm[:, :, h, :], ov[:, :, 0:64], mden[:, h, :].unsqueeze(2).to_broadcast([P, 4, 64]), MUL, z)
        b.done(z)
        return z

    ml_ok, nrm, ym = [], {}, [ya]

    def ml_norm(h):
        x_ = hm[:, :, h, :]
        r = small[:, 32 + 4 * h:36 + 4 * h]
        t, free = tmp.take()
        tv = t.t[:, 0:256].rearrange("p (i n) -> p i n", i=4)
        a = act(tv, x_, ACT.Square, ml_ok[h], free)
        mh_ = mo[:, :, h * 64:(h + 1) * 64]
        zr = recip(mh_, mh_, mo_)
        gh_ = mg[:, :, h * 64:(h + 1) * 64]
        zg = tt(gh_, gh_, mh_, MUL, zr, mg_, eng="pool")
        z = red(r, tv, ADD, a)
        t.done(z)
        nrm[h] = (rstd_of(r, r, 64, z), zg)

    def ml_last(h):
        x_ = hm[:, :, h, :]
        a, zg = nrm[h]
        z = tt(x_, x_, small[:, 32 + 4 * h:36 + 4 * h].unsqueeze(2).to_broadcast([P, 4, 64]), MUL, a)
        ym.append(tt(yt[:, :, 384 + h * 64:448 + h * 64], x_, mg[:, :, h * 64:(h + 1) * 64], MUL, z, zg))

    for h in range(9):
        if h < 6:
            ml_decay(h)
        if 1 <= h <= 6:
            ml_ok.append(ml_out(h - 1))
        if h == 6:
            ahead(state["next"])
        if 2 <= h <= 7:
            ml_norm(h - 2)
        if h >= 3:
            ml_last(h - 3)
    q.barrier()
    s2.close()

    def turn_y(y, kts, *deps):
        return transpose_tokens(y, 4, tuple(deps), lambda kt, b, h: split_bank(b, h, hhi[:, kt, :], hlo[:, kt, :]), kts)

    s3 = ExitStack()
    gq = sbuf("gq", [P, T], scope=s3)
    gk = sbuf("gk", [P, T], scope=s3)
    gv = sbuf("gv", [P, 4, 256], scope=s3)
    gg = sbuf("gg", [P, 4, 256], scope=s3)
    ATT = sbuf("ATT", [P, 4, 4, P], scope=s3)
    AX_ = [sbuf(f"AX{J}", [P, 4, (3 - J) * P], scope=s3) for J in range(3)]
    msk = sbuf("msk", [P, 7, P], scope=s3)
    ggn = sbuf("ggn", [P, 256], scope=s3)
    hg = sbuf("hg", [P, 4, 4, 64], scope=s3)
    nref = sbuf("nref", [P, 3], scope=s3)
    kl = Ring([Slot(sbuf(f"kl{i}", [P, T], scope=s3)) for i in range(2)])
    ql = Ring([Slot(sbuf(f"ql{i}", [P, T], scope=s3)) for i in range(2)])
    bar = q.last()
    l_a = dma(ggn[:], d["gla_norm_g"][0:1, :].to_broadcast([P, 256]), s_u, bar)
    z0 = mset(msk[:], 0.0)
    z1 = mset(ATT[:], 0.0)
    mk_ = []
    for li in range(7):
        s = 64 >> li
        nb = P // (2 * s)
        v4 = msk[:, li, :].rearrange("p (a b s) -> p a b s", a=nb, b=2)[:, :, 1, :]
        z = mset(v4, 1.0, z0)
        z = sel(v4, [[-2 * s, nb], [0, s]], ALU.is_ge, 0.0, 0, 1, z)
        z = sel(v4, [[2 * s, nb], [0, s]], ALU.is_ge, 0.0, s - 1, -1, z)
        mk_.append(z)
    table("silu_and_others")
    gg_ok = []
    for c, (b, h) in enumerate(tm_group("gg", hhi, hlo, 4, 256)):
        a = act(gg[:, c, :], b.t[:, 0:256], ACT.Silu, h)
        b.done(a)
        gg_ok.append(tt(gg[:, c, :], gg[:, c, :], ggn[:], MUL, a, l_a, eng="pool"))
    table("natural_log_exp_and_others")
    b, h = fm_tile("gqk", hhi, hlo, 8, T)
    zq = act(gq[:], b.t[:], ACT.Identity, h, scale=32 ** -0.5)
    b.done(zq)
    b, h = fm_tile("gqk", hhi, hlo, 8, T)
    zk = cp(gk[:], b.t[:], h)
    b.done(zk)
    LV = {}

    def level(li):
        if li == 7:
            LV[li] = (gk, gq, zk, zq, None, None)
            return
        t, free = tmp.take()
        (k2, f1), (q2, f2) = kl.take(), ql.take()
        if li < 7:
            s = 64 >> li
            nb = T // (2 * s)
            bv = bT[:].rearrange("p (a s) -> p a s", s=2 * s)
            tv = t.t[:].rearrange("p (a s) -> p a s", s=2 * s)
            z = tt(tv, bv, bv[:, :, s - 1:s].to_broadcast([P, nb, 2 * s]), SUB, zb, free)
            a = act(t.t[:], t.t[:], ACT.Abs, z)
            a = act(t.t[:], t.t[:], ACT.Exp, a, scale=-1.0)
            zk2 = tt(k2.t[:], gk[:], t.t[:], MUL, a, zk, f1)
            zq2 = tt(q2.t[:], gq[:], t.t[:], MUL, a, zq, f2, eng="pool")
        else:
            J = li - 8
            n = (3 - J) * P
            e_ = bT[:, J * P + 127:J * P + 128]
            zr = ts(nref[:, J:J + 1], e_, -1.0, None, MUL, None, zb)
            a1 = act(t.t[:, 0:P], bT[:, J * P:(J + 1) * P], ACT.Exp, zb, free, scale=-1.0, bias=e_)
            a2 = act(t.t[:, P:T - J * P], bT[:, (J + 1) * P:T], ACT.Exp, zr, bias=nref[:, J:J + 1])
            zk2 = tt(k2.t[:, 0:P], gk[:, J * P:(J + 1) * P], t.t[:, 0:P], MUL, a1, f1, zk)
            zq2 = tt(q2.t[:, 0:n], gq[:, (J + 1) * P:T], t.t[:, P:T - J * P], MUL, a2, f2, zq)
        t.done(zk2, zq2)
        LV[li] = (k2.t, q2.t, zk2, zq2, k2, q2)

    level(8)
    level(9)
    gv_ = []
    for c, (b, h) in enumerate(tm_group("gv", hhi, hlo, 4, 256)):
        z = evac(gv[:, c, :], b.t[:, 0:256], h)
        b.done(z)
        gv_.append(z)
    yr = turn_y(yt, range(0, 6), ym)

    ax_ = {}
    prev = {h: z1 for h in range(4)}
    order = [8, 9, 10, 0, 1, 2, 3, 4, 5, 6, 7]
    for at_i, li in enumerate(order):
        K_, Q_, zk2, zq2, k2, q2 = LV.pop(li)
        bs = []
        for h in range(4):
            b, free = RA.take()
            hp = slice(32 * h, 32 * h + 32)
            if li >= 8:
                n = (11 - li) * P
                g = mm(b.t[:, 0:n], K_[hp, 0:P], Q_[hp, 0:n], True, True, zk2, zq2, free)
            else:
                for c in range(4):
                    g = mm(b.t[:, c * P:(c + 1) * P], K_[hp, c * P:(c + 1) * P], Q_[hp, c * P:(c + 1) * P], True,
                           True, zk2, zq2, free)
            bs.append((b, g))
        if k2 is not None:
            k2.done(g)
            q2.done(g)
        if at_i + 2 < len(order):
            level(order[at_i + 2])
        for h, (b, g) in enumerate(bs):
            if li >= 8:
                z = evac(AX_[li - 8][:, h, :], b.t[:, 0:n], g)
                ax_[li - 8, h] = z
            else:
                mb = (msk[:, li, :] if li < 7 else ident[:]).bitcast(I32).unsqueeze(1).to_broadcast([P, 4, P])
                bv4 = b.t[:].rearrange("p (c n) -> p c n", c=4)
                z = q.op("dve", lambda e, h=h, mb=mb, bv4=bv4: e.copy_predicated(ATT[:, :, h, :], mb, bv4),
                         (g, mk_[li] if li < 7 else None, prev[h]))
                prev[h] = z
            b.done(z)
    ahead(state["next"])
    gn, yz = {}, []

    def gla_last(i):
        z = tt(hg[:, i], hg[:, i], small[:, 64 + 4 * i:68 + 4 * i].unsqueeze(2).to_broadcast([P, 4, 64]), MUL, gn[i])
        yz.append(tt(yt[:, i, 768:1024], hg[:, i].rearrange("p h n -> p (h n)"), gg[:, i, :], MUL, z, gg_ok))

    for at_i, i in enumerate((3, 2, 1, 0)):
        b, free = RA.take()
        for h in range(4):
            o = b.t[:, h * 64:(h + 1) * 64]
            for J in range(i):
                mm(o, AX_[J][:, h, (i - J - 1) * P:(i - J) * P], gv[:, J, h * 64:(h + 1) * 64], J == 0, False,
                   ax_[J, h], gv_[J], free)
            g = mm(o, ATT[:, i, h, :], gv[:, i, h * 64:(h + 1) * 64], i == 0, True, prev[h], gv_[i], free)
        z = cp(hg[:, i, :, :], b.t[:, 0:256].rearrange("p (h n) -> p h n", h=4), g)
        b.done(z)
        t, free = tmp.take()
        r = small[:, 64 + 4 * i:68 + 4 * i]
        a = act(t.t[:, 0:256], hg[:, i].rearrange("p h n -> p (h n)"), ACT.Square, z, free)
        z = red(r, t.t[:, 0:256].rearrange("p (h n) -> p h n", h=4), ADD, a)
        t.done(z)
        gn[i] = rstd_of(r, r, 64, z)
        if at_i:
            gla_last(i + 1)
    gla_last(0)
    q.barrier()
    s3.close()

    xlast = {"h": [None] * 8}
    stats = {"pend": []}

    def stat_begin():
        stats["b"], stats["free"] = stat, stat.take()
        stats["n"] = 0

    def stat_add(k, dep, whole=False):
        stats["pend"].append(squares(xT[:, k, :], dep, whole=whole or k == 7))

    def stat_sum():
        for x_ in stats["pend"]:
            stats["g"] = sum_parts(stat.t[:], (ones, onesr), x_, stats["n"] == 0, stats["n"] == 7, stats["free"])
            stats["n"] += 1
        stats["pend"] = []

    def fm_norm(gname, g0):
        stat_sum()
        assert stats["n"] == 8
        rb, f2 = hold.take()
        a = rstd_of(rb.t[:], stat.t[:], D, stats["g"], f2)
        stat.done(a)
        out_ = []
        for k in range(8):
            t, f2 = tmp.take()
            z0_ = stt(t.t[:], xT[:, k, :], col(gname, g0 + k), rb.t[:], MUL, MUL, a, f2, xlast["h"][k])
            a2 = acopy(hhi[:, k, :], t.t[:], z0_)
            z = tt(hlo[:, k, :], t.t[:], hhi[:, k, :].bitcast(F32), SUB, a2, eng="pool" if k % 2 else "dve")
            t.done(z)
            out_.append((a2, z))
        rb.done(z0_)
        return out_

    s4 = ExitStack()
    fgr = sbuf("fgr", [P, D], scope=s4)
    l_f = dma(fgr[:], d["final_g"].rearrange("(a n) -> a n", a=1).to_broadcast([P, D]), s_u, q.last())
    turn_last = lambda: yr.extend(turn_y(yt, range(6, 8), yz))
    rs_, rst = [], []
    at_ = 112

    def scaled(o, c):
        xc = xt[:, c, o:o + 256]
        return stt(xc, xc, small[:, at_ + c:at_ + c + 1], fgr[:, o:o + 256], MUL, MUL, rst[c], l_f)

    sqs = small[:, 96:112].rearrange("p (c g) -> p c g", c=4)
    zs_ = mset(sqs, 0.0, q.last())
    for gi, g0 in enumerate((0, 384, 768)):
        n = min(384, D - g0)
        for c, (b, h) in enumerate(tm_group("wo1", hhi, hlo, 4, n, yr, turn_last if gi == 0 else None)):
            z = tt(xt[:, c, g0:g0 + n], b.t[:, 0:n], xt[:, c, g0:g0 + n], ADD, h)
            b.done(z)
            t, free = tmp.take()
            a = act(t.t[:, 0:n], xt[:, c, g0:g0 + n], ACT.Square, z, free, zs_, acc=sqs[:, c, gi:gi + 1])
            t.done(a)
            rs_.append(a)
            if gi == 2:
                rc = small[:, at_ + c:at_ + c + 1]
                z = red(rc, sqs[:, c, :], ADD, rs_)
                rst.append(rstd_of(rc, rc, D, z))
                if c > 0:
                    scaled(0, c - 1)
    xz = []

    def to_x(kt, b, h):
        z = acopy(xT[:, kt, :], b.t[:], h)
        b.done(z)
        stat_sum()
        stat_add(kt, z, True)
        xz.append(z)
        return z

    stat_begin()

    z = scaled(0, 3)
    for o in range(0, D, 256):
        zn = [scaled(o + 256, c) for c in range(4)][-1] if o + 256 < D else None
        transpose_tokens(xt, 4, z, to_x, (o // P, o // P + 1))
        z = zn
    xlast["h"] = xz
    hr = fm_norm("norm_mix", 0)
    q.barrier()
    s4.close()
    mscope.close()


    def head_normed(key, dst, gcol, dep=None, gdep=None):
        b, h = fm_tile(key, hhi, hlo, 8, T, dep)
        parts = squares(b.t[:], h)
        yield None
        b2, free = RA.take()
        g = sum_parts(b2.t[:], (blk, blkr), parts, True, True, free)
        t2, free = tmp.take()
        a = rstd_of(t2.t[:], b2.t[:], 64, g, free)
        b2.done(a)
        if type(dst) is not tuple:
            z = stt(dst, b.t[:], gcol, t2.t[:], MUL, MUL, a, gdep)
            b.done(z)
        else:
            z = stt(t2.t[:], b.t[:], gcol, t2.t[:], MUL, MUL, a, gdep)
            b.done(z)
            a = acopy(dst[0], t2.t[:], z)
            z = tt(dst[1], t2.t[:], dst[0].bitcast(F32), SUB, a, eng="pool")
        t2.done(z)
        yield z

    def head_normed_all(jobs):
        out_, before = [], None
        for j in jobs:
            g = head_normed(*j)
            next(g)
            if before:
                out_.append(next(before))
            before = g
        return out_, lambda: out_.append(next(before))

    def turned_outputs(l, scope, over=()):
        yr = Ring([Slot(sbuf(f"y{l}_{i}", [P, 4, P], scope=scope)) for i in range(2)])
        for s_ in yr.s:
            s_.done(*over)
        res, used = [None] * 8, {}

        def dst(g):
            s_, free = yr.take()
            used[g] = s_
            return lambda i: s_.t[:, i, :].rearrange("p (h n) -> p h n", h=2), free

        def post(g0, z):
            kt = (g0 + 6) % 8
            b, free = RT.take()
            for c in range(4):
                g = tr(b.t[:, c * P:(c + 1) * P], used[g0].t[:, c, :], ident[:], z, free)
            used[g0].done(g)
            res[kt] = split_bank(b, g, hhi[:, kt, :], hlo[:, kt, :])
        return res, dst, post

    def out_product(l, yr):
        hs = []
        stat_begin()
        for m in range(8):
            b, h = fm_tile("wo", hhi, hlo, 8, T, yr)
            stat_sum()
            z = tt(xT[:, m, :], b.t[:], xT[:, m, :], ADD, h)
            b.done(z)
            stat_add(m, z)
            hs.append(z)
        xlast["h"] = hs
        q.barrier()

    def ffn(l, final, extra=None):
        hr = fm_norm("norm_ffn", 8 * l)
        table("silu_and_others")
        fs = ExitStack()
        ahi = sbuf(f"ahi{l}", [P, 11, T], F32R, scope=fs)
        alo = sbuf(f"alo{l}", [P, 11, T], F32R, scope=fs)
        cr = Ring([Slot(sbuf(f"cr{l}_{i}", [P, T], scope=fs)) for i in range(4)])
        ob = Ring([Slot(sbuf(f"ob{l}_{i}", [P, 4, P], scope=fs)) for i in range(2)]) if final else None
        dlast = None
        hs = [None] * 8

        def conv(b, h, ch):
            t, free = cr.take()
            cw = lambda j: col(f"cw{l}", 3 * ch + j)
            a = act(t.t[:], b.t[:], ACT.Identity, h, free, scale=cw(2), bias=col(f"cb{l}", ch))
            z = stt(t.t[:, 1:T], b.t[:, 0:T - 1], cw(1), t.t[:, 1:T], MUL, ADD, a)
            z = stt(t.t[:, 2:T], b.t[:, 0:T - 2], cw(0), t.t[:, 2:T], MUL, ADD, z)
            b.done(z)
            return t, z

        def gate(ct, tg, zg, tv, zv):
            a = act(tg.t[:], tg.t[:], ACT.Silu, zg)
            z = tt(tg.t[:], tg.t[:], tv.t[:], MUL, a, zv, eng="pool")
            tv.done(z)
            yield None
            a2 = acopy(ahi[:, ct, :], tg.t[:], z, dlast)
            z = tt(alo[:, ct, :], tg.t[:], ahi[:, ct, :].bitcast(F32), SUB, a2, eng="pool")
            tg.done(z)
            yield z

        store = []

        def put_out(m, z):
            b, free = RA.take()
            for c in range(4):
                g2 = tr(b.t[:, c * P:(c + 1) * P], xT[:, m, c * P:(c + 1) * P], ident[:], z, free)
            o, free = ob.take()
            z = evac(o.t[:], b.t[:].rearrange("p (c n) -> p c n", c=4), g2, free)
            b.done(z)
            dd = dma(out.rearrange("a (c p) n -> p (a c) n", p=P)[:, :, m * P:(m + 1) * P], o.t[:], s_out[m % 2], z)
            o.done(dd)
            last_out[m % 2] = dd

        fm_first(("up", "up"), hhi, hlo, 8, T, hr)
        for half_ in range(2):
            fin = []
            behind = None
            for ct in range(11):
                ch = 11 * half_ + ct
                if extra and ch == 2:
                    extra(fs)
                b, h = fm_tile("up", hhi, hlo, 8, T, hr)
                if behind:
                    next(behind)
                tg, zg = conv(b, h, ch)
                b, h = fm_tile("up", hhi, hlo, 8, T, hr)
                if behind:
                    fin.append(next(behind))
                tv, zv = conv(b, h, 22 + ch)
                behind = gate(ct, tg, zg, tv, zv)
            next(behind)
            fin.append(next(behind))
            if half_ == 1 and not final:
                part_ring(f"sqf{l}", 1, fs)
                table("natural_log_exp_and_others")
                stat_begin()
            for m in range(8):
                w = weights("down")
                b, free = RA.take()
                for k in range(11):
                    g = mm3(b.t[:], w.hi[:, k, :], w.lo[:, k, :], ahi[:, k, :], alo[:, k, :], k == 0, k == 10,
                            w.rdy, free, fin[k])
                w.done(g)
                if half_ == 1 and not final:
                    stat_sum()
                z = tt(xT[:, m, :], b.t[:], xT[:, m, :], ADD, g, hs[m])
                b.done(z)
                hs[m] = z
                if half_ == 1 and not final:
                    stat_add(m, z)
                if final and half_ == 1:
                    store.append((m, z))
                if final and half_ == 1 and m > 0:
                    put_out(*store.pop(0))
            if store:
                put_out(*store.pop(0))
            dlast = g

        xlast["h"] = hs
        nhr = fm_norm("norm_mix", 8) if not final else None
        sq_ring["now"] = None
        q.barrier()
        fs.close()
        return nhr

    last_out = [None, None]

    L0 = ExitStack()
    fqh, fql, fkh, fkl = [sbuf(n, [P, 6, T], F32R, scope=L0) for n in ("fqh", "fql", "fkh", "fkl")]
    fv = sbuf("fv", [P, 4, 768], scope=L0)
    mqT = sbuf("mqT", [P, 2, T], scope=L0)
    cum = sbuf("cum", [12, T], scope=L0)
    fpre = sbuf("fpre", [12, T], scope=L0)
    gs = sbuf("gs", [P, 4], scope=L0)
    cb = sbuf("cb", [P, T], BF16, scope=L0)
    cres = sbuf("cres", [12, T], scope=L0)
    selb = sbuf("selb", [P, 12], BF16, scope=L0)
    SQ = ExitStack()
    part_ring("sq0", 2, SQ)
    zs = ts(gs[:, 0:1], col("fq"), 0.125, None, MUL, None, l_c)
    zs = ts(gs[:, 1:2], col("mq", 0), 0.125, None, MUL, None, l_c)
    fm_first(("ff", "fm"), hhi, hlo, 8, T, hr)
    b, h = fm_tile("ff", hhi, hlo, 8, T)
    a = act(fpre[:], b.t[0:12, :], ACT.Identity, h, l_c, bias=fb[:, 0:1])
    b.done(a)
    z = log_sigmoid(fpre[:], fpre[:], 12, T, a)
    zc = q.op("dve", lambda e: e.tensor_tensor_scan(cum[:], ones[0:12, 0:1].to_broadcast([12, T]), fpre[:], 0.0, MUL, ADD), (z,))
    fqk_, last_norm = head_normed_all([("fm", mqT[:, m, :], gs[:, 1:2]) for m in range(2)]
                           + [("fqk", (fqh[:, m, :], fql[:, m, :]), gs[:, 0:1], hr, zs) for m in range(6)]
                           + [("fqk", (fkh[:, m, :], fkl[:, m, :]), col("fk")) for m in range(6)])
    zm = mset(cb[:], 0.0, q.last())
    z = cp(cb[0:12, :], cum[:], zc, zm)
    z = tt(cres[:], cum[:], cb[0:12, :], SUB, z)
    z = cp(cb[32:44, :], cres[:], z)
    z = tt(cres[:], cres[:], cb[32:44, :], SUB, z)
    z_cb = cp(cb[64:76, :], cres[:], z)
    z = stt(selb[:], identb[:, 0:12], -1.0, identb[:, 32:44], MUL, SUB, C)
    z_sel = tt(selb[:], selb[:], identb[:, 64:76], SUB, z)

    fv_ = {}
    for g0 in (0, 384):
        for c, (b, h) in enumerate(tm_group("fv", hhi, hlo, 4, 384, None, last_norm if g0 == 0 else None)):
            z = evac(fv[:, c, g0:g0 + 384], b.t[:, 0:384], h)
            b.done(z)
            fv_[c, g0 // 384] = z
    mq_, fqk_ = fqk_[0:2], fqk_[2:]
    fq_, fk_ = fqk_[0:6], fqk_[6:12]

    def fox_h(h):
        hf, m = half(h), h // 2
        return Head(lambda i: (fqh[hf, m, i * P:(i + 1) * P], fq_[m]),
                    lambda n: (fkh[hf, m, 0:n], fk_[m]),
                    lambda j: (fv[:, j, h * 64:(h + 1) * 64], fv_[j, h // 6]),
                    lambda i: P * (i + 1), True,
                    low=lambda i, n: (fql[hf, m, i * P:(i + 1) * P], fkl[hf, m, 0:n]),
                    add=lambda n: (selb[0:76, h:h + 1].to_broadcast([76, P]), cb[0:76, 0:n], z_cb, z_sel))

    def mem_heads(l, mqT, mq_):
        kg = ts(kmg[:], kmn[:], col("mk", l), None, MUL, None, l_c)
        return [Head(lambda i, h=h: (mqT[half(h), h // 2, i * P:(i + 1) * P], mq_[h // 2]),
                     lambda n, h=h: (kmg[half(h), h // 2, :], kg),
                     lambda j, h=h: (vmem[:, j, h * 64:(h + 1) * 64], None),
                     lambda i: 256) for h in range(4)]

    SQ.close()
    sq_ring["now"] = None
    over = q.last()
    yr, dst, post = turned_outputs(0, L0, over)
    sc, _ = attention("fox", mem_heads(0, mqT, mq_) + [fox_h(h) for h in range(12)], dst, post, free=over)
    sc.close()
    part_ring("sq2", 1, L0, q.last())
    out_product(0, yr)
    sq_ring["now"] = None
    L0.close()

    def rope_tables(fs):
        pi_ = sbuf("posi", [P, 4], I32, scope=fs)
        pf = sbuf("posf", [P, 4], scope=fs)
        iv = sbuf("ivf", [P, 16], scope=fs)
        an = sbuf("ang", [P, 4, 16], scope=fs)
        kk = sbuf("kk", [P, 4, 16], scope=fs)
        r_ = sbuf("rr", [P, 2, 4, 16], scope=fs)
        l_p = dma(pi_[:], d["pos"], s_u, q.last())
        inv = np.float32(10000.0) ** (-np.arange(0, 32, 2, dtype=np.float32) / np.float32(32))
        for j in range(16):
            m = mset(iv[:, j:j + 1], float(np.float32(inv[j])))
        z = cp(pf[:], pi_[:], l_p)
        z = tt(an[:], pf[:].unsqueeze(2).to_broadcast([P, 4, 16]), iv[:].unsqueeze(1).to_broadcast([P, 4, 16]),
               MUL, z, m)
        magic = 12582912.0
        c1 = 6.28125
        c2 = float(np.float32(2 * np.pi - 6.28125) // np.float32(2 ** -20) * 2 ** -20)
        c3 = float(2 * np.pi - 6.28125 - c2)
        lim = 3.1415925
        zz = z
        for w, (quarter, shift, dst_) in enumerate(((0.0, 0.0, sinT), (0.25, float(np.pi / 2), cosT))):
            z = ts(kk[:], an[:], float(1 / (2 * np.pi)), quarter, MUL, ADD, zz)
            z = ts(kk[:], kk[:], magic, None, ADD, None, z)
            z = ts(kk[:], kk[:], -magic, None, ADD, None, z)
            z = stt(r_[:, w], kk[:], -c1, an[:], MUL, ADD, z)
            z = stt(r_[:, w], kk[:], -c2, r_[:, w], MUL, ADD, z)
            z = stt(r_[:, w], kk[:], -c3, r_[:, w], MUL, ADD, z)
            z = ts(r_[:, w], r_[:, w], shift, lim, ADD, MIN, z)
            z = ts(r_[:, w], r_[:, w], -lim, None, MAX, None, z)
            a = act(dst_[:], r_[:, w], ACT.Sin, z)
            zz = [zz, z]
        rope_ok.append(a)

    rope_ok = []
    hr = ffn(0, False, rope_tables)

    L1 = ExitStack()
    grp = [Slot((sbuf(f"qt{i}", [P, 4, 4, 96], scope=L1), sbuf(f"kt{i}", [P, 4, 4, 96], scope=L1)))
           for i in range(2)]
    vts = [sbuf(f"vt{i}", [P, 4, 4, 64], scope=L1) for i in range(3)]
    mqT1 = sbuf("mqT1", [P, 2, T], scope=L1)
    gs1 = sbuf("gs1", [P, 1], scope=L1)
    gq96 = sbuf("gq96", [96, 2], scope=L1)
    l_q = dma(gq96[:, 0:1], d["mla_q_gain_2"].rearrange("a n -> n a"), s_u, q.last())
    l_q = dma(gq96[:, 1:2], d["mla_k_gain_2"].rearrange("a n -> n a"), s_u)
    lhi = sbuf("lhi", [P, 3, T], F32R, scope=L1)
    llo = sbuf("llo", [P, 3, T], F32R, scope=L1)
    krr = sbuf("krr", [P, 4, 32], scope=L1)
    krt = sbuf("krt", [P, 4, 4, 16], scope=L1)
    zs = ts(gs1[:], col("mq", 1), 0.125, None, MUL, None, l_c)
    zg = ts(gq96[:, 0:1], gq96[:, 0:1], 96 ** -0.5, None, MUL, None, l_q)

    def latent(tiles, key, n, gname, base, dep=None):
        bs = []
        b2, f2 = RO.take()
        for m in range(tiles):
            b, h = fm_tile(key, hhi, hlo, 8, T, dep, RS)
            t, free = tmp.take()
            a = act(t.t[:], b.t[:], ACT.Square, h, free)
            g = mm(b2.t[:], ones[:], t.t[:], m == 0, m == tiles - 1, a, f2)
            t.done(g)
            bs.append(b)
        rb, free = hold.take()
        a = rstd_of(rb.t[:], b2.t[:], n, g, free)
        b2.done(a)
        zl = []
        for m in range(tiles):
            t, free = tmp.take()
            z = stt(t.t[:], bs[m].t[:], col(gname, m), rb.t[:], MUL, MUL, a, free)
            bs[m].done(z)
            a2 = acopy(lhi[:, base + m, :], t.t[:], z)
            z = tt(llo[:, base + m, :], t.t[:], lhi[:, base + m, :].bitcast(F32), SUB, a2)
            t.done(z)
            zl.append(z)
        rb.done(zl[-1])
        return zl

    fm_first(("ql", "ql"), hhi, hlo, 8, T, hr, RS)
    ql_ = latent(2, "ql", 256, "qa", 0, hr)
    kvl_ = latent(1, "kvl", 128, "kva", 2)
    w = weights("kr")
    b, free = RA.take()
    for k in range(8):
        g = mm3(b.t[0:32, :], w.hi[:, k, :], w.lo[:, k, :], hhi[:, k, :], hlo[:, k, :], k == 0, k == 7, w.rdy, free)
    w.done(g)
    t, free = tmp.take()
    z = cp(t.t[0:32, :], b.t[0:32, :], g, free)
    b.done(z)
    b, free = RA.take()
    for c in range(4):
        g = tr(b.t[:, c * 32:(c + 1) * 32], t.t[0:32, c * P:(c + 1) * P], ident[0:32, 0:32], z, free)
    t.done(g)
    z_kr = cp(krr[:].rearrange("p c n -> p (c n)"), b.t[:, 0:P], g)
    b.done(z_kr)
    mq_, last_norm = head_normed_all([("mm", mqT1[:, m, :], gs1[:, 0:1], None, zs) for m in range(2)])

    def rope(x1, x2, cc, ss, t4, *deps, eng="dve"):
        z1_ = tt(t4[0], x1, cc, MUL, *deps, eng=eng)
        z2_ = tt(t4[1], x2, ss, MUL, eng=eng)
        z3_ = tt(t4[2], x1, ss, MUL, eng=eng)
        z4_ = tt(t4[3], x2, cc, MUL, eng=eng)
        z5_ = tt(x1, t4[0], t4[1], SUB, z1_, z2_, z3_, eng=eng)
        return tt(x2, t4[2], t4[3], ADD, z3_, z4_, z5_, eng=eng)

    zk_ = rope(krr[:, :, 0:16], krr[:, :, 16:32], cosT[:], sinT[:], [krt[:, i] for i in range(4)], z_kr, rope_ok)
    held_, f_h = hold.take()
    r4 = [krt] + [held_.t[:, o:o + 256].rearrange("p (c h n) -> p c h n", c=4, h=4) for o in (0, 256)]
    r4 += [sbuf("r43", [P, 4, 4, 16], scope=L1)]
    r16 = sbuf("r16", [P, 6, 16], scope=L1)
    GR = {}

    def mla_group(j, ring):
        st_ = {}
        cb_ = cosT[:].unsqueeze(2).to_broadcast([P, 4, 4, 16])
        sb_ = sinT[:].unsqueeze(2).to_broadcast([P, 4, 4, 16])
        vt = vts[j]
        rq, rk = r16[:, 2 * j, :], r16[:, 2 * j + 1, :]

        def begin():
            s_ = grp[j % 2]
            st_["free"] = s_.take()
            st_["q"], st_["k"] = s_.t
            st_["zr"] = cp(s_.t[1][:, :, :, 64:96], krr[:].unsqueeze(2).to_broadcast([P, 4, 4, 32]), zk_,
                           st_["free"], eng="pool")
            st_["qz"], st_["kz"] = [], []
            GR[j] = [s_, [], st_["kz"]]

        def q_tile(c):
            if c == 0:
                begin()
                st_["w"] = weights("qup")
            w = st_["w"]
            b, free = ring.take()
            for k in range(2):
                g = mm3(b.t[:, 0:384], lhi[:, k, c * P:(c + 1) * P], llo[:, k, c * P:(c + 1) * P],
                        w.hi[:, k, :], w.lo[:, k, :], k == 0, k == 1, w.rdy, free, ql_)
            z = evac(st_["q"][:, c], b.t[:, 0:384].rearrange("p (h n) -> p h n", h=4), g, st_["free"])
            b.done(z)
            st_["qz"].append(z)
            if c == 3:
                w.done(g)

        def kv_tile(c):
            if c == 0:
                st_["w"] = weights("kvup")
            w = st_["w"]
            b, free = ring.take()
            g = mm3(b.t[:], lhi[:, 2, c * P:(c + 1) * P], llo[:, 2, c * P:(c + 1) * P],
                    w.hi[:, 0, :], w.lo[:, 0, :], True, True, w.rdy, free, kvl_)
            bv = b.t[:].rearrange("p (h n) -> p h n", h=4)
            a = acopy(st_["k"][:, c, :, 0:64], bv[:, :, 0:64], g, st_["free"])
            z = cp(vt[:, c], bv[:, :, 64:128], a, st_["free"])
            b.done(z)
            st_["kz"] += [a, z]
            if c == 3:
                w.done(g)

        def turn_1():
            x1, x2 = st_["q"][:, :, :, 64:80], st_["q"][:, :, :, 80:96]
            st_["a"] = [tt(r4[0][:], x1, cb_, MUL, st_["qz"], rope_ok, f_h, q.end["dve"], eng="pool"),
                        tt(r4[1][:], x2, sb_, MUL, eng="pool")]

        def turn_2():
            x1, x2 = st_["q"][:, :, :, 64:80], st_["q"][:, :, :, 80:96]
            st_["a"] += [tt(r4[2][:], x1, sb_, MUL, eng="pool"), tt(r4[3][:], x2, cb_, MUL, eng="pool")]

        def turn_3():
            x1, x2 = st_["q"][:, :, :, 64:80], st_["q"][:, :, :, 80:96]
            z = tt(x1, r4[0][:], r4[1][:], SUB, st_["a"], eng="pool")
            st_["qr"] = [z, tt(x2, r4[2][:], r4[3][:], ADD, st_["a"], eng="pool")]

        def square(x, c, *deps):
            t, free = tmp.take()
            a = act(t.t[:, 0:384], x[:, c].rearrange("p h n -> p (h n)"), ACT.Square, deps, free)
            st_[c] = (t, a)

        def sums(rr, c):
            t, a = st_[c]
            z = red(rr[:, 4 * c:4 * c + 4], t.t[:, 0:384].rearrange("p (h n) -> p h n", h=4), ADD, a)
            t.done(z)
            st_["sum"] = z

        def scale(x, rr):
            sr = x[:].rearrange("p c h n -> p (c h) n")
            a = rstd_of(rr, rr, 96, st_["sum"])
            GR[j][1].append(tt(sr, sr, rr.unsqueeze(2).to_broadcast([P, 16, 96]), MUL, a, eng="pool"))

        def sq_k(c):
            return square(st_["k"], c, st_["kz"], st_["zr"])

        def sq_q(c):
            return square(st_["q"], c, st_["qr"])

        return [lambda: q_tile(0), lambda: q_tile(1), lambda: q_tile(2), lambda: q_tile(3),
                lambda: (kv_tile(0), turn_1()), lambda: (kv_tile(1), turn_2()), lambda: (kv_tile(2), turn_3()),
                lambda: (kv_tile(3), sq_k(0)),
                lambda: (sums(rk, 0), sq_k(1)), lambda: (sums(rk, 1), sq_k(2)), lambda: (sums(rk, 2), sq_k(3)),
                lambda: (sums(rk, 3), sq_q(0)),
                lambda: (scale(st_["k"], rk), sums(rq, 0), sq_q(1)),
                lambda: (sums(rq, 1), sq_q(2)), lambda: (sums(rq, 2), sq_q(3)), lambda: sums(rq, 3),
                lambda: scale(st_["q"], rq)]

    qh_r, kh_r = [Ring([Slot((sbuf(f"m{n}h{i}", [96, T], F32R, scope=L1), sbuf(f"m{n}l{i}", [96, T], F32R, scope=L1)))
                        for i in range(2)]) for n in ("q", "k")]
    QK = {}

    mem1 = mem_heads(1, mqT1, mq_)
    steps = mla_group(0, RA)
    for f in steps[0:3] + [last_norm] + steps[3:8]:
        f()
    side_ = {}
    for t0, fs_ in ((-1, steps[8:]), (7, mla_group(1, RT)), (26, [lambda: GR[0][0].done(q.end["pe"])]),
                    (27, mla_group(2, RT))):
        for t, f in enumerate(fs_):
            side_.setdefault(t0 + (t if t0 != 27 else t // 2 if t < 8 else t - 4), []).append(f)

    def side(t):
        for f in side_.get(t, ()):
            f()

    def mla_start(h):
        if h >= 2:
            QK[h - 2][0].done(q.end["pe"])
            QK[h - 2][2].done(q.end["pe"])
        s_, nz = GR[h // 4][0:2]
        outs = []
        for src, ring, gi in ((s_.t[0], qh_r, 0), (s_.t[1], kh_r, 1)):
            b, free = RT.take()
            for c in range(4):
                g = tr(b.t[0:96, c * P:(c + 1) * P], src[:, c, h % 4, :], ident[:], free, nz)
            o_, f2 = ring.take()
            hi, lo = o_.t
            a = act(hi[:], b.t[0:96, :], ACT.Identity, g, f2, zg, l_q, scale=gq96[:, gi:gi + 1])
            z = stt(lo[:], b.t[0:96, :], gq96[:, gi:gi + 1], hi[:].bitcast(F32), MUL, SUB, a)
            b.done(z)
            outs += [o_, [a, z]]
        QK[h] = outs

    def mla_h(h):
        return Head(lambda i: (QK[h][0].t[0][:, i * P:(i + 1) * P], QK[h][1]),
                    lambda n: (QK[h][2].t[0][:, 0:n], QK[h][3]),
                    lambda j: (vts[h // 4][:, j, h % 4, :], GR[h // 4][2]),
                    lambda i: P * (i + 1), True, prep=lambda: mla_start(h),
                    low=lambda i, n: (QK[h][0].t[1][:, i * P:(i + 1) * P], QK[h][2].t[1][:, 0:n]))

    yr, dst, post = turned_outputs(1, L1)
    sc, _ = attention("mla", mem1 + [mla_h(h) for h in range(12)], dst, post, side)
    held_.done(*q.last())
    sc.close()
    part_ring("sq1", 1, L1, q.last())
    out_product(1, yr)
    sq_ring["now"] = None
    L1.close()
    ffn(1, True)
    assert state["next"] == len(chunks)

    q.number()
    with nc.Block() as block:
        @block.sync
        def _(e):
            q.emit("sp", e, sems)
            for _, s, n in last_out:
                e.wait_ge(s, n)

        @block.scalar
        def _(e):
            q.emit("act", e, sems)

        @block.vector
        def _(e):
            q.emit("dve", e, sems)

        @block.gpsimd
        def _(e):
            q.emit("pool", e, sems)

        @block.tensor
        def _(e):
            q.emit("pe", e, sems)
    ctx.close()


def lay_out(inputs):
    a = {k: np.asarray(v) for k, v in inputs.items()}
    a["gates"] = np.concatenate([a["w_in"][0][:, 3072:3084], np.zeros((D, 20), np.float32),
                                 a["w_in"][0][:, 3980:3996]], axis=1)
    parts = []
    for _, name, l, k0, kt, c0, n in plan_chunks():
        w = a[name] if l is None else a[name][l]
        parts.append(w[k0:k0 + kt * P, c0:c0 + n].reshape(kt, P, n).transpose(1, 0, 2).reshape(-1))
    vec = np.zeros((P, NVEC), np.float32)

    def put(name, m):
        c, n = VECS[name]
        vec[:, c:c + n] = m

    put("norm_g", a["norm_g"][0].reshape(8, P).T)
    put("conv_w", a["conv_w"][0].reshape(4, 6, P).transpose(2, 1, 0).reshape(P, 24))
    put("norm_mix", a["norm_mix_2"].reshape(16, P).T)
    put("norm_ffn", a["norm_ffn_2"].reshape(16, P).T)
    put("mem_norm", a["mem_norm_2"].reshape(8, P).T)
    put("qa", a["mla_qa_norm_2"][0].reshape(2, P).T)
    put("kva", a["mla_kva_norm_2"].reshape(1, P).T)
    put("b_alpha", a["b_alpha"].reshape(1, P).T)
    put("fq", np.tile(a["fox_q_gain_2"][0], 2)[:, None])
    put("fk", np.tile(a["fox_k_gain_2"][0], 2)[:, None])
    put("mq", np.tile(a["mem_q_gain_2"], (1, 2)).T)
    put("mk", np.tile(a["mem_k_gain_2"], (1, 2)).T)
    for l in range(2):
        put(f"cw{l}", a["ffn_conv_w_2"][l].reshape(3, 44, P).transpose(2, 1, 0).reshape(P, 132))
        put(f"cb{l}", a["ffn_conv_b_2"][l].reshape(44, P).T)
    rel = a["rel_bias"][0]
    out = {"pos": a["positions_2"].reshape(4, P).T, "wts": np.concatenate(parts), "vecs": vec,
           "rel_ext": np.concatenate([rel, np.repeat(rel[:, 256:257], 640 - 257, axis=1)], axis=1)}
    for k in ("x", "mem_2", "fox_b_f_2", "b_gates", "ml_norm_g", "gla_norm_g", "w_alpha", "final_g",
              "mla_q_gain_2", "mla_k_gain_2"):
        out[k] = a[k]
    return {k: np.ascontiguousarray(v) for k, v in out.items()}


def kernel(**inputs):
    import concourse.bacc as bacc
    from concourse.bass_utils import run_bass_kernel_spmd

    nc = bacc.Bacc("TRN2", target_bir_lowering=False, num_devices=1)
    arrays = lay_out(inputs)
    d = {k: nc.dram_tensor(f"in_{k}", v.shape, mybir.dt.from_np(v.dtype), kind="ExternalInput").ap()
         for k, v in arrays.items()}
    out = nc.dram_tensor("out_0", (1, T, D), F32, kind="ExternalOutput").ap()
    build(nc, d, out)
    r = run_bass_kernel_spmd(nc, [{f"in_{k}": v for k, v in arrays.items()}], core_ids=[0])
    return r.results[0]["out_0"]
```
